# Optimizing a Trainium2 kernel written in Bass

```python
import jax, jax.numpy as jnp
from jax import lax
import numpy as np
import math

D_MODEL = 2048
BATCH = 1
SEQ = 256
DEPTH = 1

D_MIX = D_MODEL
HG_DK = 128
HG_DV = 128
HG_WIDTH = D_MIX // 2
HG_HEADS = HG_WIDTH // HG_DV
HG_QK = HG_HEADS * HG_DK
GDN_DK = 128
GDN_DV = 128
GDN_WIDTH = D_MIX - HG_WIDTH
GDN_HEADS = GDN_WIDTH // GDN_DV
GDN_QK = GDN_HEADS * GDN_DK
CONV_K = 4
CHUNK = 64
D_FF = 4 * D_MODEL
N_MOD = 6
EPS = 1e-6

HG_COLS = 2 * HG_QK + 2 * HG_WIDTH
GDN_CONV_CH = 2 * GDN_QK + GDN_WIDTH
GDN_COLS = GDN_CONV_CH + GDN_WIDTH + 2 * GDN_HEADS
IN_COLS = HG_COLS + GDN_COLS


def rmsnorm(x, w):
    x32 = x.astype(jnp.float32)
    y = x32 * lax.rsqrt(jnp.mean(x32 * x32, axis=-1, keepdims=True) + EPS)
    return (y * w.astype(jnp.float32)).astype(x.dtype)

def l2norm(x):
    return x * lax.rsqrt(jnp.sum(x * x, axis=-1, keepdims=True) + EPS)

def to_chunks(x):
    B, T, H, D = x.shape
    return x.reshape(B, T // CHUNK, CHUNK, H, D).transpose(1, 0, 3, 2, 4)

def from_chunks(x):
    N, B, H, C, D = x.shape
    return x.transpose(1, 0, 3, 2, 4).reshape(B, N * C, H, D)

def causal_conv(u, w):
    ch = u.shape[-1]
    return lax.conv_general_dilated(
        u, w[:, None, :].astype(u.dtype), window_strides=(1,), padding=[(CONV_K - 1, 0)],
        dimension_numbers=('NWC', 'WIO', 'NWC'), feature_group_count=ch)

def hgrn2_chunked(q, log_f, k, v):
    B, T, H, DK = q.shape
    DV = v.shape[-1]
    causal = jnp.tril(jnp.ones((CHUNK, CHUNK), dtype=bool))

    def step(S, xs):
        qc, lfc, kc, vc = xs
        b = jnp.cumsum(lfc, axis=-2)
        diff = b[:, :, :, None, :] - b[:, :, None, :, :]
        decay = jnp.exp(jnp.where(causal[None, None, :, :, None], diff, -jnp.inf))
        attn = jnp.einsum('bhtk,bhsk,bhtsk->bhts', qc, kc, decay)
        o = (jnp.einsum('bhts,bhsv->bhtv', attn, vc)
             + jnp.einsum('bhtk,bhkv->bhtv', qc * jnp.exp(b), S))
        b_last = b[:, :, -1:, :]
        S_new = (S * jnp.exp(b_last[:, :, 0, :, None])
                 + jnp.einsum('bhsk,bhsv->bhkv', kc * jnp.exp(b_last - b), vc))
        return S_new, o

    S0 = jnp.zeros((B, H, DK, DV), jnp.float32)
    _, o = lax.scan(step, S0, (to_chunks(q), to_chunks(log_f), to_chunks(k), to_chunks(v)))
    return from_chunks(o)

def gated_delta_chunked(q, k, v, log_a, beta):
    B, T, H, DK = q.shape
    DV = v.shape[-1]
    qc, kc, vc = to_chunks(q), to_chunks(k), to_chunks(v)
    g = jnp.cumsum(to_chunks(log_a[..., None])[..., 0], axis=-1)
    bc = to_chunks(beta[..., None])[..., 0]
    incl = jnp.tril(jnp.ones((CHUNK, CHUNK), dtype=bool))
    strict = jnp.tril(jnp.ones((CHUNK, CHUNK), dtype=bool), -1)
    gamma = jnp.exp(jnp.where(incl, g[..., :, None] - g[..., None, :], -jnp.inf))
    kk = jnp.einsum('nbhtk,nbhsk->nbhts', kc, kc)
    m = jnp.where(strict, bc[..., :, None] * kk * gamma, 0.0)
    a_mat = jnp.eye(CHUNK, dtype=jnp.float32) + m
    rhs = jnp.concatenate([vc * bc[..., None], kc * (bc * jnp.exp(g))[..., None]], axis=-1)
    sol = lax.linalg.triangular_solve(a_mat, rhs, left_side=True, lower=True, unit_diagonal=True)
    u, w = sol[..., :DV], sol[..., DV:]
    qk = jnp.einsum('nbhtk,nbhsk->nbhts', qc, kc) * gamma
    q_dec = qc * jnp.exp(g)[..., None]
    k_tail = kc * jnp.exp(g[..., -1:] - g)[..., None]
    tail = jnp.exp(g[..., -1])

    def step(S, xs):
        u_c, w_c, qk_c, qd_c, kt_c, tl_c = xs
        v_new = u_c - jnp.einsum('bhck,bhkv->bhcv', w_c, S)
        o = jnp.einsum('bhck,bhkv->bhcv', qd_c, S) + jnp.einsum('bhts,bhsv->bhtv', qk_c, v_new)
        S = S * tl_c[..., None, None] + jnp.einsum('bhck,bhcv->bhkv', kt_c, v_new)
        return S, o

    S0 = jnp.zeros((B, H, DK, DV), jnp.float32)
    _, o = lax.scan(step, S0, (u, w, qk, q_dec, k_tail, tail))
    return from_chunks(o)

def hgrn2_group(p, lb, norm_w):
    B, T, _ = p.shape
    dt = p.dtype
    p32 = p.astype(jnp.float32)
    q = p32[..., :HG_QK].reshape(B, T, HG_HEADS, HG_DK)
    f_logit = p32[..., HG_QK:2 * HG_QK].reshape(B, T, HG_HEADS, HG_DK)
    i_in = p32[..., 2 * HG_QK:2 * HG_QK + HG_WIDTH].reshape(B, T, HG_HEADS, HG_DV)
    g_out = p[..., 2 * HG_QK + HG_WIDTH:].reshape(B, T, HG_HEADS, HG_DV)
    f = lb + (1.0 - lb) * jax.nn.sigmoid(f_logit)
    o = hgrn2_chunked(q, jnp.log(f), 1.0 - f, i_in).astype(dt)
    o = rmsnorm(o, norm_w) * jax.nn.silu(g_out)
    return o.reshape(B, T, HG_WIDTH)

def gdn_group(p, conv_w, a_log, dt_bias, norm_w):
    B, T, _ = p.shape
    dt = p.dtype
    qkv = jax.nn.silu(causal_conv(p[..., :GDN_CONV_CH], conv_w)).astype(jnp.float32)
    q = l2norm(qkv[..., :GDN_QK].reshape(B, T, GDN_HEADS, GDN_DK)) * (GDN_DK ** -0.5)
    k = l2norm(qkv[..., GDN_QK:2 * GDN_QK].reshape(B, T, GDN_HEADS, GDN_DK))
    v = qkv[..., 2 * GDN_QK:].reshape(B, T, GDN_HEADS, GDN_DV)
    off = GDN_CONV_CH
    g_out = p[..., off:off + GDN_WIDTH].reshape(B, T, GDN_HEADS, GDN_DV)
    a = p[..., off + GDN_WIDTH:off + GDN_WIDTH + GDN_HEADS].astype(jnp.float32)
    b = p[..., off + GDN_WIDTH + GDN_HEADS:].astype(jnp.float32)
    log_a = -jnp.exp(a_log.astype(jnp.float32)) * jax.nn.softplus(a + dt_bias.astype(jnp.float32))
    beta = jax.nn.sigmoid(b)
    o = gated_delta_chunked(q, k, v, log_a, beta).astype(dt)
    o = rmsnorm(o, norm_w) * jax.nn.silu(g_out)
    return o.reshape(B, T, GDN_WIDTH)

def first_inputs(seed: int = 0) -> dict:
    key = jax.random.key(seed)
    ks = jax.random.split(key, 20)
    f32 = jnp.float32
    nrm = lambda k, s, sc: jax.random.normal(k, s, f32) * sc
    gain = lambda k, s: 1.0 + 0.05 * jax.random.normal(k, s, f32)
    dtv = jnp.exp(jax.random.uniform(ks[13], (DEPTH, GDN_HEADS), f32, np.log(1e-3), np.log(1e-1)))
    return {
        "x": nrm(ks[0], (BATCH, SEQ, D_MODEL), 1.0),
        "c": nrm(ks[1], (BATCH, D_MODEL), 1.0),
        "w_ada": nrm(ks[2], (DEPTH, D_MODEL, N_MOD * D_MODEL), 0.5 * D_MODEL ** -0.5),
        "b_ada": nrm(ks[3], (DEPTH, N_MOD * D_MODEL), 0.02),
        "pre_mix_norm": gain(ks[4], (DEPTH, D_MODEL)),
        "post_mix_norm": gain(ks[5], (DEPTH, D_MODEL)),
        "pre_ffn_norm": gain(ks[6], (DEPTH, D_MODEL)),
        "post_ffn_norm": gain(ks[7], (DEPTH, D_MODEL)),
        "w_in": nrm(ks[8], (DEPTH, D_MODEL, IN_COLS), D_MODEL ** -0.5),
        "hg_lb_logits": nrm(ks[9], (DEPTH + 1, HG_HEADS, HG_DK), 0.5),
        "hg_norm": gain(ks[10], (DEPTH, HG_DV)),
        "gdn_conv_w": nrm(ks[11], (DEPTH, CONV_K, GDN_CONV_CH), CONV_K ** -0.5),
        "gdn_a_log": jnp.log(jax.random.uniform(ks[12], (DEPTH, GDN_HEADS), f32, 1.0, 16.0)),
        "gdn_dt_bias": dtv + jnp.log(-jnp.expm1(-dtv)),
        "gdn_norm": gain(ks[14], (DEPTH, GDN_DV)),
        "w_out": nrm(ks[15], (DEPTH, D_MIX, D_MODEL), D_MIX ** -0.5),
        "w_ff1": nrm(ks[16], (DEPTH, D_MODEL, D_FF), D_MODEL ** -0.5),
        "w_ff2": nrm(ks[17], (DEPTH, D_FF, D_MODEL), D_FF ** -0.5),
    }

def first_block(x, c, w_ada, b_ada, pre_mix_norm, post_mix_norm, pre_ffn_norm, post_ffn_norm,
              w_in, hg_lb_logits, hg_norm, gdn_conv_w, gdn_a_log, gdn_dt_bias, gdn_norm,
              w_out, w_ff1, w_ff2):
    lb_all = jnp.cumsum(jax.nn.softmax(hg_lb_logits.astype(jnp.float32), axis=0), axis=0)
    c_act = jax.nn.silu(c)
    for l in range(DEPTH):
        mod = c_act @ w_ada[l] + b_ada[l]
        sh_m, sc_m, gt_m, sh_f, sc_f, gt_f = jnp.split(mod[:, None, :], N_MOD, axis=-1)
        h = rmsnorm(x, pre_mix_norm[l]) * (1.0 + sc_m) + sh_m
        proj = h @ w_in[l]
        o_hg = hgrn2_group(proj[..., :HG_COLS], lb_all[l], hg_norm[l])
        o_gdn = gdn_group(proj[..., HG_COLS:], gdn_conv_w[l], gdn_a_log[l], gdn_dt_bias[l], gdn_norm[l])
        y = jnp.concatenate([o_hg, o_gdn], axis=-1) @ w_out[l]
        x = x + gt_m * rmsnorm(y, post_mix_norm[l])
        h = rmsnorm(x, pre_ffn_norm[l]) * (1.0 + sc_f) + sh_f
        y = jnp.square(jax.nn.relu(h @ w_ff1[l])) @ w_ff2[l]
        x = x + gt_f * rmsnorm(y, post_ffn_norm[l])
    return x


HEAD_DIM = 64
Q_BLOCK = 128
RMS_EPS = 1e-6
MASK_VALUE = -1e30
ALIBI_MAX_EXP = 8.0
FOX_HEADS = 7
NSA_HEADS = 8
NSA_KV_GROUPS = 2
NSA_CMP_LEN = 32
NSA_CMP_STRIDE = 16
NSA_SEL_BLOCK = 64
NSA_TOP_N = 16
NSA_WINDOW = 512
NSA_FORCE_SCORE = 1e4
DIL_CONFIGS = ((128, 1), (512, 4), (2048, 16))
DIL_HEADS_PER_GROUP = 3
DIL_HEADS = DIL_HEADS_PER_GROUP * len(DIL_CONFIGS)
DIFF_HEADS = 4
DIFF_QK_DIM = 64
DIFF_V_DIM = 2 * DIFF_QK_DIM
MIX_WIDTH = (FOX_HEADS + NSA_HEADS + DIL_HEADS) * HEAD_DIM + DIFF_HEADS * DIFF_V_DIM
D_FF_2 = ((8 * D_MODEL + 3 * 256 - 1) // (3 * 256)) * 256
NSA_KV = NSA_KV_GROUPS * HEAD_DIM
IN_SPLITS = (
    ('fox_q', FOX_HEADS * HEAD_DIM), ('fox_k', FOX_HEADS * HEAD_DIM), ('fox_v', FOX_HEADS * HEAD_DIM), ('fox_f', FOX_HEADS),
    ('nsa_q', NSA_HEADS * HEAD_DIM),
    ('nsa_cmp_k', NSA_KV), ('nsa_cmp_v', NSA_KV), ('nsa_slc_k', NSA_KV), ('nsa_slc_v', NSA_KV), ('nsa_win_k', NSA_KV), ('nsa_win_v', NSA_KV),
    ('nsa_gate', NSA_HEADS * 3),
    ('dil_q', DIL_HEADS * HEAD_DIM), ('dil_k', DIL_HEADS * HEAD_DIM), ('dil_v', DIL_HEADS * HEAD_DIM),
    ('diff_q', DIFF_HEADS * 2 * DIFF_QK_DIM), ('diff_k', DIFF_HEADS * 2 * DIFF_QK_DIM), ('diff_v', DIFF_HEADS * DIFF_V_DIM),
)
N_IN = sum(w for _, w in IN_SPLITS)


def rms_norm(x, gain):
    xf = x.astype(jnp.float32)
    y = xf * lax.rsqrt(jnp.mean(xf * xf, axis=-1, keepdims=True) + RMS_EPS)
    return (y * gain.astype(jnp.float32)).astype(x.dtype)

def masked_softmax(s, mask):
    p = jax.nn.softmax(jnp.where(mask, s, MASK_VALUE), axis=-1)
    return jnp.where(mask, p, 0.0)

def alibi_slopes(n_heads):
    return jnp.asarray(2.0 ** (-ALIBI_MAX_EXP * np.arange(1, n_heads + 1) / n_heads), jnp.float32)

def blocks_to_seq(o):
    o = jnp.moveaxis(o, 0, 1)
    return o.reshape(o.shape[0], o.shape[1] * o.shape[2], *o.shape[3:])

def fox_attention(q, k, v, f_logit, f_bias):
    B, S, H, dh = q.shape
    scale = dh ** -0.5
    log_f = jax.nn.log_sigmoid(f_logit.astype(jnp.float32) + f_bias.astype(jnp.float32))
    cum = jnp.cumsum(log_f, axis=1).transpose(0, 2, 1)
    pos = jnp.arange(S)

    def block(i):
        qs = i * Q_BLOCK
        tq = qs + jnp.arange(Q_BLOCK)
        qb = lax.dynamic_slice_in_dim(q, qs, Q_BLOCK, 1)
        cq = lax.dynamic_slice_in_dim(cum, qs, Q_BLOCK, 2)
        s = jnp.einsum('bqhd,bkhd->bhqk', qb, k).astype(jnp.float32) * scale
        s = s + cq[..., None] - cum[:, :, None, :]
        p = jax.nn.softmax(jnp.where(pos[None, :] <= tq[:, None], s, MASK_VALUE), axis=-1)
        return jnp.einsum('bhqk,bkhd->bqhd', p.astype(v.dtype), v)

    o = blocks_to_seq(lax.map(block, jnp.arange(S // Q_BLOCK)))
    return o.reshape(B, S, H * dh)

def cmp_to_sel_matrix(n_cmp, n_sel):
    a = NSA_SEL_BLOCK // NSA_CMP_STRIDE
    b = NSA_CMP_LEN // NSA_CMP_STRIDE
    j = np.arange(n_sel)[:, None, None]
    idx = a * j + np.arange(a)[None, :, None] - np.arange(b)[None, None, :]
    jj = np.broadcast_to(j, idx.shape)
    ok = (idx >= 0) & (idx < n_cmp)
    m = np.zeros((n_cmp, n_sel), np.float32)
    np.add.at(m, (idx[ok], jj[ok]), 1.0)
    return m

def nsa_attention(q, k_cmp, v_cmp, k_slc, v_slc, k_win, v_win, gate_logit, cmp_w1, cmp_w2, cmp_pos):
    B, S, H, dh = q.shape
    G = k_cmp.shape[2]
    hpg = H // G
    scale = dh ** -0.5
    slopes = alibi_slopes(H).reshape(G, hpg)[None, :, :, None, None]
    ratio = NSA_CMP_LEN // NSA_CMP_STRIDE
    n_chunk = S // NSA_CMP_STRIDE
    n_cmp = n_chunk - ratio + 1
    n_sel = S // NSA_SEL_BLOCK
    n_top = min(NSA_TOP_N, n_sel)

    def compress(t, w1, w2, pos_emb):
        ch = t.reshape(B, n_chunk, NSA_CMP_STRIDE, G, dh)
        blk = jnp.concatenate([ch[:, r:r + n_cmp] for r in range(ratio)], axis=2)
        blk = (blk + pos_emb[:, None, :]).transpose(0, 1, 3, 2, 4).reshape(B, n_cmp, G, NSA_CMP_LEN * dh)
        return jax.nn.gelu(blk @ w1) @ w2

    kc = compress(k_cmp, cmp_w1[0], cmp_w2[0], cmp_pos[0])
    vc = compress(v_cmp, cmp_w1[1], cmp_w2[1], cmp_pos[1])
    cmp_end = jnp.arange(n_cmp) * NSA_CMP_STRIDE + (NSA_CMP_LEN - 1)
    cmp_to_sel = jnp.asarray(cmp_to_sel_matrix(n_cmp, n_sel), jnp.float32)
    k_blocks = k_slc.transpose(0, 2, 1, 3).reshape(B, G, n_sel, NSA_SEL_BLOCK, dh)
    v_blocks = v_slc.transpose(0, 2, 1, 3).reshape(B, G, n_sel, NSA_SEL_BLOCK, dh)
    pad = ((0, 0), (NSA_WINDOW, 0), (0, 0), (0, 0))
    k_win_p = jnp.pad(k_win, pad)
    v_win_p = jnp.pad(v_win, pad)
    gates = jax.nn.sigmoid(gate_logit).reshape(B, S, G, hpg, 3)
    sel_ids = jnp.arange(n_sel)
    win_offsets = jnp.arange(Q_BLOCK + NSA_WINDOW) - NSA_WINDOW
    sel_offsets = jnp.arange(NSA_SEL_BLOCK)

    def block(i):
        qs = i * Q_BLOCK
        tq = qs + jnp.arange(Q_BLOCK)
        qb = lax.dynamic_slice_in_dim(q, qs, Q_BLOCK, 1).reshape(B, Q_BLOCK, G, hpg, dh)
        dist_c = (tq[:, None] - cmp_end[None, :]).astype(jnp.float32)
        s_c = jnp.einsum('bqgjd,bcgd->bgjqc', qb, kc).astype(jnp.float32) * scale - slopes * dist_c
        p_c = masked_softmax(s_c, dist_c >= 0)
        o_c = jnp.einsum('bgjqc,bcgd->bqgjd', p_c.astype(vc.dtype), vc)
        imp = jnp.einsum('bgjqc,cn->bgqn', p_c, cmp_to_sel)
        cur = (tq // NSA_SEL_BLOCK)[:, None]
        forced = (sel_ids == 0) | (sel_ids == cur) | (sel_ids == cur - 1)
        causal = sel_ids * NSA_SEL_BLOCK <= tq[:, None]
        score = jnp.where(causal, jnp.where(forced, NSA_FORCE_SCORE, imp), MASK_VALUE)
        _, top_idx = lax.top_k(score, n_top)
        flat = top_idx.reshape(B, G, Q_BLOCK * n_top)[..., None, None]
        ks = jnp.take_along_axis(k_blocks, flat, axis=2).reshape(B, G, Q_BLOCK, n_top * NSA_SEL_BLOCK, dh)
        vs = jnp.take_along_axis(v_blocks, flat, axis=2).reshape(B, G, Q_BLOCK, n_top * NSA_SEL_BLOCK, dh)
        kpos = (top_idx[..., None] * NSA_SEL_BLOCK + sel_offsets).reshape(B, G, Q_BLOCK, n_top * NSA_SEL_BLOCK)
        dist_s = (tq[:, None] - kpos).astype(jnp.float32)[:, :, None]
        s_s = jnp.einsum('bqgjd,bgqkd->bgjqk', qb, ks).astype(jnp.float32) * scale - slopes * dist_s
        p_s = masked_softmax(s_s, dist_s >= 0)
        o_s = jnp.einsum('bgjqk,bgqkd->bqgjd', p_s.astype(vs.dtype), vs)
        kw = lax.dynamic_slice_in_dim(k_win_p, qs, Q_BLOCK + NSA_WINDOW, 1)
        vw = lax.dynamic_slice_in_dim(v_win_p, qs, Q_BLOCK + NSA_WINDOW, 1)
        kpos_w = qs + win_offsets
        dist_w = tq[:, None] - kpos_w[None, :]
        mask_w = (dist_w >= 0) & (dist_w < NSA_WINDOW) & (kpos_w[None, :] >= 0)
        s_w = jnp.einsum('bqgjd,bkgd->bgjqk', qb, kw).astype(jnp.float32) * scale - slopes * dist_w.astype(jnp.float32)
        p_w = masked_softmax(s_w, mask_w)
        o_w = jnp.einsum('bgjqk,bkgd->bqgjd', p_w.astype(vw.dtype), vw)
        g = lax.dynamic_slice_in_dim(gates, qs, Q_BLOCK, 1)
        return g[..., 0:1] * o_c + g[..., 1:2] * o_s + g[..., 2:3] * o_w

    o = blocks_to_seq(lax.map(block, jnp.arange(S // Q_BLOCK)))
    return o.reshape(B, S, H * dh)

def dilated_attention(q, k, v):
    B, S, H, dh = q.shape
    scale = dh ** -0.5
    slopes = alibi_slopes(H)
    hpg = DIL_HEADS_PER_GROUP
    k_groups = [k[:, :, g * hpg:(g + 1) * hpg] for g in range(len(DIL_CONFIGS))]
    v_groups = [v[:, :, g * hpg:(g + 1) * hpg] for g in range(len(DIL_CONFIGS))]

    def block(i):
        qs = i * Q_BLOCK
        tq = qs + jnp.arange(Q_BLOCK)
        qb = lax.dynamic_slice_in_dim(q, qs, Q_BLOCK, 1)
        outs, lses = [], []
        for g, (window, dilation) in enumerate(DIL_CONFIGS):
            steps = jnp.arange(window // dilation + 1) * dilation
            kidx = tq[:, None] - steps[None, :]
            valid = kidx >= 0
            kidx = jnp.maximum(kidx, 0)
            kg = k_groups[g][:, kidx]
            vg = v_groups[g][:, kidx]
            s = jnp.einsum('bqhd,bqkhd->bhqk', qb[:, :, g * hpg:(g + 1) * hpg], kg).astype(jnp.float32) * scale
            s = s - slopes[g * hpg:(g + 1) * hpg][:, None, None] * steps.astype(jnp.float32)
            s = jnp.where(valid, s, MASK_VALUE)
            lse = jax.nn.logsumexp(s, axis=-1)
            p = jnp.exp(s - lse[..., None])
            outs.append(jnp.einsum('bhqk,bqkhd->bqhd', p.astype(vg.dtype), vg))
            lses.append(lse)
        w = jax.nn.softmax(jnp.stack(lses, axis=0), axis=0).transpose(0, 1, 3, 2)[..., None]
        return jnp.concatenate([o * w[g].astype(o.dtype) for g, o in enumerate(outs)], axis=2)

    o = blocks_to_seq(lax.map(block, jnp.arange(S // Q_BLOCK)))
    return o.reshape(B, S, H * dh)

def diff_attention(q, k, v, lam_vecs, subln_g, lam_init):
    B, S, H, _, dq = q.shape
    dv = v.shape[-1]
    scale = dq ** -0.5
    lv = lam_vecs.astype(jnp.float32)
    lam = jnp.exp(jnp.sum(lv[0] * lv[1])) - jnp.exp(jnp.sum(lv[2] * lv[3])) + lam_init
    slopes = alibi_slopes(H)[None, :, None, None, None]
    pos = jnp.arange(S)

    def block(i):
        qs = i * Q_BLOCK
        tq = qs + jnp.arange(Q_BLOCK)
        qb = lax.dynamic_slice_in_dim(q, qs, Q_BLOCK, 1)
        dist = tq[:, None] - pos[None, :]
        s = jnp.einsum('bqhmd,bkhmd->bhmqk', qb, k).astype(jnp.float32) * scale - slopes * dist.astype(jnp.float32)
        p = jax.nn.softmax(jnp.where(dist >= 0, s, MASK_VALUE), axis=-1)
        a = p[:, :, 0] - lam * p[:, :, 1]
        return jnp.einsum('bhqk,bkhd->bqhd', a.astype(v.dtype), v)

    o = blocks_to_seq(lax.map(block, jnp.arange(S // Q_BLOCK)))
    o = rms_norm(o, subln_g) * (1.0 - lam_init)
    return o.reshape(B, S, H * dv)

def hybrid_mixer(u, w_in, fox_f_bias, cmp_w1, cmp_w2, cmp_pos, diff_lambda, diff_subln_g, diff_lam_init, w_out):
    B, S, _ = u.shape
    proj = u @ w_in
    offsets = [int(o) for o in np.cumsum([w for _, w in IN_SPLITS])[:-1]]
    p = dict(zip([n for n, _ in IN_SPLITS], jnp.split(proj, offsets, axis=-1)))

    def hd(name, *shape):
        return p[name].reshape(B, S, *shape)

    o_fox = fox_attention(hd('fox_q', FOX_HEADS, HEAD_DIM), hd('fox_k', FOX_HEADS, HEAD_DIM),
                          hd('fox_v', FOX_HEADS, HEAD_DIM), p['fox_f'], fox_f_bias)
    o_nsa = nsa_attention(hd('nsa_q', NSA_HEADS, HEAD_DIM),
                          hd('nsa_cmp_k', NSA_KV_GROUPS, HEAD_DIM), hd('nsa_cmp_v', NSA_KV_GROUPS, HEAD_DIM),
                          hd('nsa_slc_k', NSA_KV_GROUPS, HEAD_DIM), hd('nsa_slc_v', NSA_KV_GROUPS, HEAD_DIM),
                          hd('nsa_win_k', NSA_KV_GROUPS, HEAD_DIM), hd('nsa_win_v', NSA_KV_GROUPS, HEAD_DIM),
                          hd('nsa_gate', NSA_HEADS, 3), cmp_w1, cmp_w2, cmp_pos)
    o_dil = dilated_attention(hd('dil_q', DIL_HEADS, HEAD_DIM), hd('dil_k', DIL_HEADS, HEAD_DIM),
                              hd('dil_v', DIL_HEADS, HEAD_DIM))
    o_diff = diff_attention(hd('diff_q', DIFF_HEADS, 2, DIFF_QK_DIM), hd('diff_k', DIFF_HEADS, 2, DIFF_QK_DIM),
                            hd('diff_v', DIFF_HEADS, DIFF_V_DIM), diff_lambda, diff_subln_g, diff_lam_init)
    o = jnp.concatenate([o_fox, o_nsa, o_dil, o_diff], axis=-1)
    return o @ w_out

def swiglu(u, w_gate, w_up, w_down):
    return (jax.nn.silu(u @ w_gate) * (u @ w_up)) @ w_down

def second_inputs(seed: int = 0) -> dict:
    key = jax.random.key(seed)
    ks = jax.random.split(key, 18)
    D = D_MODEL

    def nrm(k, shape, scale):
        return jax.random.normal(k, shape, jnp.float32) * scale

    return {
        'x': nrm(ks[0], (BATCH, SEQ, D), 1.0),
        'c': nrm(ks[1], (BATCH, D), 1.0),
        'ada_w': nrm(ks[2], (DEPTH, D, 6 * D), 0.5 * D ** -0.5),
        'ada_b': nrm(ks[3], (DEPTH, 6 * D), 0.02),
        'norm_mix_g': 1.0 + nrm(ks[4], (DEPTH, D), 0.02),
        'norm_ffn_g': 1.0 + nrm(ks[5], (DEPTH, D), 0.02),
        'w_in': nrm(ks[6], (DEPTH, D, N_IN), D ** -0.5),
        'fox_f_bias': 3.0 + nrm(ks[7], (DEPTH, FOX_HEADS), 0.5),
        'nsa_cmp_w1': nrm(ks[8], (DEPTH, 2, NSA_CMP_LEN * HEAD_DIM, HEAD_DIM), (NSA_CMP_LEN * HEAD_DIM) ** -0.5),
        'nsa_cmp_w2': nrm(ks[9], (DEPTH, 2, HEAD_DIM, HEAD_DIM), 1.5 * HEAD_DIM ** -0.5),
        'nsa_cmp_pos': nrm(ks[10], (DEPTH, 2, NSA_CMP_LEN, HEAD_DIM), 0.1),
        'diff_lambda': nrm(ks[11], (DEPTH, 4, DIFF_QK_DIM), 0.1),
        'diff_subln_g': 1.0 + nrm(ks[12], (DEPTH, DIFF_V_DIM), 0.02),
        'w_out': nrm(ks[13], (DEPTH, MIX_WIDTH, D), MIX_WIDTH ** -0.5),
        'ffn_w_gate': nrm(ks[14], (DEPTH, D, D_FF_2), D ** -0.5),
        'ffn_w_up': nrm(ks[15], (DEPTH, D, D_FF_2), D ** -0.5),
        'ffn_w_down': nrm(ks[16], (DEPTH, D_FF_2, D), D_FF_2 ** -0.5),
        'final_norm_g': 1.0 + nrm(ks[17], (D,), 0.02),
    }

def second_block(x, c, ada_w, ada_b, norm_mix_g, norm_ffn_g, w_in, fox_f_bias, nsa_cmp_w1, nsa_cmp_w2,
              nsa_cmp_pos, diff_lambda, diff_subln_g, w_out, ffn_w_gate, ffn_w_up, ffn_w_down, final_norm_g):
    c_act = jax.nn.silu(c)
    h = x
    for layer in range(DEPTH):
        mod = c_act @ ada_w[layer] + ada_b[layer]
        sh1, sc1, g1, sh2, sc2, g2 = [m[:, None, :] for m in jnp.split(mod, 6, axis=-1)]
        lam_init = 0.8 - 0.6 * math.exp(-0.3 * layer)
        u = rms_norm(h, norm_mix_g[layer]) * (1.0 + sc1) + sh1
        h = h + g1 * hybrid_mixer(u, w_in[layer], fox_f_bias[layer], nsa_cmp_w1[layer], nsa_cmp_w2[layer],
                                  nsa_cmp_pos[layer], diff_lambda[layer], diff_subln_g[layer], lam_init, w_out[layer])
        u = rms_norm(h, norm_ffn_g[layer]) * (1.0 + sc2) + sh2
        h = h + g2 * swiglu(u, ffn_w_gate[layer], ffn_w_up[layer], ffn_w_down[layer])
    return rms_norm(h, final_norm_g)


def setup_inputs(seed=0):
    out = dict(first_inputs(seed))
    for name, value in second_inputs(seed + 1).items():
        if name != "x":
            out[name + "_2"] = value
    return out


def reference(
    x, c, w_ada, b_ada, pre_mix_norm, post_mix_norm, pre_ffn_norm, post_ffn_norm, w_in,
    hg_lb_logits, hg_norm, gdn_conv_w, gdn_a_log, gdn_dt_bias, gdn_norm, w_out, w_ff1, w_ff2,
    c_2, ada_w_2, ada_b_2, norm_mix_g_2, norm_ffn_g_2, w_in_2, fox_f_bias_2, nsa_cmp_w1_2,
    nsa_cmp_w2_2, nsa_cmp_pos_2, diff_lambda_2, diff_subln_g_2, w_out_2, ffn_w_gate_2,
    ffn_w_up_2, ffn_w_down_2, final_norm_g_2,
):
    x = first_block(
        x, c, w_ada, b_ada, pre_mix_norm, post_mix_norm, pre_ffn_norm, post_ffn_norm, w_in,
        hg_lb_logits, hg_norm, gdn_conv_w, gdn_a_log, gdn_dt_bias, gdn_norm, w_out, w_ff1,
        w_ff2,
    )
    return second_block(
        x, c_2, ada_w_2, ada_b_2, norm_mix_g_2, norm_ffn_g_2, w_in_2, fox_f_bias_2,
        nsa_cmp_w1_2, nsa_cmp_w2_2, nsa_cmp_pos_2, diff_lambda_2, diff_subln_g_2, w_out_2,
        ffn_w_gate_2, ffn_w_up_2, ffn_w_down_2, final_norm_g_2,
    )


_drawn_inputs = setup_inputs


def setup_inputs(seed=0):
    import zlib

    import numpy as np

    out = dict(_drawn_inputs(seed))
    spreads = {}
    factors = {'post_mix_norm': 3.46,
     'pre_ffn_norm': 3.545,
     'post_ffn_norm': 3.823,
     'hg_norm': 4.441,
     'gdn_norm': 5.573,
     'ada_b_2': 2.953,
     'norm_mix_g_2': 8.0,
     'norm_ffn_g_2': 8.0,
     'fox_f_bias_2': 40.287,
     'nsa_cmp_pos_2': 7.829,
     'diff_lambda_2': 6.421,
     'diff_subln_g_2': 49.244,
     'final_norm_g_2': 21.22}
    for name, (base, spread) in spreads.items():
        noise = np.random.default_rng([zlib.crc32(name.encode()), seed]).standard_normal(out[name].shape)
        drawn = base * np.exp(spread * noise) if base else spread * noise
        out[name] = __import__('jax').numpy.asarray(drawn.astype(out[name].dtype))
    for name, factor in factors.items():
        out[name] = (out[name] * factor).astype(out[name].dtype)
    return out
```

```python
from contextlib import ExitStack

import numpy as np

import concourse.bass as bass
from concourse import mybir

ALU = mybir.AluOpType
ACT = mybir.ActivationFunctionType
AX = mybir.AxisListType
F32 = mybir.dt.float32
I32 = mybir.dt.int32

P = 128
SEQ = 256
TT = SEQ // P
D = 2048
KT = D // P
NMOD = 6 * KT
EPS = 1e-6

RING = 4
TURN = 8
KG = 4
CW = 512
NT = CW // P

HH = 8
HW = HH * P
LEVELS = [64, 32, 16, 8, 4, 2, 1]
D_FF = 4 * D
D_FF2 = 5632
N_IN2 = 5919

HQ, HF, HI, HG, GQ, GK, GV, GG = range(0, 64, 8)

VEC_PARTS = [("b_ada", 96), ("norms", 82), ("conv", 96), ("b_ada_2", 96), ("norms_2", 49), ("pos", 64)]
VEC_AT = {}
for _name, _rows in VEC_PARTS:
    VEC_AT[_name] = sum(r for n, r in VEC_PARTS[:len(VEC_AT)])
N_VEC = sum(r for _, r in VEC_PARTS)
C_BADA = VEC_AT["b_ada"]
C_PREMIX, C_POSTMIX, C_PREFFN, C_POSTFFN = (VEC_AT["norms"] + 16 * n for n in range(4))
C_HGNORM, C_GDNNORM, C_LB = (VEC_AT["norms"] + n for n in (64, 65, 66))
C_CONV = VEC_AT["conv"]
C_BADA2 = VEC_AT["b_ada_2"]
C_MIX2, C_FFN2, C_SUBLN, C_FINAL = (VEC_AT["norms_2"] + n for n in (0, 16, 32, 33))
C_POS = VEC_AT["pos"]


class Chain:

    def __init__(self, sem):
        self.sem, self.n = sem, 0

    def mark(self, ins):
        self.n += 1
        ins.then_inc(self.sem, 1)
        return self.n

    def link(self, eng, ins):
        eng.wait_ge(self.sem, self.mark(ins))


class Core:
    pass


def bcast(ap, n, axis=1):
    a = ap.unsqueeze(axis)
    return a.to_broadcast(list(a.shape[:axis]) + [n] + list(a.shape[axis + 1:]))



class Stream:

    def __init__(self, source, unit, turns, first):
        self.source, self.unit, self.turns, self.first = source, unit, turns, first
        self.groups = unit * turns


def by_columns(w, chunk0=0):
    v = w.rearrange("(g k p) n -> p g k n", p=P, k=KG)
    return lambda i, q: v[:, q % 4, :, bass.ds((i * 2 + (q // 4 + chunk0)) * CW, CW)]


def refill(sp, core, stream, i, q):
    slot = q % RING
    if isinstance(i, int):
        g = stream.first + stream.unit * i + q
        slot = g % RING
        if g >= RING:
            sp.wait_ge(core.used, g - RING + 1)
    else:
        sp.wait_ge(core.used, i * stream.unit + (stream.first + q - RING + 1))
    src = stream.source(i, q)
    sp.dma_start(core.ring[:, slot, 0:src.shape[1], 0:src.shape[2]], src).then_inc(core.landed[slot], 16)


def prefetch(sp, core, stream):
    for g in range(RING):
        refill(sp, core, stream, g // stream.unit, g % stream.unit)


def load_rest(sp, core, stream):
    if stream.unit % RING == 0:
        with sp.Fori(0, stream.turns - 1) as i:
            for q in range(RING, stream.unit):
                refill(sp, core, stream, i, q)
            for q in range(RING):
                refill(sp, core, stream, i + 1, q)
        for q in range(RING, stream.unit):
            refill(sp, core, stream, stream.turns - 1, q)
    else:
        for g in range(RING, stream.groups):
            refill(sp, core, stream, g // stream.unit, g % stream.unit)



def phase_setup(nc, core, t):
    vec_rows = core.big[:, 16:19, :].rearrange("p a b -> p (a b)").rearrange("p (v n) -> p v n", n=P)
    c_rows = core.big[0:32, 20, 0:P]
    x_rows = core.big[:, 0:16, :].rearrange("p a b -> p (a b)").rearrange("p (t f) -> p t f", t=TT)
    with ExitStack() as ctx:
        x_in, vec_in, c_in, small_in, ones_done, ident_done, vec_t, c_t, x_t, x_free, made = (
            ctx.enter_context(nc.semaphore(n)) for n in
            ("x_in", "vec_in", "c_in", "small_in", "ones_done", "ident_done", "vec_t", "c_t", "x_t", "x_free",
             "made"))
        lb_tmp = ctx.enter_context(nc.sbuf_tensor("lb_tmp", [P, 4, HH], F32))
        block = ctx.enter_context(nc.Block())

        @block.sync
        def _(sp):
            rows = lambda a, r: a.rearrange("l n -> (l n)").rearrange("(r p) -> r p", p=P)
            sp.dma_start(c_rows[0:KT], rows(t["c"], KT)).then_inc(c_in, 16)
            sp.dma_start(c_rows[KT:2 * KT], rows(t["c_2"], KT)).then_inc(c_in, 16)
            sp.dma_start(x_rows, t["x"][0].rearrange("(t p) f -> p t f", p=P)).then_inc(x_in, 16)

        @block.scalar
        def _(act):
            def load(part, at, src):
                act.dma_start(vec_rows[at:at + src.shape[0], part, 0:src.shape[1]], src).then_inc(vec_in, 16)

            rows = lambda a: a.rearrange("l n -> (l n)").rearrange("(r p) -> r p", p=P)
            load(0, 0, rows(t["b_ada"]))
            for n, name in enumerate(("pre_mix_norm", "post_mix_norm", "pre_ffn_norm", "post_ffn_norm")):
                load(1, 16 * n, rows(t[name]))
            load(1, 64, t["hg_norm"])
            load(1, 65, t["gdn_norm"])
            load(1, 66, t["hg_lb_logits"].rearrange("l h d -> (l h) d"))
            load(2, 0, t["gdn_conv_w"][0].rearrange("k (c p) -> (k c) p", p=P))
            load(3, 0, rows(t["ada_b_2"]))
            load(4, 0, rows(t["norm_mix_g_2"]))
            load(4, 16, rows(t["norm_ffn_g_2"]))
            load(4, 32, t["diff_subln_g_2"])
            load(4, 33, t["final_norm_g_2"].rearrange("(r p) -> r p", p=P))
            pos = t["nsa_cmp_pos_2"][0].rearrange("a l d -> (a l) d")
            load(5, 0, pos)
            act.dma_start(vec_rows[0:64, 5, 64:128], pos).then_inc(vec_in, 16)
            with nc.allow_non_contiguous_dma("eight numbers, one a partition"):
                act.dma_start(core.gdn_cols[:, 0:1], t["gdn_a_log"].rearrange("l h -> h l")).then_inc(small_in, 16)
                act.dma_start(core.gdn_cols[:, 1:2], t["gdn_dt_bias"].rearrange("l h -> h l")).then_inc(small_in, 16)
            with nc.allow_non_contiguous_dma("the 16 gate columns"):
                act.dma_start(core.w_gates[:], t["w_in"][0, :, 8192:8208].rearrange("(k p) n -> p k n", p=P)
                              ).then_inc(small_in, 16)
            act.wait_ge(c_t, 1)
            core.act.mark(nc.scalar.activation(core.c_act[:], core.ps[:, 5, 0:2 * KT], ACT.Silu))
            for j in range(KT // 2):
                act.wait_ge(x_t, j + 1)
                nc.scalar.activation(core.xT[:, 2 * j:2 * j + 2, :], core.ps[:, j % 4, :], ACT.Copy
                                     ).then_inc(x_free, 1)
            act.wait_ge(made, 2)
            core.act.link(act, nc.scalar.activation(lb_tmp[:, 1, :], lb_tmp[:, 0, :], ACT.Exp))
            core.act.link(act, nc.scalar.activation(lb_tmp[:, 2, :], lb_tmp[:, 3, :], ACT.Exp))
            act.wait_ge(small_in, 48)
            core.act.link(act, nc.scalar.activation(core.gdn_cols[:, 2:3], core.gdn_cols[:, 0:1], ACT.Exp))

        @block.gpsimd
        def _(pool):
            nc.gpsimd.memset(core.ident[:], 0.0).then_inc(core.pool.sem, 1)
            core.pool.n += 1
            pool.wait_ge(core.pool.sem, core.pool.n)
            nc.gpsimd.affine_select(out=core.ident[:], in_=core.ident[:], compare_op=ALU.not_equal, fill=1.0,
                                    base=0, pattern=[[-1, P]], channel_multiplier=1).then_inc(ident_done, 1)
            nc.gpsimd.memset(core.ones[:], 1.0).then_inc(ones_done, 1)
            pool.wait_ge(ones_done, 1)
            nc.gpsimd.affine_select(out=core.incl[:], in_=core.ones[:], compare_op=ALU.is_ge, fill=0.0,
                                    base=0, pattern=[[1, P]], channel_multiplier=-1)
            nc.gpsimd.affine_select(out=core.strict[:], in_=core.ones[:], compare_op=ALU.is_gt, fill=0.0,
                                    base=0, pattern=[[1, P]], channel_multiplier=-1)
            for n, L in enumerate(LEVELS):
                nb = P // (2 * L)
                for m, lo in ((core.up_mask, 0), (core.low_mask, L)):
                    v = m[:, n, :].rearrange("p (b two l) -> p b two l", b=nb, two=2)
                    o = core.ones[:].rearrange("p (b two l) -> p b two l", b=nb, two=2)
                    half = 1 if lo == 0 else 0
                    core.pool.link(pool, nc.gpsimd.memset(m[:, n, :], 0.0))
                    core.pool.link(pool, nc.gpsimd.affine_select(
                        out=v[:, :, half, :], in_=o[:, :, half, :], compare_op=ALU.is_ge, fill=0.0, base=-lo,
                        pattern=[[-2 * L, nb], [0, L]], channel_multiplier=1))
                    core.pool.link(pool, nc.gpsimd.affine_select(
                        out=v[:, :, half, :], in_=v[:, :, half, :], compare_op=ALU.is_gt, fill=0.0, base=lo + L,
                        pattern=[[2 * L, nb], [0, L]], channel_multiplier=-1))
            core.pool.link(pool, nc.gpsimd.memset(core.keep[:], 1.0))
            core.pool.link(pool, nc.gpsimd.memset(core.eps[:], EPS))
            core.pool.link(pool, nc.gpsimd.memset(core.one[:], 1.0))
            core.pool.link(pool, nc.gpsimd.memset(core.keep[:].rearrange("p (c t) -> p c t", c=TT)[:, :, 0:1], 0.0))
            core.pool.link(pool, nc.gpsimd.memset(core.pick[:], 0.0))
            core.pool.link(pool, nc.gpsimd.affine_select(
                out=core.pick[:], in_=core.pick[:], compare_op=ALU.not_equal, fill=1.0, base=0,
                pattern=[[-1, HH], [0, P]], channel_multiplier=1))

        @block.tensor
        def _(pe):
            pe.wait_ge(ident_done, 1)
            pe.wait_ge(c_in, 32)
            nc.tensor.transpose(core.ps[:, 5, 0:2 * KT], c_rows, core.ident[0:32, 0:32]).then_inc(c_t, 1)
            pe.wait_ge(x_in, 16)
            for j in range(KT // 2):
                if j >= 4:
                    pe.wait_ge(x_free, j - 3)
                for f in range(2):
                    for tt in range(TT):
                        ins = nc.tensor.transpose(core.ps[:, j % 4, (f * TT + tt) * P:(f * TT + tt + 1) * P],
                                                  x_rows[:, tt, (2 * j + f) * P:(2 * j + f + 1) * P], core.ident[:])
                ins.then_inc(x_t, 1)
            pe.wait_ge(vec_in, 16 * 16)
            for n, (name, rows) in enumerate(VEC_PARTS):
                ins = nc.tensor.transpose(core.ps[:, 4, VEC_AT[name]:VEC_AT[name] + rows],
                                          vec_rows[0:rows, n, :], core.ident[0:rows, 0:rows])
            ins.then_inc(vec_t, 1)

        @block.vector
        def _(dve):
            v = core.dve
            for f in (core.free[0], core.free[1]):
                dve.sem_inc(f, NT)
            dve.wait_ge(vec_t, 1)
            v.link(dve, nc.vector.tensor_copy(core.cols[:], core.ps[:, 4, 0:N_VEC]))
            a, b = core.cols[:, C_LB:C_LB + HH], core.cols[:, C_LB + HH:C_LB + 2 * HH]
            v.link(dve, nc.vector.tensor_tensor(lb_tmp[:, 3, :], a, b, ALU.max))
            nc.vector.tensor_tensor(lb_tmp[:, 0, :], a, lb_tmp[:, 3, :], ALU.subtract).then_inc(made, 1)
            nc.vector.tensor_tensor(lb_tmp[:, 3, :], b, lb_tmp[:, 3, :], ALU.subtract).then_inc(made, 1)
            dve.wait_ge(core.act.sem, 4)
            v.link(dve, nc.vector.tensor_tensor(lb_tmp[:, 2, :], lb_tmp[:, 1, :], lb_tmp[:, 2, :], ALU.add))
            v.link(dve, nc.vector.reciprocal(lb_tmp[:, 2, :], lb_tmp[:, 2, :]))
            v.link(dve, nc.vector.tensor_tensor(core.lb[:, 0, :], lb_tmp[:, 1, :], lb_tmp[:, 2, :], ALU.mult))
            v.link(dve, nc.vector.tensor_scalar(core.lb[:, 1, :], core.lb[:, 0, :], -1.0, 1.0, ALU.mult, ALU.add))
            v.link(dve, nc.vector.tensor_scalar(core.gdn_cols[:, 3:4], core.gdn_cols[:, 2:3], -1.0, None, ALU.mult))



AK = 2
ASLOTS = 4
ATURN = 2
AGROUPS = KT // AK


class Ada:

    def __init__(self, ctx, nc, core, w, which, chunk0, turns):
        self.nc, self.core, self.which, self.chunk0, self.turns = nc, core, which, chunk0, turns
        self.w = w.rearrange("(g k p) n -> p g k n", p=P, k=AK)
        self.before = core.ada_turns
        core.ada_turns += turns
        sb = lambda name, shape: ctx.enter_context(nc.sbuf_tensor(name, shape, F32))
        self.ring = sb(f"ada_weights_{self.before}", [P, ASLOTS, AK, CW])
        self.acc = sb(f"ada_sums_{self.before}", [P, ATURN, 2, CW])
        self.row = sb(f"ada_row_{self.before}", [1, ATURN, CW])

    def load(self, pool, i, q):
        chunk = i * ATURN + (q // AGROUPS + self.chunk0)
        pool.dma_start(self.ring[:, q % ASLOTS], self.w[:, q % AGROUPS, :, bass.ds(chunk * CW, CW)]
                       ).then_inc(self.core.ada_landed[q % ASLOTS], 16)

    def load_when_free(self, pool, i, q):
        steps = AK * AGROUPS * ATURN
        pool.wait_ge(self.core.ada_steps, i * steps + (self.before * steps + AK * (q - ASLOTS + 1)))
        self.load(pool, i, q)

    def loads(self, pool):
        n = ATURN * AGROUPS
        for q in range(ASLOTS):
            self.load(pool, 0, q)
        with pool.Fori(0, self.turns - 1) as i:
            for q in range(ASLOTS, n):
                self.load_when_free(pool, i, q)
            for q in range(ASLOTS):
                self.load_when_free(pool, i + 1, q)
        for q in range(ASLOTS, n):
            self.load_when_free(pool, self.turns - 1, q)

    def multiply(self, dve, i):
        nc, core = self.nc, self.core
        per_slot = ATURN * AGROUPS // ASLOTS
        dve.wait_ge(core.ada_rows_ready, i * ATURN + self.before * ATURN)
        for c in range(ATURN):
            for k in range(KT):
                q = c * AGROUPS + k // AK
                if k % AK == 0:
                    dve.wait_ge(core.ada_landed[q % ASLOTS],
                                i * (16 * per_slot) + 16 * (self.before * per_slot + q // ASLOTS + 1))
                w = self.ring[:, q % ASLOTS, k % AK, :]
                acc = self.acc[:, c, k % 2, :]
                number = core.c_act[:, KT * self.which + k:KT * self.which + k + 1]
                if k < 2:
                    ins = nc.vector.tensor_scalar(acc, w, number, None, ALU.mult)
                else:
                    dve.wait_ge(core.ada_steps, i * (KT * ATURN) + (self.before * KT * ATURN + KT * c + k - 1))
                    ins = nc.vector.scalar_tensor_tensor(out=acc, in0=w, scalar=number, in1=acc, op0=ALU.mult,
                                                         op1=ALU.add)
                ins.then_inc(core.ada_steps, 1)
            dve.wait_ge(core.ada_steps, i * (KT * ATURN) + (self.before * KT * ATURN + KT * (c + 1)))
            nc.vector.tensor_tensor(self.acc[:, c, 0, :], self.acc[:, c, 0, :], self.acc[:, c, 1, :], ALU.add
                                    ).then_inc(core.ada_sums_ready, 1)

    def sum_rows(self, pe, i, bank0):
        nc, core = self.nc, self.core
        for c in range(ATURN):
            pe.wait_ge(core.ada_sums_ready, i * ATURN + (self.before * ATURN + c + 1))
            for h in range(2):
                ins = nc.tensor.matmul(core.ps[0:1, bank0 + 2 * c + h, SEQ:2 * SEQ], core.ones[:, 0:1],
                                       self.acc[:, c, 0, h * SEQ:(h + 1) * SEQ], start=True, stop=True)
            ins.then_inc(core.ada_rows_ready, 1)
        pe.wait_ge(core.ada_rows_taken, i + (self.before + 1))

    def store_rows(self, act, i, bank0):
        nc, core = self.nc, self.core
        act.wait_ge(core.ada_rows_ready, i * ATURN + (self.before * ATURN + ATURN))
        act.wait_ge(core.ada_stored, i * 16 + self.before * 16)
        nc.scalar.activation(self.row[:].rearrange("p c (h n) -> p (c h) n", h=2),
                             core.ps[0:1, bank0:bank0 + 2 * ATURN, SEQ:2 * SEQ], ACT.Copy).then_inc(core.ada_rows_taken, 1)
        act.wait_ge(core.ada_rows_taken, i + (self.before + 1))
        act.dma_start(core.mod_dram[self.which:self.which + 1, bass.ds((i * ATURN + self.chunk0) * CW, ATURN * CW)],
                      self.row[:].rearrange("p c n -> p (c n)")).then_inc(core.ada_stored, 16)


def phase_ada_first(nc, core, t):
    with ExitStack() as ctx:
        ada = Ada(ctx, nc, core, t["w_ada"][0], 0, 0, 4)
        block = ctx.enter_context(nc.Block())

        @block.sync
        def _(sp):
            prefetch(sp, core, core.streams["in_1"])

        @block.gpsimd
        def _(pool):
            ada.loads(pool)

        @block.vector
        def _(dve):
            with dve.Fori(0, ada.turns) as i:
                ada.multiply(dve, i)

        @block.tensor
        def _(pe):
            with pe.Fori(0, ada.turns) as i:
                ada.sum_rows(pe, i, 0)

        @block.scalar
        def _(act):
            with act.Fori(0, ada.turns) as i:
                ada.store_rows(act, i, 0)


def phase_modulation(nc, core, which, chunk0, chunks):
    n = NT * chunks
    with ExitStack() as ctx:
        rows_in, turned = core.mod_rows_in, core.mod_turned
        core.mods += 1
        rows = ctx.enter_context(nc.sbuf_tensor(f"mod_rows_{which}_{chunk0}", [n, P], F32))
        block = ctx.enter_context(nc.Block())

        @block.sync
        def _(sp):
            sp.wait_ge(core.ada_stored, 16 * core.ada_turns)
            src = core.mod_dram[which, chunk0 * CW:(chunk0 + chunks) * CW].rearrange("(r p) -> r p", p=P)
            sp.dma_start(rows[:], src).then_inc(rows_in, 16)

        @block.tensor
        def _(pe):
            pe.wait_ge(rows_in, 16 * core.mods)
            nc.tensor.transpose(core.ps[:, 7, 0:n], rows[:], core.ident[0:n, 0:n]).then_inc(turned, 1)

        @block.vector
        def _(dve):
            dve.wait_ge(turned, core.mods)
            bias = (C_BADA, C_BADA2)[which] + NT * chunk0
            core.dve.link(dve, nc.vector.tensor_tensor(core.mod[:, which, NT * chunk0:NT * chunk0 + n],
                                                       core.ps[:, 7, 0:n], core.cols[:, bias:bias + n], ALU.add))



def phase_norm(nc, core, gain, which=None, shift=None, scale=None):
    sq = core.big[:, 0:KT, :]
    n0 = core.norms
    core.norms += 1
    with ExitStack() as ctx:
        sq_ready, sums_ready, ms_ready, root_ready, inv_ready = core.norm_sems
        rs = ctx.enter_context(nc.sbuf_tensor(f"inv_rms_{gain}", [P, SEQ], F32))
        block = ctx.enter_context(nc.Block())

        @block.scalar
        def _(act):
            for n in range(4):
                nc.scalar.activation(sq[:, 4 * n:4 * n + 4, :], core.xT[:, 4 * n:4 * n + 4, :], ACT.Square
                                     ).then_inc(sq_ready, 1)
            act.wait_ge(ms_ready, n0 + 1)
            nc.scalar.activation(rs[:], rs[:], ACT.Sqrt).then_inc(root_ready, 1)
            for k in range(1, KT, 2):
                act.wait_ge(inv_ready, 4 * n0 + k // 4 + 1)
                if which is None:
                    nc.scalar.activation(core.hT[:, k, :], core.hT[:, k, :], ACT.Copy,
                                         scale=core.aff[:, 0, k:k + 1])
                else:
                    nc.scalar.activation(core.hT[:, k, :], core.hT[:, k, :], ACT.Identity,
                                         bias=core.mod[:, which, shift + k:shift + k + 1],
                                         scale=core.aff[:, 0, k:k + 1])

        @block.tensor
        def _(pe):
            for k in range(KT):
                if k % 4 == 0:
                    pe.wait_ge(sq_ready, 4 * n0 + k // 4 + 1)
                ins = nc.tensor.matmul(core.ps[:, 0, 0:SEQ], core.ones[:], sq[:, k, :],
                                       start=(k == 0), stop=(k == KT - 1))
            ins.then_inc(sums_ready, 1)

        @block.vector
        def _(dve):
            v = core.dve
            if which is None:
                v.link(dve, nc.vector.tensor_copy(core.aff[:, 0, :], core.cols[:, gain:gain + KT]))
            else:
                v.link(dve, nc.vector.scalar_tensor_tensor(
                    out=core.aff[:, 0, :], in0=core.mod[:, which, scale:scale + KT], scalar=1.0,
                    in1=core.cols[:, gain:gain + KT], op0=ALU.add, op1=ALU.mult))
            dve.wait_ge(sums_ready, n0 + 1)
            nc.vector.tensor_scalar(rs[:], core.ps[:, 0, 0:SEQ], 1.0 / D, EPS, ALU.mult, ALU.add
                                    ).then_inc(ms_ready, 1)
            dve.wait_ge(root_ready, n0 + 1)
            v.link(dve, nc.vector.reciprocal(rs[:], rs[:]))
            for n in range(4):
                nc.vector.tensor_tensor(core.hT[:, 4 * n:4 * n + 4, :], core.xT[:, 4 * n:4 * n + 4, :],
                                        bcast(rs[:], 4), ALU.mult).then_inc(inv_ready, 1)
            dve.wait_ge(inv_ready, 4 * n0 + 4)
            for k in range(0, KT, 2):
                if which is None:
                    nc.vector.tensor_scalar(core.hT[:, k, :], core.hT[:, k, :], core.aff[:, 0, k:k + 1], None,
                                            ALU.mult)
                else:
                    nc.vector.tensor_scalar(core.hT[:, k, :], core.hT[:, k, :], core.aff[:, 0, k:k + 1],
                                            core.mod[:, which, shift + k:shift + k + 1], ALU.mult, ALU.add)


def phase_residual_norm(nc, core, y, gain, gate):
    sq = core.big[:, 0:KT, :]
    n0 = core.norms
    core.norms += 1
    with ExitStack() as ctx:
        sq_ready, sums_ready, ms_ready, root_ready, scaled = core.norm_sems
        rs = ctx.enter_context(nc.sbuf_tensor(f"inv_rms_{gain}", [P, SEQ], F32))
        block = ctx.enter_context(nc.Block())

        @block.scalar
        def _(act):
            for n in range(4):
                nc.scalar.activation(sq[:, 4 * n:4 * n + 4, :], y[:, 4 * n:4 * n + 4, :], ACT.Square
                                     ).then_inc(sq_ready, 1)
            act.wait_ge(ms_ready, n0 + 1)
            nc.scalar.activation(rs[:], rs[:], ACT.Sqrt).then_inc(root_ready, 1)

        @block.tensor
        def _(pe):
            for k in range(KT):
                if k % 4 == 0:
                    pe.wait_ge(sq_ready, 4 * n0 + k // 4 + 1)
                ins = nc.tensor.matmul(core.ps[:, 0, 0:SEQ], core.ones[:], sq[:, k, :],
                                       start=(k == 0), stop=(k == KT - 1))
            ins.then_inc(sums_ready, 1)

        @block.vector
        def _(dve):
            v = core.dve
            v.link(dve, nc.vector.tensor_tensor(core.aff[:, 0, :], core.mod[:, 0, gate:gate + KT],
                                                core.cols[:, gain:gain + KT], ALU.mult))
            dve.wait_ge(sums_ready, n0 + 1)
            nc.vector.tensor_scalar(rs[:], core.ps[:, 0, 0:SEQ], 1.0 / D, EPS, ALU.mult, ALU.add
                                    ).then_inc(ms_ready, 1)
            dve.wait_ge(root_ready, n0 + 1)
            v.link(dve, nc.vector.reciprocal(rs[:], rs[:]))
            for n in range(4):
                nc.vector.tensor_tensor(core.hT[:, 4 * n:4 * n + 4, :], y[:, 4 * n:4 * n + 4, :],
                                        bcast(rs[:], 4), ALU.mult).then_inc(scaled, 1)
            dve.wait_ge(scaled, 4 * n0 + 4)
            for k in range(KT):
                nc.vector.scalar_tensor_tensor(out=core.xT[:, k, :], in0=core.hT[:, k, :],
                                               scalar=core.aff[:, 0, k:k + 1], in1=core.xT[:, k, :],
                                               op0=ALU.mult, op1=ALU.add)



def phase_product(nc, core, name, following, src, evacuate, on="act", ada=None):
    st = core.streams[name]
    per_chunk = 4 if st.unit == TURN else st.unit
    tr0, f0 = core.tiles_ready_n, list(core.claimed)
    chunks = st.unit // per_chunk
    with ExitStack() as ctx:
        ada = Ada(ctx, nc, core, *ada, st.turns) if ada else None
        block = ctx.enter_context(nc.Block())

        @block.sync
        def _(sp):
            load_rest(sp, core, st)
            if following:
                prefetch(sp, core, core.streams[following])

        @block.tensor
        def _(pe):
            with pe.Fori(0, st.turns) as i:
                for c in range(chunks):
                    for kg in range(per_chunk):
                        q = c * per_chunk + kg
                        fills = st.unit // RING
                        pe.wait_ge(core.landed[q % RING],
                                   i * (16 * fills) + 16 * ((st.first + q) // RING + 1))
                        for nt in range(NT):
                            if kg == 0:
                                pe.wait_ge(core.free[c], i * NT + (f0[c] + nt + 1))
                            for k in range(KG):
                                kt = KG * kg + k
                                ins = nc.tensor.matmul(core.ps[:, NT * c + nt, 0:SEQ],
                                                       core.ring[:, q % RING, k, nt * P:(nt + 1) * P], src(kt),
                                                       start=(kt == 0), stop=(kt == KG * per_chunk - 1))
                            if kg == per_chunk - 1 and nt < NT - 1:
                                ins.then_inc(core.tile_ready, 1)
                        ins.then_inc(core.used, 1)
                if ada:
                    if chunks == 2:
                        pe.wait_ge(core.free[0], i * NT + (f0[0] + 2 * NT))
                    ada.sum_rows(pe, i, 0 if chunks == 2 else NT)

        def empty(eng):
            with eng.Fori(0, st.turns) as i:
                for c in range(chunks):
                    for nt in range(NT):
                        if nt < NT - 1:
                            eng.wait_ge(core.tile_ready, i * (3 * chunks) + (tr0 + 3 * c + nt + 1))
                        else:
                            eng.wait_ge(core.used, i * st.unit + (st.first + per_chunk * (c + 1)))
                        evacuate(eng, i * (chunks * NT) + (c * NT + nt), core.ps[:, NT * c + nt, 0:SEQ]
                                 ).then_inc(core.free[c], 1)
                if ada:
                    ada.store_rows(eng, i, 0 if chunks == 2 else NT)

        if ada:
            @block.gpsimd
            def _(pool):
                ada.loads(pool)

            @block.vector
            def _(dve):
                with dve.Fori(0, ada.turns) as i:
                    ada.multiply(dve, i)

        if on == "act":
            @block.scalar
            def _(act):
                empty(act)
        else:
            @block.vector
            def _(dve):
                empty(dve)
    core.tiles_ready_n += 3 * chunks * st.turns
    for c in range(chunks):
        core.claimed[c] += NT * st.turns



class Banks:

    COUNT = 6

    def __init__(self, ctx, nc, uses):
        self.at, self.order = {}, []
        seen = {"act": 0, "dve": 0}
        for name, engine in uses:
            seen[engine] += 1
            self.at[name] = len(self.order)
            self.order.append((engine, seen[engine]))
        self.filled = ctx.enter_context(nc.semaphore("bank_filled"))
        self.emptied = {e: ctx.enter_context(nc.semaphore(f"bank_emptied_{e}")) for e in seen}

    def bank(self, name):
        return self.at[name] % self.COUNT

    def wait_empty(self, pe, name):
        before = self.at[name] - self.COUNT
        if before >= 0:
            engine, n = self.order[before]
            pe.wait_ge(self.emptied[engine], n)

    def wait_filled(self, eng, name):
        eng.wait_ge(self.filled, self.at[name] + 1)



def phase_hgrn(nc, core):
    big, ps = core.big, core.ps
    flat = lambda a, n: big[:, a:a + n, :].rearrange("p a b -> p (a b)")
    q_all, k_all = flat(HQ, HH), flat(HF, HH)
    NL = len(LEVELS) + 1
    uses = [("gates", "act")] + [(("v", n), "act") for n in range(4)] + [(("diag", n), "dve") for n in range(4)]
    uses += [(("cross", n), "act") for n in range(2)]
    uses += [(("level", l, n), "dve") for l in range(1, NL) for n in range(4)]
    uses += [(("o", n), "act") for n in range(4)] + [(("ss", n), "act") for n in range(4)]
    with ExitStack() as ctx:
        banks = Banks(ctx, nc, uses)
        sem = lambda n: ctx.enter_context(nc.semaphore(n))
        sig_ready, f_ready, lf_ready, k_ready, diff_ready, exp_ready, prod_ready, a_ready, v_ready, sq_ready, \
            rs_ready, silu_ready = (sem(n) for n in (
                "sig_ready", "f_ready", "lf_ready", "k_ready", "diff_ready", "exp_ready", "prod_ready", "a_ready",
                "v_ready", "sq_ready", "rs_ready", "silu_ready"))
        b = ctx.enter_context(nc.sbuf_tensor("log_decay", [P, HH * SEQ], F32))
        X = ctx.enter_context(nc.sbuf_tensor("scaled", [P, 2, HH * SEQ], F32))
        A = ctx.enter_context(nc.sbuf_tensor("attn_t", [P, HH, 3, P], F32))
        block = ctx.enter_context(nc.Block())

        @block.scalar
        def _(act):
            hf = flat(HF, HH)
            nc.scalar.activation(hf, hf, ACT.Sigmoid).then_inc(sig_ready, 1)
            for g in (HG, GG):
                nc.scalar.activation(flat(g, HH), flat(g, HH), ACT.Silu).then_inc(silu_ready, 1)
            banks.wait_filled(act, "gates")
            nc.scalar.activation(core.gates[:], ps[0:HH, banks.bank("gates"), :], ACT.Copy
                                 ).then_inc(banks.emptied["act"], 1)
            act.wait_ge(f_ready, 1)
            nc.scalar.activation(X[:, 1, :], X[:, 0, :], ACT.Ln).then_inc(lf_ready, 1)
            for n in range(4):
                banks.wait_filled(act, ("v", n))
                nc.scalar.activation(big[:, HI + 2 * n:HI + 2 * n + 2, :], ps[:, banks.bank(("v", n)), :], ACT.Copy
                                     ).then_inc(banks.emptied["act"], 1)
            for l in range(NL):
                act.wait_ge(diff_ready, l + 1)
                nc.scalar.activation(X[:, l % 2, :], X[:, l % 2, :], ACT.Exp).then_inc(exp_ready, 1)
                if l == 1:
                    for n in range(2):
                        banks.wait_filled(act, ("cross", n))
                        nc.scalar.activation(A[:, 4 * n:4 * n + 4, 2, :],
                                             ps[:, banks.bank(("cross", n)), :].rearrange("p (h t) -> p h t", h=4),
                                             ACT.Copy).then_inc(banks.emptied["act"], 1)
            for n in range(4):
                banks.wait_filled(act, ("o", n))
                pso = ps[:, banks.bank(("o", n)), :]
                nc.scalar.activation(X[:, 0, 512 * n:512 * n + 512], pso, ACT.Square).then_inc(sq_ready, 1)
                nc.scalar.activation(core.hT[:, 2 * n:2 * n + 2, :], pso, ACT.Copy
                                     ).then_inc(banks.emptied["act"], 1)
            for n in range(4):
                banks.wait_filled(act, ("ss", n))
                core.act.link(act, nc.scalar.activation(X[:, 1, 512 * n:512 * n + 512],
                                                        ps[:, banks.bank(("ss", n)), :], ACT.Ln,
                                                        bias=core.eps[:], scale=1.0 / P))
            nc.scalar.activation(X[:, 1, :], X[:, 1, :], ACT.Exp, scale=-0.5).then_inc(rs_ready, 1)

        @block.tensor
        def _(pe):
            bank = banks.bank("gates")
            for m in range(2):
                for k in range(KT):
                    ins = nc.tensor.matmul(ps[0:HH, bank, m * SEQ:(m + 1) * SEQ], core.w_gates[:, k, m * HH:(m + 1) * HH],
                                           core.hT[:, k, :], start=(k == 0), stop=(k == KT - 1))
            ins.then_inc(banks.filled, 1)
            for n in range(4):
                for j in range(4):
                    ins = nc.tensor.transpose(ps[:, banks.bank(("v", n)), j * P:(j + 1) * P],
                                              big[:, HI + 2 * n + j // 2, (j % 2) * P:(j % 2 + 1) * P], core.ident[:])
                ins.then_inc(banks.filled, 1)
            pe.wait_ge(k_ready, 1)
            for n in range(4):
                banks.wait_empty(pe, ("diag", n))
                for j in range(4):
                    at = n * 512 + j * P
                    ins = nc.tensor.matmul(ps[:, banks.bank(("diag", n)), j * P:(j + 1) * P], k_all[:, at:at + P],
                                           q_all[:, at:at + P], start=True, stop=True)
                ins.then_inc(banks.filled, 1)
            for l in range(NL):
                pe.wait_ge(prod_ready, l + 1)
                if l == 0:
                    for n in range(2):
                        banks.wait_empty(pe, ("cross", n))
                        for j in range(4):
                            at = (4 * n + j) * SEQ
                            ins = nc.tensor.matmul(ps[:, banks.bank(("cross", n)), j * P:(j + 1) * P],
                                                   X[:, 0, at:at + P], X[:, 0, at + P:at + SEQ],
                                                   start=True, stop=True)
                        ins.then_inc(banks.filled, 1)
                else:
                    for n in range(4):
                        banks.wait_empty(pe, ("level", l, n))
                        for j in range(4):
                            at = n * 512 + j * P
                            ins = nc.tensor.matmul(ps[:, banks.bank(("level", l, n)), j * P:(j + 1) * P],
                                                   X[:, l % 2, at:at + P], X[:, l % 2, at:at + P],
                                                   start=True, stop=True)
                        ins.then_inc(banks.filled, 1)
            pe.wait_ge(banks.emptied["act"], 7)
            pe.wait_ge(a_ready, 1)
            for n in range(4):
                banks.wait_empty(pe, ("o", n))
                for j in range(2):
                    h = 2 * n + j
                    out = ps[:, banks.bank(("o", n)), j * SEQ:(j + 1) * SEQ]
                    v0, v1 = big[:, HI + h, 0:P], big[:, HI + h, P:SEQ]
                    nc.tensor.matmul(out[:, 0:P], v0, A[:, h, 0, :], start=True, stop=True)
                    nc.tensor.matmul(out[:, P:SEQ], v0, A[:, h, 2, :], start=True, stop=False)
                    ins = nc.tensor.matmul(out[:, P:SEQ], v1, A[:, h, 1, :], start=False, stop=True)
                ins.then_inc(banks.filled, 1)
            for n in range(4):
                banks.wait_empty(pe, ("ss", n))
                pe.wait_ge(sq_ready, n + 1)
                nc.tensor.matmul(ps[:, banks.bank(("ss", n)), :], core.ones[:], X[:, 0, 512 * n:512 * n + 512],
                                 start=True, stop=True).then_inc(banks.filled, 1)

        @block.vector
        def _(dve):
            v = core.dve
            dve.wait_ge(sig_ready, 1)
            for h in range(HH):
                ins = nc.vector.tensor_scalar(X[:, 0, h * SEQ:(h + 1) * SEQ], big[:, HF + h, :], core.lb[:, 1, h:h + 1],
                                              core.lb[:, 0, h:h + 1], ALU.mult, ALU.add)
            ins.then_inc(f_ready, 1)
            dve.wait_ge(f_ready, 1)
            nc.vector.tensor_scalar(k_all, X[:, 0, :], -1.0, 1.0, ALU.mult, ALU.add).then_inc(k_ready, 1)
            dve.wait_ge(lf_ready, 1)
            for h in range(HH):
                ins = nc.vector.tensor_tensor_scan(b[:, h * SEQ:(h + 1) * SEQ], core.keep[:],
                                                   X[:, 1, h * SEQ:(h + 1) * SEQ], 0.0, ALU.mult, ALU.add)
            v.link(dve, ins)

            def halves(a, L):
                w = a.rearrange("p (n two l) -> p n two l", two=2, l=L)
                return w[:, :, 0, :], w[:, :, 1, :]

            def level_L(l):
                return P if l == 0 else LEVELS[l - 1]

            def diffs(l):
                L = level_L(l)
                if l >= 2:
                    banks.wait_filled(dve, ("cross", 1) if l == 2 else ("level", l - 2, 3))
                b0, b1 = halves(b[:], L)
                x0, x1 = halves(X[:, l % 2, :], L)
                ref = b0[:, :, L - 1:L].to_broadcast(list(b0.shape))
                nc.vector.tensor_tensor(x0, ref, b0, ALU.subtract)
                if l == 0:
                    nc.vector.tensor_copy(x1, b1).then_inc(diff_ready, 1)
                else:
                    nc.vector.tensor_tensor(x1, b1, ref, ALU.subtract).then_inc(diff_ready, 1)

            def products(l):
                L = level_L(l)
                x0, x1 = halves(X[:, l % 2, :], L)
                k0, _ = halves(k_all, L)
                _, q1 = halves(q_all, L)
                dve.wait_ge(exp_ready, l + 1)
                nc.vector.tensor_tensor(x0, x0, k0, ALU.mult)
                nc.vector.tensor_tensor(x1, x1, q1, ALU.mult).then_inc(prod_ready, 1)

            def take(l):
                for n in range(4):
                    banks.wait_filled(dve, ("level", l, n))
                    nc.vector.copy_predicated(
                        A[:, 2 * n:2 * n + 2, 0:2, :],
                        bcast(bcast(core.up_mask[:, l - 1, :].bitcast(I32), 2), 2),
                        ps[:, banks.bank(("level", l, n)), :].rearrange("p (h c t) -> p h c t", h=2, c=2)
                    ).then_inc(banks.emptied["dve"], 1)

            diffs(0)
            for n in range(4):
                banks.wait_filled(dve, ("diag", n))
                nc.vector.tensor_tensor(A[:, 2 * n:2 * n + 2, 0:2, :],
                                        ps[:, banks.bank(("diag", n)), :].rearrange("p (h c t) -> p h c t", h=2, c=2),
                                        bcast(bcast(core.ident[:], 2), 2), ALU.mult
                                        ).then_inc(banks.emptied["dve"], 1)
            dve.wait_ge(banks.emptied["dve"], 4)
            for l in range(NL):
                if l + 1 < NL:
                    diffs(l + 1)
                products(l)
                if l >= 2:
                    if l >= 3:
                        dve.wait_ge(banks.emptied["dve"], 4 + 4 * (l - 2))
                    take(l - 1)
            dve.wait_ge(banks.emptied["dve"], 4 + 4 * (NL - 2))
            take(NL - 1)
            dve.wait_ge(banks.emptied["dve"], 4 + 4 * (NL - 1))
            dve.sem_inc(a_ready, 1)
            dve.wait_ge(silu_ready, 1)
            dve.wait_ge(rs_ready, 1)
            o = core.hT[:, 0:HH, :].rearrange("p a b -> p (a b)")
            v.link(dve, nc.vector.scalar_tensor_tensor(out=o, in0=o, scalar=core.cols[:, C_HGNORM:C_HGNORM + 1],
                                                       in1=X[:, 1, :], op0=ALU.mult, op1=ALU.mult))
            v.link(dve, nc.vector.tensor_tensor(o, o, flat(HG, HH), ALU.mult))



def phase_gdn(nc, core):
    big, ps = core.big, core.ps
    flat = lambda a, n: big[:, a:a + n, :].rearrange("p a b -> p (a b)")
    blocks = lambda a: flat(a, HH).rearrange("p (n t) -> p n t", t=P)
    q_all, k_all = flat(GQ, HH), flat(GK, HH)
    inv_levels = list(reversed(LEVELS))[1:]
    NI = len(inv_levels)
    uses = [(("ssq", n), "act") for n in range(8)] + [("columns", "dve")]
    uses += [(("rows", h), "act") for h in range(HH)] + [(("v", n), "act") for n in range(4)]
    uses += [(("kt", n), "dve") for n in range(2)]
    uses += [(("qk", n), "dve") for n in range(4)] + [(("kk", n), "dve") for n in range(4)]
    uses += [(("nt", n), "dve") for n in range(4)]
    for l in range(NI):
        uses += [(("p", l, n), "act") for n in range(4)]
        for n in range(4):
            uses += [(("d", l, n), "dve")] if l < NI - 1 else []
            uses += [(("dt", l, n), "dve")]
    uses += [(("vn0", n), "act") for n in range(2)] + [(("s", n), "act") for n in range(2)]
    uses += [(("ks", n), "dve") for n in range(2)] + [(("vn1", n), "act") for n in range(2)]
    uses += [(("o", n), "act") for n in range(4)] + [(("ss", n), "act") for n in range(4)]
    with ExitStack() as ctx:
        banks = Banks(ctx, nc, uses)
        sem = lambda n: ctx.enter_context(nc.semaphore(n))
        first_tap, conv_done, conv_act, squares, norm_rs, qk_normed, sp_b, z_ready, g_ready, eg_ready, \
            g1_ready, g1_exp, nt_ready, tu_ready, r0_ready, eg_bc, qd_ready, sq_ready, \
            rs_ready, r1_ready, qkm_ready = (sem(n) for n in (
                "first_tap", "conv_done", "conv_act", "squares", "norm_rs", "qk_normed", "sp_b", "z_ready",
                "g_ready", "eg_ready", "g1_ready", "g1_exp", "nt_ready", "tu_ready", "r0_ready",
                "eg_bc", "qd_ready", "sq_ready", "rs_ready", "r1_ready", "qkm_ready"))
        W = ctx.enter_context(nc.sbuf_tensor("gdn_work", [P, 5, HH * SEQ], F32))
        G1, QK, NT_, GB, BB = (W[:, n, :] for n in range(5))
        rows = ctx.enter_context(nc.sbuf_tensor("gdn_rows", [HH, 6, SEQ], F32))
        pc = ctx.enter_context(nc.sbuf_tensor("gdn_token_cols", [P, 8, HH], F32))
        C0, C1, C2, C3 = 0, 8, 16, 24
        T, U, P1 = blocks(C0), blocks(C1), blocks(C2)
        KTOK, QD = blocks(C3)[:, 0:HH, :], blocks(C3)[:, HH:2 * HH, :]
        R, VN = blocks(C0), blocks(C2)
        S = G1.rearrange("p (n t) -> p n t", t=P)[:, 0:HH, :]
        block = ctx.enter_context(nc.Block())
        quad = lambda a, n: a[:, 4 * n:4 * n + 4, :]
        quad_ps = lambda name: ps[:, banks.bank(name), :].rearrange("p (n t) -> p n t", t=P)
        as_blocks = lambda a: a.rearrange("p (n t) -> p n t", t=P)

        @block.scalar
        def _(act):
            a = core.act
            gates = core.gates
            a.link(act, nc.scalar.activation(rows[:, 1, :], gates[:, SEQ:2 * SEQ], ACT.Sigmoid))
            for part in range(3):
                for j in range(HH):
                    w = C_CONV + 3 * 3 * HH + part * HH + j
                    ins = nc.scalar.activation(big[:, C0 + part * HH + j, :], big[:, GQ + part * HH + j, :], ACT.Copy,
                                               scale=core.cols[:, w:w + 1])
                ins.then_inc(first_tap, 1)
            for part in range(3):
                act.wait_ge(conv_done, part + 1)
                nc.scalar.activation(flat(GQ + part * HH, HH), flat(C0 + part * HH, HH), ACT.Silu
                                     ).then_inc(conv_act, 1)
            act.wait_ge(conv_act, 2)
            for part, sq in ((0, G1), (1, QK)):
                nc.scalar.activation(sq, flat(GQ + part * HH, HH), ACT.Square).then_inc(squares, 1)
            act.wait_ge(z_ready, 1)
            a.link(act, nc.scalar.activation(rows[:, 4, :], rows[:, 4, :], ACT.Exp))
            nc.scalar.activation(rows[:, 4, :], rows[:, 4, :], ACT.Ln, bias=core.one[0:HH, :]).then_inc(sp_b, 1)
            for n in range(8):
                banks.wait_filled(act, ("ssq", n))
                dst = (NT_ if n < 4 else GB)[:, 512 * (n % 4):512 * (n % 4) + 512]
                nc.scalar.activation(dst, ps[:, banks.bank(("ssq", n)), :], ACT.Ln, bias=core.eps[:]
                                     ).then_inc(banks.emptied["act"], 1)
            act.wait_ge(banks.emptied["act"], 8)
            nc.scalar.activation(NT_, NT_, ACT.Exp, scale=-0.5).then_inc(norm_rs, 1)
            nc.scalar.activation(GB, GB, ACT.Exp, scale=-0.5).then_inc(norm_rs, 1)
            act.wait_ge(g_ready, 1)
            nc.scalar.activation(rows[:, 2, :], rows[:, 0, :], ACT.Exp).then_inc(eg_ready, 1)
            nc.scalar.activation(rows[:, 3, 0:P], rows[:, 0, 0:P], ACT.Exp, scale=-1.0, bias=rows[:, 0, P - 1:P]
                                 ).then_inc(eg_ready, 1)
            act.wait_ge(qk_normed, 1)
            for h in range(HH):
                banks.wait_filled(act, ("rows", h))
                nc.scalar.activation(W[:, 3:5, h * SEQ:(h + 1) * SEQ],
                                     ps[:, banks.bank(("rows", h)), :].rearrange("p (a t) -> p a t", a=2), ACT.Copy
                                     ).then_inc(banks.emptied["act"], 1)
            for n in range(4):
                banks.wait_filled(act, ("v", n))
                nc.scalar.activation(big[:, GV + 2 * n:GV + 2 * n + 2, :], ps[:, banks.bank(("v", n)), :], ACT.Copy
                                     ).then_inc(banks.emptied["act"], 1)
            act.wait_ge(g1_ready, 1)
            nc.scalar.activation(G1, G1, ACT.Exp).then_inc(g1_exp, 1)
            nc.scalar.activation(GB, GB, ACT.Exp).then_inc(eg_bc, 1)
            for l in range(NI):
                for n in range(4):
                    banks.wait_filled(act, ("p", l, n))
                    nc.scalar.activation(quad(P1, n), quad_ps(("p", l, n)), ACT.Copy
                                         ).then_inc(banks.emptied["act"], 1)
            for name, dst in (("vn0", VN[:, 0:HH, :]), ("s", S), ("vn1", VN[:, HH:2 * HH, :])):
                for n in range(2):
                    banks.wait_filled(act, (name, n))
                    nc.scalar.activation(dst[:, 4 * n:4 * n + 4, :], quad_ps((name, n)), ACT.Copy
                                         ).then_inc(banks.emptied["act"], 1)
            for n in range(4):
                banks.wait_filled(act, ("o", n))
                pso = ps[:, banks.bank(("o", n)), :]
                nc.scalar.activation(BB[:, 512 * n:512 * n + 512], pso, ACT.Square).then_inc(sq_ready, 1)
                nc.scalar.activation(core.hT[:, HH + 2 * n:HH + 2 * n + 2, :], pso, ACT.Copy
                                     ).then_inc(banks.emptied["act"], 1)
            for n in range(4):
                banks.wait_filled(act, ("ss", n))
                a.link(act, nc.scalar.activation(GB[:, 512 * n:512 * n + 512], ps[:, banks.bank(("ss", n)), :],
                                                 ACT.Ln, bias=core.eps[:], scale=1.0 / P))
            nc.scalar.activation(GB, GB, ACT.Exp, scale=-0.5).then_inc(rs_ready, 1)

        n_act = {name: banks.order[banks.at[name]][1] for name, e in uses if e == "act"}
        n_dve = {name: banks.order[banks.at[name]][1] for name, e in uses if e == "dve"}

        @block.tensor
        def _(pe):
            def fill(name, parts):
                banks.wait_empty(pe, name)
                for out, lhsT, rhs, start, stop in parts:
                    ins = nc.tensor.matmul(out, lhsT, rhs, start=start, stop=stop)
                ins.then_inc(banks.filled, 1)

            def fill_turned(name, sources):
                banks.wait_empty(pe, name)
                for j, s in enumerate(sources):
                    ins = nc.tensor.transpose(quad_ps(name)[:, j, :], s, core.ident[:])
                ins.then_inc(banks.filled, 1)

            for n in range(8):
                pe.wait_ge(squares, n // 4 + 1)
                sq = (G1 if n < 4 else QK)[:, 512 * (n % 4):512 * (n % 4) + 512]
                fill(("ssq", n), [(ps[:, banks.bank(("ssq", n)), :], core.ones[:], sq, True, True)])
            pe.wait_ge(eg_ready, 2)
            banks.wait_empty(pe, "columns")
            for j, (r, c) in enumerate(((0, 0), (0, 1), (1, 0), (1, 1), (2, 1), (3, 0))):
                ins = nc.tensor.transpose(ps[:, banks.bank("columns"), j * HH:(j + 1) * HH],
                                          rows[:, r, c * P:(c + 1) * P], core.ident[0:HH, 0:HH])
            ins.then_inc(banks.filled, 1)
            for h in range(HH):
                fill(("rows", h), [(ps[:, banks.bank(("rows", h)), :], core.pick[:, h, :],
                                    rows[:, 0:2, :].rearrange("p a t -> p (a t)"), True, True)])
            pe.wait_ge(conv_act, 3)
            for n in range(4):
                fill_turned(("v", n), [big[:, GV + 2 * n + j // 2, (j % 2) * P:(j % 2 + 1) * P] for j in range(4)])
            pe.wait_ge(qk_normed, 1)
            for n in range(2):
                fill_turned(("kt", n), [big[:, GK + 4 * n + j, 0:P] for j in range(4)])
            for name, rhs in (("qk", q_all), ("kk", k_all)):
                for n in range(4):
                    fill((name, n), [(quad_ps((name, n))[:, j, :], k_all[:, 512 * n + j * P:512 * n + (j + 1) * P],
                                      rhs[:, 512 * n + j * P:512 * n + (j + 1) * P], True, True) for j in range(4)])
            pe.wait_ge(nt_ready, 1)
            NTb = as_blocks(NT_)
            for n in range(4):
                fill_turned(("nt", n), [NTb[:, 4 * n + j, :] for j in range(4)])
            for l in range(NI):
                for n in range(4):
                    pe.wait_ge(tu_ready, 4 * l + n + 1)
                    fill(("p", l, n), [(quad_ps(("p", l, n))[:, j, :], NTb[:, 4 * n + j, :], T[:, 4 * n + j, :],
                                        True, True) for j in range(4)])
                for n in range(4):
                    pe.wait_ge(banks.emptied["act"], n_act[("p", l, n)])
                    if l < NI - 1:
                        fill(("d", l, n), [(quad_ps(("d", l, n))[:, j, :], U[:, 4 * n + j, :], P1[:, 4 * n + j, :],
                                            True, True) for j in range(4)])
                    fill(("dt", l, n), [(quad_ps(("dt", l, n))[:, j, :], P1[:, 4 * n + j, :], U[:, 4 * n + j, :],
                                         True, True) for j in range(4)])
            pe.wait_ge(tu_ready, 4 * NI + 4)
            pe.wait_ge(r0_ready, 1)
            for n in range(2):
                fill(("vn0", n), [(quad_ps(("vn0", n))[:, j, :], U[:, 2 * (4 * n + j), :], R[:, 4 * n + j, :],
                                   True, True) for j in range(4)])
            for n in range(2):
                pe.wait_ge(banks.emptied["act"], n_act[("vn0", n)])
                fill(("s", n), [(quad_ps(("s", n))[:, j, :], KTOK[:, 4 * n + j, :], VN[:, 4 * n + j, :],
                                 True, True) for j in range(4)])
            for n in range(2):
                pe.wait_ge(banks.emptied["act"], n_act[("s", n)])
                fill(("ks", n), [(quad_ps(("ks", n))[:, j, :], big[:, GK + 4 * n + j, P:SEQ], S[:, 4 * n + j, :],
                                  True, True) for j in range(4)])
            for n in range(2):
                pe.wait_ge(r1_ready, n + 1)
                fill(("vn1", n), [(quad_ps(("vn1", n))[:, j, :], U[:, 2 * (4 * n + j) + 1, :],
                                   R[:, HH + 4 * n + j, :], True, True) for j in range(4)])
            pe.wait_ge(qd_ready, 1)
            pe.wait_ge(qkm_ready, 1)
            QKb = as_blocks(QK)
            for n in range(4):
                pe.wait_ge(banks.emptied["act"], n_act[("vn1", n // 2)])
                parts = []
                for j in range(2):
                    h = 2 * n + j
                    out = ps[:, banks.bank(("o", n)), j * SEQ:(j + 1) * SEQ]
                    parts += [(out[:, 0:P], VN[:, h, :], QKb[:, 2 * h, :], True, True),
                              (out[:, P:SEQ], S[:, h, :], QD[:, h, :], True, False),
                              (out[:, P:SEQ], VN[:, HH + h, :], QKb[:, 2 * h + 1, :], False, True)]
                fill(("o", n), parts)
            for n in range(4):
                pe.wait_ge(sq_ready, n + 1)
                fill(("ss", n), [(ps[:, banks.bank(("ss", n)), :], core.ones[:], BB[:, 512 * n:512 * n + 512],
                                  True, True)])

        @block.vector
        def _(dve):
            v = core.dve
            v.link(dve, nc.vector.tensor_scalar(rows[:, 5, :], core.gates[:, 0:SEQ], core.gdn_cols[:, 1:2], None,
                                                ALU.add))
            v.link(dve, nc.vector.tensor_scalar(rows[:, 4, :], rows[:, 5, :], -1.0, None, ALU.mult))
            nc.vector.tensor_tensor(rows[:, 4, :], rows[:, 4, :], rows[:, 5, :], ALU.min).then_inc(z_ready, 1)
            for part in range(3):
                dve.wait_ge(first_tap, part + 1)
                for tap in (2, 1, 0):
                    back = 3 - tap
                    for j in range(HH):
                        w = C_CONV + tap * 3 * HH + part * HH + j
                        dst = big[:, C0 + part * HH + j, back:SEQ]
                        ins = nc.vector.scalar_tensor_tensor(
                            out=dst, in0=big[:, GQ + part * HH + j, 0:SEQ - back], scalar=core.cols[:, w:w + 1],
                            in1=dst, op0=ALU.mult, op1=ALU.add)
                    if tap:
                        v.link(dve, ins)
                ins.then_inc(conv_done, 1)
            dve.wait_ge(sp_b, 1)
            v.link(dve, nc.vector.scalar_tensor_tensor(out=rows[:, 4, :], in0=rows[:, 5, :], scalar=0.0,
                                                       in1=rows[:, 4, :], op0=ALU.max, op1=ALU.add))
            v.link(dve, nc.vector.tensor_scalar(rows[:, 4, :], rows[:, 4, :], core.gdn_cols[:, 3:4], None, ALU.mult))
            nc.vector.tensor_tensor_scan(rows[:, 0, :], core.keep[0:HH, :], rows[:, 4, :], 0.0, ALU.mult, ALU.add
                                         ).then_inc(g_ready, 1)
            dve.wait_ge(norm_rs, 2)
            nc.vector.scalar_tensor_tensor(out=q_all, in0=q_all, scalar=float(P) ** -0.5, in1=NT_, op0=ALU.mult,
                                           op1=ALU.mult)
            nc.vector.tensor_tensor(k_all, k_all, GB, ALU.mult).then_inc(qk_normed, 1)
            banks.wait_filled(dve, "columns")
            nc.vector.tensor_copy(pc[:, 0:6, :], ps[:, banks.bank("columns"), 0:6 * HH].rearrange(
                "p (a h) -> p a h", a=6)).then_inc(banks.emptied["dve"], 1)
            dve.wait_ge(banks.emptied["dve"], 1)
            nc.vector.scalar_tensor_tensor(out=pc[:, 6, :], in0=pc[:, 3, :], scalar=-1.0, in1=pc[:, 4, :],
                                           op0=ALU.mult, op1=ALU.mult)
            dve.wait_ge(banks.emptied["act"], n_act[("rows", HH - 1)])
            for h in range(HH):
                for c in range(2):
                    at = h * SEQ + c * P
                    ins = nc.vector.tensor_scalar(G1[:, at:at + P], GB[:, at:at + P], pc[:, c, h:h + 1], 0.0,
                                                  ALU.subtract, ALU.min)
            ins.then_inc(g1_ready, 1)
            for n in range(2):
                banks.wait_filled(dve, ("kt", n))
                for j in range(4):
                    ins = nc.vector.tensor_scalar(KTOK[:, 4 * n + j, :], quad_ps(("kt", n))[:, j, :],
                                                  pc[:, 5, 4 * n + j:4 * n + j + 1], None, ALU.mult)
                ins.then_inc(banks.emptied["dve"], 1)
            dve.wait_ge(g1_exp, 1)
            for name, dst in (("qk", QK), ("kk", NT_)):
                for n in range(4):
                    banks.wait_filled(dve, (name, n))
                    nc.vector.tensor_tensor(dst[:, 512 * n:512 * n + 512], ps[:, banks.bank((name, n)), :],
                                            G1[:, 512 * n:512 * n + 512], ALU.mult).then_inc(banks.emptied["dve"], 1)
            dve.wait_ge(banks.emptied["dve"], n_dve[("kk", 3)])
            v.link(dve, nc.vector.tensor_tensor(NT_, NT_, BB, ALU.mult))
            nc.vector.scalar_tensor_tensor(out=as_blocks(NT_), in0=as_blocks(NT_), scalar=-1.0,
                                           in1=bcast(core.strict[:], 2 * HH), op0=ALU.mult, op1=ALU.mult
                                           ).then_inc(nt_ready, 1)
            nc.vector.tensor_copy(T, bcast(core.ident[:], 2 * HH))
            v.mark(nc.vector.tensor_copy(U, bcast(core.ident[:], 2 * HH)))
            nc.vector.tensor_tensor(as_blocks(QK), as_blocks(QK), bcast(core.incl[:], 2 * HH), ALU.mult
                                    ).then_inc(qkm_ready, 1)
            dve.wait_ge(nt_ready, 1)
            dve.wait_ge(v.sem, v.n)
            for n in range(4):
                banks.wait_filled(dve, ("nt", n))
                nc.vector.copy_predicated(quad(T, n), bcast(core.low_mask[:, len(LEVELS) - 1, :].bitcast(I32), 4),
                                          quad_ps(("nt", n))).then_inc(banks.emptied["dve"], 1)
                nc.vector.copy_predicated(quad(U, n), bcast(core.up_mask[:, len(LEVELS) - 1, :].bitcast(I32), 4),
                                          quad(as_blocks(NT_), n)).then_inc(tu_ready, 1)
            dve.wait_ge(eg_bc, 1)
            nc.vector.tensor_tensor(QD, big[:, GQ:GQ + HH, P:SEQ],
                                    GB.rearrange("p (h t) -> p h t", t=SEQ)[:, :, P:SEQ], ALU.mult
                                    ).then_inc(qd_ready, 1)
            for l, L in enumerate(inv_levels):
                m = LEVELS.index(L)
                for n in range(4):
                    dve.wait_ge(tu_ready, 4 * l + n + 1)
                    if l < NI - 1:
                        banks.wait_filled(dve, ("d", l, n))
                        nc.vector.copy_predicated(quad(T, n), bcast(core.low_mask[:, m, :].bitcast(I32), 4),
                                                  quad_ps(("d", l, n))).then_inc(banks.emptied["dve"], 1)
                    banks.wait_filled(dve, ("dt", l, n))
                    nc.vector.copy_predicated(quad(U, n), bcast(core.up_mask[:, m, :].bitcast(I32), 4),
                                              quad_ps(("dt", l, n))).then_inc(banks.emptied["dve"], 1)
                    dve.wait_ge(banks.emptied["dve"], n_dve[("dt", l, n)])
                    dve.sem_inc(tu_ready, 1)
            dve.wait_ge(banks.emptied["act"], n_act[("v", 3)])
            for c in range(2):
                for h in range(HH):
                    ins = nc.vector.tensor_scalar(R[:, c * HH + h, :], big[:, GV + h, c * P:(c + 1) * P],
                                                  pc[:, 2 + c, h:h + 1], None, ALU.mult)
            ins.then_inc(r0_ready, 1)
            dve.wait_ge(r0_ready, 1)
            for n in range(2):
                banks.wait_filled(dve, ("ks", n))
                for j in range(4):
                    h = 4 * n + j
                    ins = nc.vector.scalar_tensor_tensor(out=R[:, HH + h, :], in0=quad_ps(("ks", n))[:, j, :],
                                                         scalar=pc[:, 6, h:h + 1], in1=R[:, HH + h, :],
                                                         op0=ALU.mult, op1=ALU.add)
                ins.then_inc(banks.emptied["dve"], 1)
                dve.wait_ge(banks.emptied["dve"], n_dve[("ks", n)])
                dve.sem_inc(r1_ready, 1)
            dve.wait_ge(rs_ready, 1)
            o = core.hT[:, HH:2 * HH, :].rearrange("p a b -> p (a b)")
            v.link(dve, nc.vector.scalar_tensor_tensor(out=o, in0=o, scalar=core.cols[:, C_GDNNORM:C_GDNNORM + 1],
                                                       in1=GB, op0=ALU.mult, op1=ALU.mult))
            v.link(dve, nc.vector.tensor_tensor(o, o, flat(GG, HH), ALU.mult))



def phase_swiglu(nc, core):
    st = core.streams["gate_up"]
    tr0, f0 = core.tiles_ready_n, list(core.claimed)
    with ExitStack() as ctx:
        gate = ctx.enter_context(nc.sbuf_tensor("gate", [P, NT, SEQ], F32))
        block = ctx.enter_context(nc.Block())

        @block.sync
        def _(sp):
            load_rest(sp, core, st)
            prefetch(sp, core, core.streams["down"])

        @block.tensor
        def _(pe):
            product_loop(nc, core, pe, st, f0)

        @block.scalar
        def _(act):
            with act.Fori(0, st.turns) as i:
                for nt in range(NT):
                    wait_tile(core, act, st, i, 0, nt, tr0)
                    act.wait_ge(core.free[1], i * NT + (f0[1] + nt + 1))
                    nc.scalar.activation(gate[:, nt, :], core.ps[:, nt, 0:SEQ], ACT.Silu).then_inc(core.free[0], 1)

        @block.vector
        def _(dve):
            with dve.Fori(0, st.turns) as i:
                for nt in range(NT):
                    dve.wait_ge(core.free[0], i * NT + (f0[0] + NT + nt + 1))
                    wait_tile(core, dve, st, i, 1, nt, tr0)
                    nc.vector.tensor_tensor(core.big[:, bass.ds(i * NT + nt, 1), :],
                                            core.ps[:, NT + nt, 0:SEQ].unsqueeze(1), gate[:, nt, :].unsqueeze(1),
                                            ALU.mult).then_inc(core.free[1], 1)
    advance(core, st)


def phase_down(nc, core, gate):
    st = core.streams["down"]
    with ExitStack() as ctx:
        chunk_done = ctx.enter_context(nc.semaphore("chunk_done"))
        taken = ctx.enter_context(nc.semaphore("taken"))
        block = ctx.enter_context(nc.Block())
        per_chunk = st.unit

        @block.sync
        def _(sp):
            load_rest(sp, core, st)

        @block.tensor
        def _(pe):
            for c in range(st.turns):
                for kg in range(per_chunk):
                    g = st.first + c * per_chunk + kg
                    pe.wait_ge(core.landed[g % RING], 16 * (g // RING + 1))
                    for nt in range(NT):
                        if kg == 0 and c >= 2:
                            pe.wait_ge(taken, NT * (c - 2) + nt + 1)
                        for k in range(KG):
                            kt = KG * kg + k
                            ins = nc.tensor.matmul(core.ps[:, NT * (c % 2) + nt, 0:SEQ],
                                                   core.ring[:, g % RING, k, nt * P:(nt + 1) * P],
                                                   core.big[:, kt, :], start=(kt == 0),
                                                   stop=(kt == KG * per_chunk - 1))
                        if kg == per_chunk - 1 and nt < NT - 1:
                            ins.then_inc(chunk_done, 1)
                    ins.then_inc(core.used, 1)

        @block.vector
        def _(dve):
            for c in range(st.turns):
                for nt in range(NT):
                    if nt < NT - 1:
                        dve.wait_ge(chunk_done, 3 * c + nt + 1)
                    else:
                        dve.wait_ge(core.used, st.first + per_chunk * (c + 1))
                    k = NT * c + nt
                    nc.vector.scalar_tensor_tensor(out=core.xT[:, k, :], in0=core.ps[:, NT * (c % 2) + nt, 0:SEQ],
                                                   scalar=core.mod[:, 1, gate + k:gate + k + 1],
                                                   in1=core.xT[:, k, :], op0=ALU.mult, op1=ALU.add
                                                   ).then_inc(taken, 1)


def product_loop(nc, core, pe, st, f0):
    with pe.Fori(0, st.turns) as i:
        for q in range(TURN):
            c = q // 4
            pe.wait_ge(core.landed[q % RING],
                       i * (16 * TURN // RING) + 16 * ((st.first + q) // RING + 1))
            for nt in range(NT):
                if q % 4 == 0:
                    pe.wait_ge(core.free[c], i * NT + (f0[c] + nt + 1))
                for k in range(KG):
                    kt = KG * (q % 4) + k
                    ins = nc.tensor.matmul(core.ps[:, NT * c + nt, 0:SEQ],
                                           core.ring[:, q % RING, k, nt * P:(nt + 1) * P], core.hT[:, kt, :],
                                           start=(kt == 0), stop=(kt == KT - 1))
                if q % 4 == 3 and nt < NT - 1:
                    ins.then_inc(core.tile_ready, 1)
            ins.then_inc(core.used, 1)


def wait_tile(core, eng, st, i, c, nt, tr0):
    if nt < NT - 1:
        eng.wait_ge(core.tile_ready, i * 6 + (tr0 + 3 * c + nt + 1))
    else:
        eng.wait_ge(core.used, i * TURN + (st.first + 4 * (c + 1)))


def advance(core, st):
    core.tiles_ready_n += 6 * st.turns
    for c in range(2):
        core.claimed[c] += NT * st.turns


def phase_write_out(nc, core, out):
    y = core.big[:, 0:16, :].rearrange("p a b -> p (a b)").rearrange("p (t f) -> p t f", t=TT)
    with ExitStack() as ctx:
        turned, copied, stored = (ctx.enter_context(nc.semaphore(n)) for n in ("turned", "copied", "stored"))
        block = ctx.enter_context(nc.Block())

        @block.tensor
        def _(pe):
            for n in range(8):
                for j in range(4):
                    ins = nc.tensor.transpose(core.ps[:, n, j * P:(j + 1) * P],
                                              core.hT[:, 4 * (n % 4) + j, (n // 4) * P:(n // 4 + 1) * P],
                                              core.ident[:])
                ins.then_inc(turned, 1)

        @block.scalar
        def _(act):
            for n in range(8):
                act.wait_ge(turned, n + 1)
                nc.scalar.activation(y[:, n // 4, 512 * (n % 4):512 * (n % 4) + 512], core.ps[:, n, :], ACT.Copy
                                     ).then_inc(copied, 1)

        @block.sync
        def _(sp):
            rows = out[0].rearrange("(t p) f -> p t f", p=P)
            for n in range(4):
                sp.wait_ge(copied, 2 * n + 2)
                t, f = n // 2, 1024 * (n % 2)
                sp.dma_start(rows[:, t, f:f + 1024], y[:, t, f:f + 1024]).then_inc(stored, 16)
            sp.wait_ge(stored, 64)



HD = 64
FOX, NSA, DIL, DIFF, GROUPS = 7, 8, 9, 4, 2
N_CMP = SEQ // 16 - 1
FAR = 1.0e32
LAM_INIT = 0.8 - 0.6
SCALE = HD ** -0.5

T_FOXQ, T_FOXK, T_NSAQ, T_CMPK, T_CMPV, T_SLCK, T_WINK, T_DILQ, T_DILK, T_DIFFQ, T_DIFFK = (
    0, 4, 8, 12, 13, 14, 15, 16, 21, 26, 30)
T_TOKENS, T_FOXROW = 34, 49
V_FOX, V_SLC, V_WIN, V_DIL, V_DIFF, V_FOXF, V_GATE, V_COLS = 0, 448, 576, 704, 1280, 1792, 1799, 1920

def _features(tile, widths, scale=1.0, at=0):
    return [("f", at + P * n, w, tile + n, scale) for n, w in enumerate(widths)]


IN_2 = [
    (0, 448, _features(T_FOXQ, [128, 128, 128, 64], SCALE)),
    (448, 448, _features(T_FOXK, [128, 128, 128, 64])),
    (896, 455, [("t", 0, 455, [(0, 448, V_FOX), (448, 7, V_FOXF)])]),
    (1351, 512, [("pair", P * n, P, n, SCALE) for n in range(4)]),
    (1863, 384, _features(T_CMPK, [128, 128, 128])),
    (2247, 408, [("t", 0, 408, [(0, 128, V_SLC), (256, 128, V_WIN), (384, 24, V_GATE)]),
                 ("f", 128, 128, T_WINK, 1.0)]),
    (2655, 512, _features(T_DILQ, [128] * 4, SCALE)),
    (3167, 448, [("f", 0, 64, T_DILQ + 4, SCALE)] + _features(T_DILK, [128] * 3, at=64)),
    (3615, 448, _features(T_DILK + 3, [128, 64]) + [("t", 192, 256, [(0, 256, V_DIL)])]),
    (4063, 320, [("t", 0, 320, [(0, 320, V_DIL + 256)])]),
    (4383, 512, _features(T_DIFFQ, [128] * 4, SCALE)),
    (4895, 512, _features(T_DIFFK, [128] * 4)),
    (5407, 256, [("t", 0, 256, [(0, 256, V_DIFF)])]),
    (5663, 256, [("t", 0, 256, [(0, 256, V_DIFF + 256)])]),
]


def in_2_source(w):
    v = w.rearrange("(g k p) n -> p g k n", p=P, k=KG)

    def source(i, q):
        at, width, _ = IN_2[2 * i + q // 4]
        return v[:, q % 4, :, at:at + width]
    return source


def tokens(core):
    return core.big[:, T_TOKENS:T_TOKENS + 15, :].rearrange("p a b -> p (a b)").rearrange(
        "p (t c) -> p t c", t=TT)


def phase_in_2(nc, core, mix, t):
    st = core.streams["in_2"]
    f0 = list(core.claimed)
    tok = tokens(core)
    with ExitStack() as ctx:
        iota_done, dist_f, causal_done, odd_done = (ctx.enter_context(nc.semaphore(n)) for n in
                                                    ("iota_done", "dist_f", "causal_done", "odd_done"))
        disti = mix.PT[:, 0, 0:2, 0:SEQ].bitcast(I32)
        odd = mix.PT[:, 0, 2:4, 0:SEQ].bitcast(I32)
        far = mix.PT[:, 1, 0:2, 0:SEQ]
        cmpi = mix.PT[:, 1, 2, 0:TT * N_CMP].rearrange("p (t c) -> p t c", t=TT).bitcast(I32)
        block = ctx.enter_context(nc.Block())

        @block.sync
        def _(sp):
            for g in range(RING, st.groups):
                refill(sp, core, st, g // TURN, g % TURN)
            prefetch(sp, core, core.streams["out_2"])

        @block.tensor
        def _(pe):
            for c, (_, _, pieces) in enumerate(IN_2):
                half = c % 2
                pe.wait_ge(core.free[half], f0[half] + NT * (c // 2 + 1))
                for kg in range(4):
                    g = st.first + 4 * c + kg
                    slot = g % RING
                    pe.wait_ge(core.landed[slot], 16 * (g // RING + 1))
                    bank = NT * half
                    for kind, at, width, *_ in pieces:
                        for part in range(TT if kind == "t" else 1):
                            for k in range(KG):
                                kt = KG * kg + k
                                w = core.ring[:, slot, k, at:at + width]
                                if kind == "t":
                                    out = core.ps[:, bank, 0:width]
                                    lhsT, rhs = core.hT[:, kt, part * P:(part + 1) * P], w
                                else:
                                    out = core.ps[0:width, bank, 0:SEQ]
                                    lhsT, rhs = w, core.hT[:, kt, :]
                                ins = nc.tensor.matmul(out, lhsT, rhs, start=(kt == 0), stop=(kt == KT - 1))
                            bank += 1
                    ins.then_inc(core.used, 1)

        @block.scalar
        def _(act):
            for g in range(GROUPS):
                rows = slice(g * HD, (g + 1) * HD)
                for a in range(2):
                    src = t["nsa_cmp_w1_2"][0, a].rearrange("(l d) o -> d l o", d=HD)
                    act.dma_start(mix.W1[rows, a], src).then_inc(mix.w_in, 16)
            for a in range(2):
                for g in range(GROUPS):
                    act.dma_start(mix.W2[0:HD, a, g * HD:(g + 1) * HD], t["nsa_cmp_w2_2"][0, a]
                                  ).then_inc(mix.w_in, 16)
            act.dma_start(mix.lam_rows[:], t["diff_lambda_2"].rearrange("l a d -> l (a d)")).then_inc(mix.w_in, 16)
            with nc.allow_non_contiguous_dma("seven numbers, one a partition"):
                act.dma_start(mix.fox_bias[:], t["fox_f_bias_2"].rearrange("l h -> h l")).then_inc(mix.w_in, 16)
            for c, (_, _, pieces) in enumerate(IN_2):
                half = c % 2
                bank = NT * half
                act.wait_ge(core.used, st.first + 4 * c + 4)
                for kind, at, width, *rest in pieces:
                    if kind == "t":
                        for part in range(TT):
                            for col, w, dst in rest[0]:
                                ins = nc.scalar.activation(tok[:, part, dst:dst + w],
                                                           core.ps[:, bank, col:col + w], ACT.Copy)
                            bank += 1
                    elif kind == "pair":
                        for h in range(2 * rest[0], 2 * rest[0] + 2):
                            r, g = h % 2 * HD, h // (NSA // GROUPS) * HD
                            ins = nc.scalar.activation(core.big[g:g + HD, T_NSAQ + h % 4, :],
                                                       core.ps[r:r + HD, bank, 0:SEQ], ACT.Copy, scale=rest[1])
                        bank += 1
                    else:
                        tile, scale = rest
                        ins = nc.scalar.activation(core.big[0:width, tile, :], core.ps[0:width, bank, 0:SEQ],
                                                   ACT.Copy, scale=scale)
                        bank += 1
                ins.then_inc(core.free[half], NT)

        @block.gpsimd
        def _(pool):
            nc.gpsimd.iota(disti, [[P, TT], [-1, SEQ]], base=0, channel_multiplier=1)
            nc.gpsimd.iota(cmpi, [[P, TT], [-16, N_CMP]], base=-31, channel_multiplier=1).then_inc(iota_done, 1)
            core.pool.link(pool, nc.gpsimd.memset(far, FAR))
            core.pool.link(pool, nc.gpsimd.memset(mix.VC[:], 0.0))
            pool.wait_ge(dist_f, 1)
            for n in range(4):
                nc.gpsimd.affine_select(out=mix.dist[:, n], in_=mix.dist[:, n], compare_op=ALU.is_ge, fill=FAR,
                                        base=0, pattern=[[P, TT], [-1, SEQ]], channel_multiplier=1)
            nc.gpsimd.affine_select(out=mix.valid_cmp[:], in_=mix.dist_cmp[:], compare_op=ALU.is_ge, fill=FAR,
                                    base=-31, pattern=[[P, TT], [-16, N_CMP]], channel_multiplier=1
                                    ).then_inc(causal_done, 1)
            pool.wait_ge(causal_done, 1)
            nc.gpsimd.affine_select(out=mix.dist[:, 1], in_=mix.dist[:, 1], compare_op=ALU.is_ge, fill=FAR,
                                    base=128, pattern=[[-P, TT], [1, SEQ]], channel_multiplier=-1
                                    ).then_inc(causal_done, 1)

        @block.vector
        def _(dve):
            dve.wait_ge(iota_done, 1)
            for n in range(4):
                nc.vector.tensor_copy(mix.dist[:, n], disti)
            nc.vector.tensor_copy(mix.dist_cmp[:], cmpi).then_inc(dist_f, 1)
            dve.wait_ge(causal_done, 2)
            for n, mod in ((2, 4), (3, 16)):
                core.dve.link(dve, nc.vector.tensor_scalar(odd, disti, mod - 1, None, ALU.bitwise_and))
                core.dve.link(dve, nc.vector.copy_predicated(mix.dist[:, n], odd, far))
            nc.vector.tensor_scalar(mix.fox_mask, mix.dist[:, 0], 0.5 * FAR, -FAR, ALU.is_ge, ALU.mult)
            core.dve.link(dve, nc.vector.tensor_copy(mix.dist_cmp[:], mix.valid_cmp[:]))
            core.dve.link(dve, nc.vector.tensor_scalar(mix.valid_cmp[:], mix.dist_cmp[:], 0.5 * FAR, None, ALU.is_lt))
    for half in range(2):
        core.claimed[half] += NT * st.turns


def alibi(heads):
    return [float(np.float32(2.0 ** (-8.0 * (h + 1) / heads))) for h in range(heads)]


def attention_packs():
    packs = []
    for heads in (range(0, 4), range(4, FOX)):
        packs.append(("fox", [(T_FOXQ + h // 2, T_FOXK + h // 2, h % 2, ("fox", h)) for h in heads],
                      [(HD * h, HD, [(m, V_FOX + HD * h)]) for m, h in enumerate(heads)], None))
    slopes = alibi(NSA)
    for i in range(0, NSA, 2):
        maps, outs = [], []
        for m, h in enumerate((i, i + 1)):
            g = h // (NSA // GROUPS)
            for k_tile in (T_SLCK, T_WINK):
                maps.append((T_NSAQ + h % 4, k_tile, g, (0, slopes[h])))
            outs.append((HD * (FOX + h), HD, [(2 * m, V_SLC + HD * g), (2 * m + 1, V_WIN + HD * g), (("cmp", h), g)]))
        packs.append(("nsa", maps, outs, i))
    slopes = alibi(DIL)
    for j in range(3):
        maps, outs = [], []
        for m, h in enumerate((j, 3 + j, 6 + j)):
            maps.append((T_DILQ + h // 2, T_DILK + h // 2, h % 2, (1 + m, slopes[h])))
            outs.append((HD * (FOX + NSA + h), HD, [(m, V_DIL + HD * h)]))
        packs.append(("dil", maps, outs, None))
    slopes = alibi(DIFF)
    for i in range(0, DIFF, 2):
        maps, outs = [], []
        for m, h in enumerate((i, i + 1)):
            maps += [(T_DIFFQ + h, T_DIFFK + h, half, (0, slopes[h])) for half in range(2)]
            outs.append((HD * (FOX + NSA + DIL) + P * h, P, [(2 * m, V_DIFF + P * h), (2 * m + 1, V_DIFF + P * h)]))
        packs.append(("diff", maps, outs, None))
    return packs


def phase_compress(nc, core, mix):
    ps, tok = core.ps, tokens(core)
    steps = ("blocks_ready", "hidden_ready", "gelu_ready", "kv_ready", "kv_taken", "sc_ready", "sc_diff", "sc_exp",
             "p_ready", "pt_ready", "pt_free", "f_turned", "f_z", "f_exp", "f_cum", "f_cols", "f_rows", "rows_free",
             "lam_sums", "lam_exp", "lam_ready", "lam_wide", "gates_ready")
    with ExitStack() as ctx:
        s = {n: ctx.enter_context(nc.semaphore(n)) for n in steps}
        blk = ctx.enter_context(nc.sbuf_tensor("blocks", [P, 2, 32, N_CMP], F32))
        hid = ctx.enter_context(nc.sbuf_tensor("cmp_hidden", [HD, 4 * N_CMP], F32))
        kc = ctx.enter_context(nc.sbuf_tensor("cmp_keys", [P, N_CMP], F32))
        sc = ctx.enter_context(nc.sbuf_tensor("cmp_scores", [P, NSA * TT, N_CMP], F32))
        st = ctx.enter_context(nc.sbuf_tensor("cmp_stats", [P, 4, NSA * TT], F32))
        frow = ctx.enter_context(nc.sbuf_tensor("fox_rows", [FOX, 3, SEQ], F32))
        lam = ctx.enter_context(nc.sbuf_tensor("lambda_parts", [1, 2, HD + 2], F32))
        block = ctx.enter_context(nc.Block())

        @block.tensor
        def _(pe):
            for c in range(TT):
                ins = nc.tensor.transpose(ps[0:FOX, 5, c * P:(c + 1) * P], tok[:, c, V_FOXF:V_FOXF + FOX], core.ident[:])
            ins.then_inc(s["f_turned"], 1)
            pe.wait_ge(mix.w_in, 16 * 10)
            for a in range(2):
                pe.wait_ge(s["blocks_ready"], a + 1)
                for g in range(GROUPS):
                    rows, at = slice(g * HD, (g + 1) * HD), (2 * a + g) * N_CMP
                    for l in range(32):
                        ins = nc.tensor.matmul(ps[0:HD, g, at:at + N_CMP], mix.W1[rows, a, l, :], blk[rows, a, l, :],
                                               start=(l == 0), stop=(l == 31))
            ins.then_inc(s["hidden_ready"], 1)
            pe.wait_ge(s["gelu_ready"], 1)
            for g in range(GROUPS):
                nc.tensor.matmul(ps[:, 2, g * N_CMP:(g + 1) * N_CMP], mix.W2[0:HD, 0, :],
                                 hid[:, g * N_CMP:(g + 1) * N_CMP], start=True, stop=True)
            for g in range(GROUPS):
                ins = nc.tensor.matmul(ps[0:N_CMP, 3, g * HD:(g + 1) * HD], hid[:, (2 + g) * N_CMP:(3 + g) * N_CMP],
                                       mix.W2[0:HD, 1, 0:HD], start=True, stop=True)
            ins.then_inc(s["kv_ready"], 1)
            pe.wait_ge(s["f_cum"], 1)
            for c in range(TT):
                ins = nc.tensor.transpose(ps[:, 5, SEQ + c * FOX:SEQ + (c + 1) * FOX], frow[:, 2, c * P:(c + 1) * P],
                                          core.ident[0:FOX, 0:FOX])
            ins.then_inc(s["f_cols"], 1)
            for h in range(FOX):
                if h >= 2:
                    pe.wait_ge(s["rows_free"], h - 1)
                nc.tensor.matmul(ps[:, (6, 4)[h % 2], 0:SEQ],
                                 core.pick[0:FOX, h, :], frow[:, 2, :], start=True, stop=True).then_inc(s["f_rows"], 1)
            pe.wait_ge(s["lam_ready"], 1)
            nc.tensor.matmul(ps[:, 5, 500:501], core.ones[0:1, :], lam[0:1, 0, HD:HD + 1], start=True, stop=True
                             ).then_inc(s["lam_wide"], 1)
            pe.wait_ge(s["kv_taken"], 1)
            for h in range(NSA):
                g = h // 4
                rows = slice(g * HD, (g + 1) * HD)
                for c in range(TT):
                    at = (h * TT + c) * N_CMP
                    ins = nc.tensor.matmul(ps[:, g, at:at + N_CMP], core.big[rows, T_NSAQ + h % 4, c * P:(c + 1) * P],
                                           kc[rows, :], start=True, stop=True)
            ins.then_inc(s["sc_ready"], 1)
            pe.wait_ge(s["p_ready"], 1)
            for n in range(4):
                for j in range(4):
                    ins = nc.tensor.transpose(ps[0:N_CMP, n, j * P:(j + 1) * P], sc[:, 4 * n + j, :], core.ident[:])
                ins.then_inc(s["pt_ready"], 1)

        @block.scalar
        def _(act):
            a = core.act
            nc.scalar.activation(mix.gates[:], tok[:, :, V_GATE:V_GATE + 3 * NSA], ACT.Sigmoid
                                 ).then_inc(s["gates_ready"], 1)
            act.wait_ge(s["hidden_ready"], 1)
            hid_g = hid[:].rearrange("p (a g c) -> p a g c", a=2, g=2)
            for g in range(GROUPS):
                ins = nc.scalar.activation(hid_g[:, :, g, :], ps[0:HD, g, 0:4 * N_CMP].rearrange(
                    "p (a g c) -> p a g c", a=2, g=2)[:, :, g, :], ACT.Gelu_apprx_tanh)
            ins.then_inc(s["gelu_ready"], 1)
            act.wait_ge(s["kv_ready"], 1)
            for g in range(GROUPS):
                rows = slice(g * HD, (g + 1) * HD)
                nc.scalar.activation(kc[rows, :], ps[rows, 2, g * N_CMP:(g + 1) * N_CMP], ACT.Copy)
            nc.scalar.activation(mix.VC[0:N_CMP, HD:3 * HD], ps[0:N_CMP, 3, 0:2 * HD], ACT.Copy
                                 ).then_inc(s["kv_taken"], 1)
            act.wait_ge(s["f_z"], 1)
            a.link(act, nc.scalar.activation(frow[:, 1, :], frow[:, 1, :], ACT.Exp))
            nc.scalar.activation(frow[:, 1, :], frow[:, 1, :], ACT.Ln, bias=core.one[0:FOX, :]).then_inc(s["f_exp"], 1)
            act.wait_ge(s["lam_sums"], 1)
            nc.scalar.activation(lam[0:1, 1, 0:2], lam[0:1, 0, HD:HD + 2], ACT.Exp).then_inc(s["lam_exp"], 1)
            act.wait_ge(s["sc_diff"], 1)
            nc.scalar.activation(sc[:], sc[:], ACT.Exp).then_inc(s["sc_exp"], 1)
            for n in range(4):
                act.wait_ge(s["pt_ready"], n + 1)
                nc.scalar.activation(mix.PTC[0:N_CMP, 2 * n:2 * n + 2, :], ps[0:N_CMP, n, :], ACT.Copy)

        @block.vector
        def _(dve):
            v = core.dve
            for a, tile in enumerate((T_CMPK, T_CMPV)):
                src = core.big[:, tile, :].rearrange("p (c l) -> p l c", l=16)
                for r in range(2):
                    pos = core.cols[:, C_POS + 32 * a + 16 * r:C_POS + 32 * a + 16 * r + 16]
                    ins = nc.vector.tensor_tensor(blk[:, a, 16 * r:16 * r + 16, :], src[:, :, r:r + N_CMP],
                                                  bcast(pos, N_CMP, 2), ALU.add)
                ins.then_inc(s["blocks_ready"], 1)
            dve.wait_ge(s["f_turned"], 1)
            dve.wait_ge(mix.w_in, 16 * 10)
            v.link(dve, nc.vector.tensor_scalar(frow[:, 0, :], ps[0:FOX, 5, 0:SEQ], mix.fox_bias[:], None, ALU.add))
            v.link(dve, nc.vector.tensor_scalar(frow[:, 1, :], frow[:, 0, :], -1.0, None, ALU.mult))
            nc.vector.tensor_tensor(frow[:, 1, :], frow[:, 1, :], frow[:, 0, :], ALU.min).then_inc(s["f_z"], 1)
            lv = mix.lam_rows[:].rearrange("p (a d) -> p a d", a=4)
            for n in range(2):
                v.link(dve, nc.vector.tensor_tensor(lam[0:1, 1, 0:HD], lv[:, 2 * n, :], lv[:, 2 * n + 1, :], ALU.mult))
                v.link(dve, nc.vector.tensor_reduce(lam[0:1, 0, HD + n:HD + n + 1], lam[0:1, 1, 0:HD], AX.X, ALU.add))
            dve.sem_inc(s["lam_sums"], 1)
            dve.wait_ge(s["f_exp"], 1)
            v.link(dve, nc.vector.scalar_tensor_tensor(out=frow[:, 1, :], in0=frow[:, 0, :], scalar=0.0,
                                                       in1=frow[:, 1, :], op0=ALU.min, op1=ALU.subtract))
            v.link(dve, nc.vector.memset(frow[:, 0, :], 1.0))
            nc.vector.tensor_tensor_scan(frow[:, 2, :], frow[:, 0, :], frow[:, 1, :], 0.0, ALU.mult, ALU.add
                                         ).then_inc(s["f_cum"], 1)
            dve.wait_ge(s["lam_exp"], 1)
            v.link(dve, nc.vector.tensor_tensor(lam[0:1, 0, HD:HD + 1], lam[0:1, 1, 1:2], lam[0:1, 1, 0:1],
                                                ALU.subtract))
            nc.vector.tensor_scalar(lam[0:1, 0, HD:HD + 1], lam[0:1, 0, HD:HD + 1], -LAM_INIT, None, ALU.add
                                    ).then_inc(s["lam_ready"], 1)
            dve.wait_ge(s["f_cols"], 1)
            nc.vector.tensor_copy(mix.fox_cum[:], ps[:, 5, SEQ:SEQ + TT * FOX].rearrange("p (c h) -> p c h", c=TT))
            for h in range(FOX):
                dve.wait_ge(s["f_rows"], h + 1)
                nc.vector.tensor_tensor(core.big[:, T_FOXROW + 2 * h:T_FOXROW + 2 * h + 2, :], mix.fox_mask,
                                        bcast(ps[:, (6, 4)[h % 2], 0:SEQ], TT), ALU.subtract
                                        ).then_inc(s["rows_free"], 1)
            dve.wait_ge(s["lam_wide"], 1)
            nc.vector.tensor_copy(mix.neg_lam[:], ps[:, 5, 500:501])
            dve.wait_ge(s["sc_ready"], 1)
            for h, slope in enumerate(alibi(NSA)):
                g = h // 4
                at = h * TT * N_CMP
                ins = nc.vector.scalar_tensor_tensor(
                    out=sc[:, h * TT:(h + 1) * TT, :], in0=mix.dist_cmp[:], scalar=-slope,
                    in1=ps[:, g, at:at + TT * N_CMP].rearrange("p (t c) -> p t c", t=TT), op0=ALU.mult, op1=ALU.add)
            v.link(dve, ins)
            v.link(dve, nc.vector.tensor_reduce(st[:, 0, :], sc[:], AX.X, ALU.max))
            nc.vector.tensor_tensor(sc[:], sc[:], bcast(st[:, 0, :], N_CMP, 2), ALU.subtract
                                    ).then_inc(s["sc_diff"], 1)
            dve.wait_ge(s["sc_exp"], 1)
            v.link(dve, nc.vector.tensor_reduce(st[:, 1, :], sc[:], AX.X, ALU.add))
            v.link(dve, nc.vector.reciprocal(st[:, 1, :], st[:, 1, :]))
            dve.wait_ge(s["gates_ready"], 1)
            v.link(dve, nc.vector.tensor_tensor(
                st[:, 2, :].rearrange("p (h t) -> p h t", t=TT), st[:, 1, :].rearrange("p (h t) -> p h t", t=TT),
                mix.gates[:].rearrange("p t (h b) -> p h t b", b=3)[:, :, :, 0], ALU.mult))
            v.link(dve, nc.vector.tensor_tensor(sc[:], sc[:], bcast(st[:, 2, :], N_CMP, 2), ALU.mult))
            nc.vector.tensor_tensor(sc[:].rearrange("p (h t) c -> p h (t c)", t=TT),
                                    sc[:].rearrange("p (h t) c -> p h (t c)", t=TT),
                                    bcast(mix.valid_cmp[:].rearrange("p t c -> p (t c)"), NSA), ALU.mult
                                    ).then_inc(s["p_ready"], 1)


def phase_attention(nc, core, mix):
    ps, tok, big = core.ps, tokens(core), core.big
    packs = attention_packs()
    N = len(packs)
    maps_before = [sum(len(p[1]) for p in packs[:n]) for n in range(N + 1)]
    pairs = [[p[2][i:i + 2] for i in range(0, len(p[2]), 2)] for p in packs]
    pairs_before = [sum(len(x) for x in pairs[:n]) for n in range(N + 1)]
    dil_before = [sum(p[0] == "dil" for p in packs[:n]) for n in range(N + 1)]
    with ExitStack() as ctx:
        sem = lambda n: ctx.enter_context(nc.semaphore(n))
        scores_ready, scores_free, max_ready, exp_ready, p_ready, pt_ready, pt_free, pv_ready, pv_free, dil_diff, \
            dil_exp, sq_ready, ss_ready, rs_ready = (sem(n) for n in (
                "scores_ready", "scores_free", "max_ready", "exp_ready", "p_ready", "pt_ready", "pt_free",
                "pv_ready", "pv_free", "dil_diff", "dil_exp", "sq_ready", "ss_ready", "rs_ready"))
        stats = ctx.enter_context(nc.sbuf_tensor("stats", [P, 2, 6, 4, TT], F32))
        block = ctx.enter_context(nc.Block())
        S, PT = mix.S, mix.PT

        @block.tensor
        def _(pe):
            def scores(n):
                for m, (qt, kt, half, _) in enumerate(packs[n][1]):
                    if n >= 1:
                        before = min(m + 1, len(packs[n - 1][1]))
                        pe.wait_ge(scores_free, maps_before[n - 1] + before)
                    rows = slice(half * HD, (half + 1) * HD)
                    for c in range(TT):
                        ins = nc.tensor.matmul(ps[:, m, c * SEQ:(c + 1) * SEQ], big[rows, qt, c * P:(c + 1) * P],
                                               big[rows, kt, :], start=True, stop=True)
                    ins.then_inc(scores_ready, 1)

            scores(0)
            for n in range(N):
                if n + 1 < N:
                    scores(n + 1)
                pe.wait_ge(p_ready, n + 1)
                for m in range(len(packs[n][1])):
                    u = maps_before[n] + m
                    if u >= 2:
                        pe.wait_ge(pt_free, u - 1)
                    for j, (c, k) in enumerate(((0, 0), (1, 0), (1, 1))):
                        ins = nc.tensor.transpose(ps[:, 4 + u % 2, j * P:(j + 1) * P],
                                                  S[:, n % 2, m, c, k * P:(k + 1) * P], core.ident[:])
                    ins.then_inc(pt_ready, 1)
                pe.wait_ge(pt_free, maps_before[n + 1])
                for x, pair in enumerate(pairs[n]):
                    u = pairs_before[n] + x
                    if u >= 1:
                        pe.wait_ge(pv_free, u)
                    for y, (row, width, terms) in enumerate(pair):
                        up = width == HD and row % P == HD
                        parts = []
                        for m, col in terms:
                            if isinstance(m, tuple):
                                c0 = HD + HD * col
                                lhsT = mix.VC[0:N_CMP, c0 - HD * up:c0 + HD]
                                parts.append((0, SEQ, lhsT, mix.PTC[0:N_CMP, m[1], :]))
                            else:
                                for k in range(TT):
                                    lhsT = tok[:, k, col - HD * up:col + width]
                                    rhs = PT[:, n % 2, m, 0:SEQ] if k == 0 else PT[:, n % 2, m, SEQ:SEQ + P]
                                    parts.append((k * P, SEQ, lhsT, rhs))
                        height = HD + HD * up if width == HD else P
                        for z, (a, b, lhsT, rhs) in enumerate(parts):
                            ins = nc.tensor.matmul(ps[0:height, 6, y * SEQ + a:y * SEQ + b], lhsT, rhs,
                                                   start=(z == 0), stop=(z == len(parts) - 1),
                                                   skip_group_check=True)
                    ins.then_inc(pv_ready, 1)
            for n in range(2):
                pe.wait_ge(sq_ready, 1)
                nc.tensor.matmul(ps[:, n, :], core.ones[:], S[:, 0, n, :, :].rearrange("p c k -> p (c k)"),
                                 start=True, stop=True).then_inc(ss_ready, 1)

        @block.scalar
        def _(act):
            def exps(n):
                b = n % 2
                act.wait_ge(max_ready, n + 1)
                for m in range(len(packs[n][1])):
                    for c in range(TT):
                        ins = nc.scalar.activation(S[:, b, m, c, :], S[:, b, m, c, :], ACT.Exp,
                                                   bias=stats[:, b, 0, m, c:c + 1], accum_out=stats[:, b, 1, m, c:c + 1])
                ins.then_inc(exp_ready, 1)

            exps(0)
            for n in range(N):
                if n + 1 < N:
                    exps(n + 1)
                if packs[n][0] == "dil":
                    part = stats[:, n % 2, 2, 0:3, :]
                    act.wait_ge(dil_diff, dil_before[n] + 1)
                    nc.scalar.activation(part, part, ACT.Exp).then_inc(dil_exp, 1)
                for m in range(len(packs[n][1])):
                    u = maps_before[n] + m
                    act.wait_ge(pt_ready, u + 1)
                    nc.scalar.activation(PT[:, n % 2, m, :], ps[:, 4 + u % 2, 0:3 * P], ACT.Copy).then_inc(pt_free, 1)
                for x, pair in enumerate(pairs[n]):
                    act.wait_ge(pv_ready, pairs_before[n] + x + 1)
                    for y, (row, width, _) in enumerate(pair):
                        rows = slice(row % P, row % P + width)
                        ins = nc.scalar.activation(core.hT[rows, row // P, :], ps[rows, 6, y * SEQ:(y + 1) * SEQ],
                                                   ACT.Copy)
                    ins.then_inc(pv_free, 1)
            act.wait_ge(pv_free, pairs_before[N])
            heads = core.hT[:, KT - DIFF:KT, :]
            nc.scalar.activation(S[:, 0, 0:2, :, :].rearrange("p m c k -> p (m c k)"),
                                 heads.rearrange("p a b -> p (a b)"), ACT.Square).then_inc(sq_ready, 1)
            for n in range(2):
                act.wait_ge(ss_ready, n + 1)
                ins = nc.scalar.activation(S[:, 1, n, :, :].rearrange("p c k -> p (c k)"), ps[:, n, :], ACT.Ln,
                                           bias=core.eps[:], scale=1.0 / P)
            core.act.link(act, ins)
            nc.scalar.activation(S[:, 1, 0:2, :, :], S[:, 1, 0:2, :, :], ACT.Exp, scale=-0.5).then_inc(rs_ready, 1)

        @block.vector
        def _(dve):
            v = core.dve

            def biases(n):
                b = n % 2
                maps = packs[n][1]
                for m, (_, _, _, (table, slope)) in enumerate(maps):
                    dve.wait_ge(scores_ready, maps_before[n] + m + 1)
                    if table == "fox":
                        for c in range(TT):
                            ins = nc.vector.scalar_tensor_tensor(
                                out=S[:, b, m, c, :], in0=ps[:, m, c * SEQ:(c + 1) * SEQ],
                                scalar=mix.fox_cum[:, c, slope:slope + 1],
                                in1=big[:, T_FOXROW + 2 * slope + c, :], op0=ALU.add, op1=ALU.add)
                    else:
                        ins = nc.vector.scalar_tensor_tensor(
                            out=S[:, b, m, :, :], in0=mix.dist[:, table], scalar=-slope,
                            in1=ps[:, m, :].rearrange("p (c k) -> p c k", c=TT), op0=ALU.mult, op1=ALU.add)
                    ins.then_inc(scores_free, 1)
                dve.wait_ge(scores_free, maps_before[n + 1])
                nc.vector.tensor_reduce(stats[:, b, 0, 0:len(maps), :], S[:, b, 0:len(maps), :, :], AX.X, ALU.max,
                                        negate=True).then_inc(max_ready, 1)

            def weigh(n):
                b = n % 2
                kind, maps, _, first = packs[n]
                M = len(maps)
                top, total, part, factor = (stats[:, b, j] for j in range(4))
                dve.wait_ge(exp_ready, n + 1)
                if kind == "dil":
                    v.link(dve, nc.vector.tensor_reduce(factor[:, 3, :], top[:, 0:3, :].rearrange("p m c -> p c m"),
                                                        AX.X, ALU.min))
                    nc.vector.tensor_tensor(part[:, 0:3, :], bcast(factor[:, 3, :], 3), top[:, 0:3, :], ALU.subtract
                                            ).then_inc(dil_diff, 1)
                    dve.wait_ge(dil_exp, dil_before[n] + 1)
                    v.link(dve, nc.vector.tensor_tensor(total[:, 0:3, :], total[:, 0:3, :], part[:, 0:3, :], ALU.mult))
                    v.link(dve, nc.vector.tensor_reduce(factor[:, 3, :], total[:, 0:3, :].rearrange("p m c -> p c m"),
                                                        AX.X, ALU.add))
                    v.link(dve, nc.vector.reciprocal(factor[:, 3, :], factor[:, 3, :]))
                    v.link(dve, nc.vector.tensor_tensor(factor[:, 0:3, :], part[:, 0:3, :], bcast(factor[:, 3, :], 3),
                                                        ALU.mult))
                else:
                    v.link(dve, nc.vector.reciprocal(factor[:, 0:M, :], total[:, 0:M, :]))
                if kind == "nsa":
                    for m in range(M):
                        g = (first + m // 2) * 3 + 1 + m % 2
                        ins = nc.vector.tensor_tensor(factor[:, m, :], factor[:, m, :], mix.gates[:, :, g], ALU.mult)
                    v.link(dve, ins)
                if kind == "diff":
                    f = factor.rearrange("p (h m) c -> p h m c", m=2)[:, :, 1, :]
                    v.link(dve, nc.vector.tensor_scalar(f, f, mix.neg_lam[:], None, ALU.mult))
                nc.vector.tensor_tensor(S[:, b, 0:M].rearrange("p m c k -> p (m c) k"),
                                        S[:, b, 0:M].rearrange("p m c k -> p (m c) k"),
                                        bcast(factor[:, 0:M, :].rearrange("p m c -> p (m c)"), SEQ, 2), ALU.mult
                                        ).then_inc(p_ready, 1)

            biases(0)
            for n in range(N):
                if n + 1 < N:
                    if n >= 1:
                        dve.wait_ge(pt_ready, maps_before[n])
                    biases(n + 1)
                weigh(n)
            v.link(dve, nc.vector.tensor_scalar(core.aff[:, 0, 0:1], core.cols[:, C_SUBLN:C_SUBLN + 1],
                                                1.0 - LAM_INIT, None, ALU.mult))
            dve.wait_ge(rs_ready, 1)
            o = core.hT[:, KT - DIFF:KT, :].rearrange("p a b -> p (a b)")
            v.link(dve, nc.vector.scalar_tensor_tensor(out=o, in0=o, scalar=core.aff[:, 0, 0:1],
                                                       in1=S[:, 1, 0:2, :, :].rearrange("p m c k -> p (m c k)"),
                                                       op0=ALU.mult, op1=ALU.mult))


def mixer_memory(nc, ctx):
    mix = Core()
    sb = lambda name, shape: ctx.enter_context(nc.sbuf_tensor(name, shape, F32))
    mix.S = sb("scores", [P, 2, 4, TT, SEQ])
    mix.W1 = mix.S[:].rearrange("p b m c k -> p (b m c k)").rearrange("p (a l o) -> p a l o", a=2, l=32)
    mix.PT = sb("maps_t", [P, 2, 4, 3 * P])
    mix.PTC = sb("cmp_maps_t", [16, NSA, SEQ])
    mix.dist = sb("distances", [P, 4, TT, SEQ])
    mix.dist_cmp, mix.valid_cmp = sb("dist_cmp", [P, TT, N_CMP]), sb("valid_cmp", [P, TT, N_CMP])
    mix.fox_mask = mix.PT[:, 0, 2:4, 0:SEQ]
    mix.fox_cum, mix.gates = sb("fox_cum", [P, TT, FOX]), sb("nsa_gates", [P, TT, 3 * NSA])
    mix.neg_lam, mix.fox_bias = sb("neg_lambda", [P, 1]), sb("fox_bias", [FOX, 1])
    mix.lam_rows = sb("lambda_rows", [1, 4 * HD])
    mix.W2 = sb("cmp_w2", [HD, 2, 2 * HD])
    mix.VC = sb("cmp_values", [16, 3 * HD])
    mix.w_in = ctx.enter_context(nc.semaphore("small_weights_in"))
    return mix



def build(nc, t, out):
    with ExitStack() as ctx:
        core = Core()
        sb = lambda name, shape, dt=F32: ctx.enter_context(nc.sbuf_tensor(name, shape, dt))
        sem = lambda name: ctx.enter_context(nc.semaphore(name))
        core.ps = ctx.enter_context(nc.psum_tensor("accumulators", [P, 8, 512], F32))
        core.xT = sb("x_t", [P, KT, SEQ])
        core.hT = sb("h_t", [P, KT, SEQ])
        core.big = sb("wide", [P, 64, SEQ])
        core.ring = sb("weights", [P, RING, KG, CW])
        core.cols = sb("small_vectors", [P, N_VEC])
        core.mod = sb("modulation", [P, 2, NMOD])
        core.c_act = sb("c_act", [P, 2 * KT])
        core.aff = sb("affine", [P, 1, KT])
        core.lb = sb("lower_bounds", [P, 2, HH])
        core.ident, core.ones, core.incl, core.strict = (sb(n, [P, P]) for n in ("ident", "ones", "incl", "strict"))
        core.up_mask, core.low_mask = (sb(n, [P, len(LEVELS), P]) for n in ("up_mask", "low_mask"))
        core.keep = sb("keep", [P, SEQ])
        core.pick = sb("pick", [HH, HH, P])
        core.gates = sb("gates", [HH, 2 * SEQ])
        core.gdn_cols = sb("gdn_cols", [HH, 4])
        core.w_gates = sb("w_gates", [P, KT, 2 * HH])
        core.eps, core.one = sb("eps", [P, 1]), sb("one", [P, 1])
        core.used = sem("weights_used")
        core.landed = [sem(f"weights_landed_{s}") for s in range(RING)]
        core.free = [sem("low_accumulators_free"), sem("high_accumulators_free")]
        core.tile_ready, core.relu_steps = sem("tile_ready"), sem("relu_steps")
        core.act, core.dve, core.pool = (Chain(sem(f"{n}_steps")) for n in ("scalar", "vector", "pool"))
        core.tiles_ready_n, core.claimed = 0, [0, 0]
        core.ada_turns, core.norms, core.mods = 0, 0, 0
        core.norm_sems = [sem(n) for n in ("squares_ready", "sums_ready", "mean_ready", "root_ready", "scaled")]
        core.mod_rows_in, core.mod_turned = sem("mod_rows_in"), sem("mod_turned")
        core.ada_landed = [sem(f"ada_landed_{s}") for s in range(ASLOTS)]
        core.ada_steps, core.ada_sums_ready, core.ada_rows_ready, core.ada_rows_taken, core.ada_stored = (
            sem(f"ada_{n}") for n in ("steps", "sums_ready", "rows_ready", "rows_taken", "stored"))
        core.mod_dram = nc.dram_tensor("modulation_rows", (2, NMOD * P), F32, kind="Internal").ap()

        core.streams, at = {}, 0
        w_ff2 = t["w_ff2"][0].rearrange("(g k p) n -> p g k n", p=P, k=KG)
        w_down = t["ffn_w_down_2"][0].rearrange("(g k p) n -> p g k n", p=P, k=KG)
        gate, up = (t[n][0].rearrange("(g k p) n -> p g k n", p=P, k=KG) for n in ("ffn_w_gate_2", "ffn_w_up_2"))
        for name, source, unit, turns in (
                ("in_1", by_columns(t["w_in"][0]), TURN, 8),
                ("out_1", by_columns(t["w_out"][0]), TURN, 2),
                ("ff_1", by_columns(t["w_ff1"][0]), TURN, 8),
                ("ff_2", lambda i, q: w_ff2[:, q, :, bass.ds(i * CW, CW)], 2 * TURN, 4),
                ("in_2", in_2_source(t["w_in_2"][0]), TURN, 7),
                ("out_2", by_columns(t["w_out_2"][0]), TURN, 2),
                ("gate_up", lambda i, q: (gate if q < 4 else up)[:, q % 4, :, bass.ds(i * CW, CW)], TURN, 11),
                ("down", lambda i, q: w_down[:, q, :, i * CW:(i + 1) * CW], 11, 4)):
            core.streams[name] = Stream(source, unit, turns, at)
            at += unit * turns

        def into(dst):
            return lambda eng, tile, acc: nc.scalar.activation(dst[:, bass.ds(tile, 1), :], acc.unsqueeze(1), ACT.Copy)

        def add_to_x(gate):
            return lambda eng, tile, acc: nc.vector.scalar_tensor_tensor(
                out=core.xT[:, bass.ds(tile, 1), :].rearrange("p a b -> p (a b)"), in0=acc,
                scalar=core.mod[:, 1, bass.ds(tile + gate, 1)],
                in1=core.xT[:, bass.ds(tile, 1), :].rearrange("p a b -> p (a b)"), op0=ALU.mult, op1=ALU.add)

        h_tile, wide_tile = (lambda kt: core.hT[:, kt, :]), (lambda kt: core.big[:, kt, :])
        def square_relu(eng, tile, acc):
            nc.scalar.activation(acc, acc, ACT.Relu).then_inc(core.relu_steps, 1)
            eng.wait_ge(core.relu_steps, tile + 1)
            return nc.scalar.activation(core.big[:, bass.ds(tile, 1), :], acc.unsqueeze(1), ACT.Square)

        w_ada, w_ada_2 = t["w_ada"][0], t["ada_w_2"][0]
        phase_setup(nc, core, t)
        phase_ada_first(nc, core, t)
        phase_modulation(nc, core, 0, 0, 8)
        phase_norm(nc, core, C_PREMIX, 0, 0, KT)
        phase_product(nc, core, "in_1", "out_1", h_tile, into(core.big), ada=(w_ada, 0, 8))
        phase_modulation(nc, core, 0, 8, 16)
        phase_hgrn(nc, core)
        phase_gdn(nc, core)
        phase_product(nc, core, "out_1", "ff_1", h_tile, into(core.big[:, KT:2 * KT, :]))
        phase_residual_norm(nc, core, core.big[:, KT:2 * KT, :], C_POSTMIX, 2 * KT)
        phase_norm(nc, core, C_PREFFN, 0, 3 * KT, 4 * KT)
        phase_product(nc, core, "ff_1", "ff_2", h_tile, square_relu, ada=(w_ada_2, 1, 0))
        phase_product(nc, core, "ff_2", "in_2", wide_tile, into(core.hT), ada=(w_ada_2, 1, 16))
        phase_modulation(nc, core, 1, 0, 24)
        phase_residual_norm(nc, core, core.hT, C_POSTFFN, 5 * KT)
        phase_norm(nc, core, C_MIX2, 1, 0, KT)
        with ExitStack() as mix_ctx:
            mix = mixer_memory(nc, mix_ctx)
            phase_in_2(nc, core, mix, t)
            phase_compress(nc, core, mix)
            phase_attention(nc, core, mix)
        phase_product(nc, core, "out_2", "gate_up", h_tile, add_to_x(2 * KT), on="dve")
        phase_norm(nc, core, C_FFN2, 1, 3 * KT, 4 * KT)
        phase_swiglu(nc, core)
        phase_down(nc, core, 5 * KT)
        phase_norm(nc, core, C_FINAL)
        phase_write_out(nc, core, out)


INPUTS = ["x", "c", "w_ada", "b_ada", "pre_mix_norm", "post_mix_norm", "pre_ffn_norm", "post_ffn_norm", "w_in",
          "hg_lb_logits", "hg_norm", "gdn_conv_w", "gdn_a_log", "gdn_dt_bias", "gdn_norm", "w_out", "w_ff1", "w_ff2",
          "c_2", "ada_w_2", "ada_b_2", "norm_mix_g_2", "norm_ffn_g_2", "w_in_2", "fox_f_bias_2", "nsa_cmp_w1_2",
          "nsa_cmp_w2_2", "nsa_cmp_pos_2", "diff_lambda_2", "diff_subln_g_2", "w_out_2", "ffn_w_gate_2",
          "ffn_w_up_2", "ffn_w_down_2", "final_norm_g_2"]


def kernel(**inputs):
    import concourse.bacc as bacc
    from concourse.bass_utils import run_bass_kernel_spmd

    nc = bacc.Bacc("TRN2", target_bir_lowering=False, num_devices=1)
    arrays, t = {}, {}
    for name in INPUTS:
        a = np.ascontiguousarray(inputs[name])
        arrays[f"in_{name}"] = a
        t[name] = nc.dram_tensor(f"in_{name}", a.shape, mybir.dt.from_np(a.dtype), kind="ExternalInput").ap()
    out = nc.dram_tensor("out", (1, SEQ, D), F32, kind="ExternalOutput").ap()
    build(nc, t, out)
    return run_bass_kernel_spmd(nc, [arrays], core_ids=[0]).results[0]["out"]
```

```python
from contextlib import ExitStack

import numpy as np

import concourse.bass as bass
from concourse import mybir

ALU = mybir.AluOpType
ACT = mybir.ActivationFunctionType
AX = mybir.AxisListType
F32 = mybir.dt.float32
F32R = mybir.dt.float32r
I32 = mybir.dt.int32

P = 128
SEQ = 256
TT = SEQ // P
D = 2048
KT = D // P
NMOD = 6 * KT
EPS = 1e-6

RING = 2
TURN = 8
KG = 4
CW = 512
NT = CW // P

HH = 8
LEVELS = [64, 32, 16, 8, 4, 2, 1]

HQ, HF, HI, HG, GQ, GK, GV, GG = range(0, 64, 8)

VEC_PARTS = [("b_ada", 96), ("norms", 82), ("conv", 96), ("b_ada_2", 96), ("norms_2", 49), ("pos", 64)]
VEC_AT = {}
for _name, _rows in VEC_PARTS:
    VEC_AT[_name] = sum(r for n, r in VEC_PARTS[:len(VEC_AT)])
N_VEC = sum(r for _, r in VEC_PARTS)
C_BADA = VEC_AT["b_ada"]
C_PREMIX, C_POSTMIX, C_PREFFN, C_POSTFFN = (VEC_AT["norms"] + 16 * n for n in range(4))
C_HGNORM, C_GDNNORM, C_LB = (VEC_AT["norms"] + n for n in (64, 65, 66))
C_CONV = VEC_AT["conv"]
C_BADA2 = VEC_AT["b_ada_2"]
C_MIX2, C_FFN2, C_SUBLN, C_FINAL = (VEC_AT["norms_2"] + n for n in (0, 16, 32, 33))
C_POS = VEC_AT["pos"]


class Chain:

    def __init__(self, sem):
        self.sem, self.n = sem, 0

    def mark(self, ins):
        self.n += 1
        ins.then_inc(self.sem, 1)
        return self.n

    def link(self, eng, ins):
        eng.wait_ge(self.sem, self.mark(ins))


class Core:
    pass


def bcast(ap, n, axis=1):
    a = ap.unsqueeze(axis)
    return a.to_broadcast(list(a.shape[:axis]) + [n] + list(a.shape[axis + 1:]))



class Stream:

    def __init__(self, source, unit, turns, first):
        self.source, self.unit, self.turns, self.first = source, unit, turns, first
        self.groups = unit * turns


def by_columns(w, chunk0=0):
    v = w.rearrange("(g k p) n -> p g k n", p=P, k=KG)
    return lambda i, q: v[:, q % 4, :, bass.ds((i * 2 + (q // 4 + chunk0)) * CW, CW)]


def refill(sp, core, stream, i, q):
    slot = q % RING
    if isinstance(i, int):
        g = stream.first + stream.unit * i + q
        slot = g % RING
        if g >= RING:
            sp.wait_ge(core.used, g - RING + 1)
    else:
        sp.wait_ge(core.used, i * stream.unit + (stream.first + q - RING + 1))
    src = stream.source(i, q)
    sp.dma_start(core.ring[:, slot, 0:src.shape[1], 0:src.shape[2]], src).then_inc(core.landed[slot], 16)


def prefetch(sp, core, stream):
    for g in range(RING):
        refill(sp, core, stream, g // stream.unit, g % stream.unit)


def load_rest(sp, core, stream):
    if stream.unit % RING == 0:
        with sp.Fori(0, stream.turns - 1) as i:
            for q in range(RING, stream.unit):
                refill(sp, core, stream, i, q)
            for q in range(RING):
                refill(sp, core, stream, i + 1, q)
        for q in range(RING, stream.unit):
            refill(sp, core, stream, stream.turns - 1, q)
    else:
        for g in range(RING, stream.groups):
            refill(sp, core, stream, g // stream.unit, g % stream.unit)



def phase_setup(nc, core, t, ada):
    vec_rows = core.big[:, 16:19, :].rearrange("p a b -> p (a b)").rearrange("p (v n) -> p v n", n=P)
    c_rows = core.big[0:32, 20, 0:P]
    x_rows = core.big[:, 0:16, :].rearrange("p a b -> p (a b)").rearrange("p (t f) -> p t f", t=TT)
    with ExitStack() as ctx:
        x_in, vec_in, c_in, small_in, ones_done, ident_done, vec_t, c_t, x_t, x_free, made = (
            ctx.enter_context(nc.semaphore(n)) for n in
            ("x_in", "vec_in", "c_in", "small_in", "ones_done", "ident_done", "vec_t", "c_t", "x_t", "x_free",
             "made"))
        lb_tmp = ctx.enter_context(nc.sbuf_tensor("lb_tmp", [P, 4, HH], F32))
        block = ctx.enter_context(nc.Block())

        @block.sync
        def _(sp):
            rows = lambda a, r: a.rearrange("l n -> (l n)").rearrange("(r p) -> r p", p=P)
            sp.dma_start(c_rows[0:KT], rows(t["c"], KT)).then_inc(c_in, 16)
            sp.dma_start(c_rows[KT:2 * KT], rows(t["c_2"], KT)).then_inc(c_in, 16)
            sp.dma_start(x_rows, t["x"][0].rearrange("(t p) f -> p t f", p=P)).then_inc(x_in, 16)
            sp.wait_ge(vec_in, 16 * 16)
            sp.wait_ge(small_in, 48)
            ada.first_loads(sp)

        @block.scalar
        def _(act):
            def load(part, at, src):
                act.dma_start(vec_rows[at:at + src.shape[0], part, 0:src.shape[1]], src).then_inc(vec_in, 16)

            rows = lambda a: a.rearrange("l n -> (l n)").rearrange("(r p) -> r p", p=P)
            load(0, 0, rows(t["b_ada"]))
            for n, name in enumerate(("pre_mix_norm", "post_mix_norm", "pre_ffn_norm", "post_ffn_norm")):
                load(1, 16 * n, rows(t[name]))
            load(1, 64, t["hg_norm"])
            load(1, 65, t["gdn_norm"])
            load(1, 66, t["hg_lb_logits"].rearrange("l h d -> (l h) d"))
            load(2, 0, t["gdn_conv_w"][0].rearrange("k (c p) -> (k c) p", p=P))
            load(3, 0, rows(t["ada_b_2"]))
            load(4, 0, rows(t["norm_mix_g_2"]))
            load(4, 16, rows(t["norm_ffn_g_2"]))
            load(4, 32, t["diff_subln_g_2"])
            load(4, 33, t["final_norm_g_2"].rearrange("(r p) -> r p", p=P))
            pos = t["nsa_cmp_pos_2"][0].rearrange("a l d -> (a l) d")
            load(5, 0, pos)
            act.dma_start(vec_rows[0:64, 5, 64:128], pos).then_inc(vec_in, 16)
            with nc.allow_non_contiguous_dma("eight numbers, one a partition"):
                act.dma_start(core.gdn_cols[:, 0:1], t["gdn_a_log"].rearrange("l h -> h l")).then_inc(small_in, 16)
                act.dma_start(core.gdn_cols[:, 1:2], t["gdn_dt_bias"].rearrange("l h -> h l")).then_inc(small_in, 16)
            with nc.allow_non_contiguous_dma("the 16 gate columns"):
                act.dma_start(core.w_gates[:], t["w_in"][0, :, 8192:8208].rearrange("(k p) n -> p k n", p=P)
                              ).then_inc(small_in, 16)
            act.wait_ge(c_t, 1)
            core.act.mark(nc.scalar.activation(core.c_act[:], core.ps[:, 5, 0:2 * KT], ACT.Silu))
            for j in range(KT // 2):
                act.wait_ge(x_t, j + 1)
                nc.scalar.activation(core.xT[:, 2 * j:2 * j + 2, :], core.ps[:, j % 4, :], ACT.Copy
                                     ).then_inc(x_free, 1)
            act.wait_ge(made, 2)
            core.act.link(act, nc.scalar.activation(lb_tmp[:, 1, :], lb_tmp[:, 0, :], ACT.Exp))
            core.act.link(act, nc.scalar.activation(lb_tmp[:, 2, :], lb_tmp[:, 3, :], ACT.Exp))
            act.wait_ge(small_in, 48)
            core.act.link(act, nc.scalar.activation(core.gdn_cols[:, 2:3], core.gdn_cols[:, 0:1], ACT.Exp))

        @block.gpsimd
        def _(pool):
            nc.gpsimd.memset(core.ident[:], 0.0).then_inc(core.pool.sem, 1)
            core.pool.n += 1
            pool.wait_ge(core.pool.sem, core.pool.n)
            nc.gpsimd.affine_select(out=core.ident[:], in_=core.ident[:], compare_op=ALU.not_equal, fill=1.0,
                                    base=0, pattern=[[-1, P]], channel_multiplier=1).then_inc(ident_done, 1)
            nc.gpsimd.memset(core.ones[:], 1.0).then_inc(ones_done, 1)
            pool.wait_ge(ones_done, 1)
            nc.gpsimd.affine_select(out=core.incl[:], in_=core.ones[:], compare_op=ALU.is_ge, fill=0.0,
                                    base=0, pattern=[[1, P]], channel_multiplier=-1)
            nc.gpsimd.affine_select(out=core.strict[:], in_=core.ones[:], compare_op=ALU.is_gt, fill=0.0,
                                    base=0, pattern=[[1, P]], channel_multiplier=-1)
            for n, L in enumerate(LEVELS):
                nb = P // (2 * L)
                for m, lo in ((core.up_mask, 0), (core.low_mask, L)):
                    v = m[:, n, :].rearrange("p (b two l) -> p b two l", b=nb, two=2)
                    o = core.ones[:].rearrange("p (b two l) -> p b two l", b=nb, two=2)
                    half = 1 if lo == 0 else 0
                    core.pool.link(pool, nc.gpsimd.memset(m[:, n, :], 0.0))
                    core.pool.link(pool, nc.gpsimd.affine_select(
                        out=v[:, :, half, :], in_=o[:, :, half, :], compare_op=ALU.is_ge, fill=0.0, base=-lo,
                        pattern=[[-2 * L, nb], [0, L]], channel_multiplier=1))
                    core.pool.link(pool, nc.gpsimd.affine_select(
                        out=v[:, :, half, :], in_=v[:, :, half, :], compare_op=ALU.is_gt, fill=0.0, base=lo + L,
                        pattern=[[2 * L, nb], [0, L]], channel_multiplier=-1))
            core.pool.link(pool, nc.gpsimd.memset(core.keep[:], 1.0))
            core.pool.link(pool, nc.gpsimd.memset(core.eps[:], EPS))
            core.pool.link(pool, nc.gpsimd.memset(core.one[:], 1.0))
            core.pool.link(pool, nc.gpsimd.memset(core.keep[:].rearrange("p (c t) -> p c t", c=TT)[:, :, 0:1], 0.0))
            core.pool.link(pool, nc.gpsimd.memset(core.pick[:], 0.0))
            core.pool.link(pool, nc.gpsimd.affine_select(
                out=core.pick[:], in_=core.pick[:], compare_op=ALU.not_equal, fill=1.0, base=0,
                pattern=[[-1, HH], [0, P]], channel_multiplier=1))

        @block.tensor
        def _(pe):
            pe.wait_ge(ident_done, 1)
            pe.wait_ge(c_in, 32)
            nc.tensor.transpose(core.ps[:, 5, 0:2 * KT], c_rows, core.ident[0:32, 0:32]).then_inc(c_t, 1)
            pe.wait_ge(x_in, 16)
            for j in range(KT // 2):
                if j >= 4:
                    pe.wait_ge(x_free, j - 3)
                for f in range(2):
                    for tt in range(TT):
                        ins = nc.tensor.transpose(core.ps[:, j % 4, (f * TT + tt) * P:(f * TT + tt + 1) * P],
                                                  x_rows[:, tt, (2 * j + f) * P:(2 * j + f + 1) * P], core.ident[:])
                ins.then_inc(x_t, 1)
            pe.wait_ge(vec_in, 16 * 16)
            for n, (name, rows) in enumerate(VEC_PARTS):
                ins = nc.tensor.transpose(core.ps[:, 4, VEC_AT[name]:VEC_AT[name] + rows],
                                          vec_rows[0:rows, n, :], core.ident[0:rows, 0:rows])
            ins.then_inc(vec_t, 1)

        @block.vector
        def _(dve):
            v = core.dve
            for f in (core.free[0], core.free[1]):
                dve.sem_inc(f, NT)
            for f in (core.ada_rows_ready, core.ada_stored):
                dve.sem_inc(f, 1)
            dve.wait_ge(vec_t, 1)
            v.link(dve, nc.vector.tensor_copy(core.cols[:], core.ps[:, 4, 0:N_VEC]))
            a, b = core.cols[:, C_LB:C_LB + HH], core.cols[:, C_LB + HH:C_LB + 2 * HH]
            v.link(dve, nc.vector.tensor_tensor(lb_tmp[:, 3, :], a, b, ALU.max))
            nc.vector.tensor_tensor(lb_tmp[:, 0, :], a, lb_tmp[:, 3, :], ALU.subtract).then_inc(made, 1)
            nc.vector.tensor_tensor(lb_tmp[:, 3, :], b, lb_tmp[:, 3, :], ALU.subtract).then_inc(made, 1)
            dve.wait_ge(core.act.sem, 4)
            v.link(dve, nc.vector.tensor_tensor(lb_tmp[:, 2, :], lb_tmp[:, 1, :], lb_tmp[:, 2, :], ALU.add))
            v.link(dve, nc.vector.reciprocal(lb_tmp[:, 2, :], lb_tmp[:, 2, :]))
            v.link(dve, nc.vector.tensor_tensor(core.lb[:, 0, :], lb_tmp[:, 1, :], lb_tmp[:, 2, :], ALU.mult))
            v.link(dve, nc.vector.tensor_scalar(core.lb[:, 1, :], core.lb[:, 0, :], -1.0, 1.0, ALU.mult, ALU.add))
            v.link(dve, nc.vector.tensor_scalar(core.gdn_cols[:, 3:4], core.gdn_cols[:, 2:3], -1.0, None, ALU.mult))



AK = 2
ASLOTS = 4
FIRST_ASLOTS = 16
ATURN = 2
AGROUPS = KT // AK


class Ada:

    def __init__(self, ctx, nc, core, w, which, chunk0, turns, slots=ASLOTS):
        self.slots, self.landed = slots, core.ada_landed[slots]
        self.landed_turns = core.ada_landed_turns[slots]
        core.ada_landed_turns[slots] += turns
        self.nc, self.core, self.which, self.chunk0, self.turns = nc, core, which, chunk0, turns
        self.w = w.rearrange("(g k p) n -> p g k n", p=P, k=AK)
        self.before = core.ada_turns
        core.ada_turns += turns
        sb = lambda name, shape: ctx.enter_context(nc.sbuf_tensor(name, shape, F32))
        self.ring = sb(f"ada_weights_{self.before}", [P, slots, AK, CW])
        self.acc = sb(f"ada_sums_{self.before}", [P, ATURN, 2, CW])
        self.row = core.gates[0:1, 0:ATURN * CW].rearrange("p (c n) -> p c n", n=CW)

    def load(self, queue, i, q):
        chunk = i * ATURN + (q // AGROUPS + self.chunk0)
        queue.dma_start(self.ring[:, q % self.slots], self.w[:, q % AGROUPS, :, bass.ds(chunk * CW, CW)]
                       ).then_inc(self.landed[q % self.slots], 16)

    def load_when_free(self, queue, i, q):
        steps = AK * AGROUPS * ATURN
        queue.wait_ge(self.core.ada_steps, i * steps + (self.before * steps + AK * (q - self.slots + 1)))
        self.load(queue, i, q)

    def first_loads(self, queue):
        for q in range(self.slots):
            self.load(queue, 0, q)

    def other_loads(self, queue):
        n = ATURN * AGROUPS
        with queue.Fori(0, self.turns - 1) as i:
            for q in range(self.slots, n):
                self.load_when_free(queue, i, q)
            for q in range(self.slots):
                self.load_when_free(queue, i + 1, q)
        for q in range(self.slots, n):
            self.load_when_free(queue, self.turns - 1, q)

    def multiply(self, dve, i):
        for s in range(ATURN * KT):
            self.step(dve, i, s)

    def step(self, dve, i, s):
        nc, core = self.nc, self.core
        per_slot = ATURN * AGROUPS // self.slots
        c, k = s // KT, s % KT
        if s == 0:
            dve.wait_ge(core.ada_rows_ready, i * ATURN + (self.before * ATURN + 1))
        q = c * AGROUPS + k // AK
        if k % AK == 0:
            dve.wait_ge(self.landed[q % self.slots],
                        i * (16 * per_slot) + 16 * (self.landed_turns * per_slot + q // self.slots + 1))
        w = self.ring[:, q % self.slots, k % AK, :]
        acc = self.acc[:, c, k % 2, :]
        number = core.c_act[:, KT * self.which + k:KT * self.which + k + 1]
        if k < 2:
            ins = nc.vector.tensor_scalar(acc, w, number, None, ALU.mult)
        else:
            dve.wait_ge(core.ada_steps, i * (KT * ATURN) + (self.before * KT * ATURN + KT * c + k - 1))
            ins = nc.vector.scalar_tensor_tensor(out=acc, in0=w, scalar=number, in1=acc, op0=ALU.mult,
                                                 op1=ALU.add)
        ins.then_inc(core.ada_steps, 1)
        if k == KT - 1:
            dve.wait_ge(core.ada_steps, i * (KT * ATURN) + (self.before * KT * ATURN + KT * (c + 1)))
            nc.vector.tensor_tensor(self.acc[:, c, 0, :], self.acc[:, c, 0, :], self.acc[:, c, 1, :], ALU.add
                                    ).then_inc(core.ada_sums_ready, 1)

    def sum_rows(self, pe, i, bank0):
        nc, core = self.nc, self.core
        for c in range(ATURN):
            pe.wait_ge(core.ada_sums_ready, i * ATURN + (self.before * ATURN + c + 1))
            for h in range(2):
                ins = nc.tensor.matmul(core.ps[0:1, bank0 + 2 * c + h, SEQ:2 * SEQ], core.ones[:, 0:1],
                                       self.acc[:, c, 0, h * SEQ:(h + 1) * SEQ], start=True, stop=True)
            ins.then_inc(core.ada_rows_ready, 1)

    def store_rows(self, act, i, bank0):
        nc, core = self.nc, self.core
        act.wait_ge(core.ada_rows_ready, i * ATURN + (self.before * ATURN + ATURN + 1))
        act.wait_ge(core.ada_stored, i * 16 + (self.before * 16 + 1))
        nc.scalar.activation(self.row.rearrange("p c (h n) -> p (c h) n", h=2),
                             core.ps[0:1, bank0:bank0 + 2 * ATURN, SEQ:2 * SEQ], ACT.Copy
                             ).then_inc(core.ada_rows_taken, 1)
        act.wait_ge(core.ada_rows_taken, i + (self.before + 1))
        act.dma_start(core.mod_dram[self.which:self.which + 1, bass.ds((i * ATURN + self.chunk0) * CW, ATURN * CW)],
                      self.row.rearrange("p c n -> p (c n)")).then_inc(core.ada_stored, 16)


def phase_ada_first(nc, core, ada):
    with ExitStack() as ctx:
        block = ctx.enter_context(nc.Block())

        @block.sync
        def _(sp):
            ada.other_loads(sp)
            prefetch(sp, core, core.streams["in_1"])

        @block.vector
        def _(dve):
            with dve.Fori(0, ada.turns) as i:
                ada.multiply(dve, i)

        @block.tensor
        def _(pe):
            sum_squares(nc, core, pe, core.norms, SUMS_X)
            with pe.Fori(0, ada.turns) as i:
                ada.sum_rows(pe, i, 0)
                pe.wait_ge(core.ada_rows_taken, i + (ada.before + 1))

        @block.scalar
        def _(act):
            for n in range(4):
                squares(nc, core, act, core.xT, n).then_inc(core.norm_sems[0], 1)
            with act.Fori(0, ada.turns) as i:
                ada.store_rows(act, i, 0)


def phase_modulation(nc, core, which, chunk0, chunks):
    n = NT * chunks
    with ExitStack() as ctx:
        rows_in, turned = core.mod_rows_in, core.mod_turned
        core.mods += 1
        rows = ctx.enter_context(nc.sbuf_tensor(f"mod_rows_{which}_{chunk0}", [n, P], F32))
        block = ctx.enter_context(nc.Block())

        @block.sync
        def _(sp):
            sp.wait_ge(core.ada_stored, 16 * core.ada_turns + 1)
            src = core.mod_dram[which, chunk0 * CW:(chunk0 + chunks) * CW].rearrange("(r p) -> r p", p=P)
            sp.dma_start(rows[:], src).then_inc(rows_in, 16)

        @block.tensor
        def _(pe):
            pe.wait_ge(rows_in, 16 * core.mods)
            nc.tensor.transpose(core.ps[:, 7, 0:n], rows[:], core.ident[0:n, 0:n]).then_inc(turned, 1)

        @block.vector
        def _(dve):
            dve.wait_ge(turned, core.mods)
            bias = (C_BADA, C_BADA2)[which] + NT * chunk0
            core.dve.link(dve, nc.vector.tensor_tensor(core.mod[:, which, NT * chunk0:NT * chunk0 + n],
                                                       core.ps[:, 7, 0:n], core.cols[:, bias:bias + n], ALU.add))



SUMS_X = 4


def squares(nc, core, act, src, n):
    return nc.scalar.activation(core.big[:, 4 * n:4 * n + 4, :], src[:, 4 * n:4 * n + 4, :], ACT.Square)


def sum_squares(nc, core, pe, n0, bank):
    sq_ready, sums_ready = core.norm_sems[:2]
    for k in range(KT):
        if k % 4 == 0:
            pe.wait_ge(sq_ready, 4 * n0 + k // 4 + 1)
        ins = nc.tensor.matmul(core.ps[:, bank, 0:SEQ], core.ones[:], core.big[:, k, :],
                               start=(k == 0), stop=(k == KT - 1))
    ins.then_inc(sums_ready, 1)


def phase_norm(nc, core, gain, which=None, shift=None, scale=None, summed=False):
    n0 = core.norms
    core.norms += 1
    with ExitStack() as ctx:
        sq_ready, sums_ready, ms_ready, root_ready, inv_ready = core.norm_sems
        rs = ctx.enter_context(nc.sbuf_tensor(f"inv_rms_{gain}", [P, SEQ], F32))
        block = ctx.enter_context(nc.Block())

        @block.scalar
        def _(act):
            if not summed:
                for n in range(4):
                    squares(nc, core, act, core.xT, n).then_inc(sq_ready, 1)
            act.wait_ge(ms_ready, n0 + 1)
            nc.scalar.activation(rs[:], rs[:], ACT.Sqrt).then_inc(root_ready, 1)
            for k in range(1, KT, 2):
                act.wait_ge(inv_ready, 4 * n0 + k // 4 + 1)
                if which is None:
                    nc.scalar.activation(core.hT[:, k, :], core.hT[:, k, :], ACT.Copy,
                                         scale=core.aff[:, 0, k:k + 1])
                else:
                    nc.scalar.activation(core.hT[:, k, :], core.hT[:, k, :], ACT.Identity,
                                         bias=core.mod[:, which, shift + k:shift + k + 1],
                                         scale=core.aff[:, 0, k:k + 1])

        @block.tensor
        def _(pe):
            if not summed:
                sum_squares(nc, core, pe, n0, SUMS_X)

        @block.vector
        def _(dve):
            v = core.dve
            if which is None:
                v.link(dve, nc.vector.tensor_copy(core.aff[:, 0, :], core.cols[:, gain:gain + KT]))
            else:
                v.link(dve, nc.vector.scalar_tensor_tensor(
                    out=core.aff[:, 0, :], in0=core.mod[:, which, scale:scale + KT], scalar=1.0,
                    in1=core.cols[:, gain:gain + KT], op0=ALU.add, op1=ALU.mult))
            dve.wait_ge(sums_ready, n0 + 1)
            nc.vector.tensor_scalar(rs[:], core.ps[:, SUMS_X, 0:SEQ], 1.0 / D, EPS, ALU.mult, ALU.add
                                    ).then_inc(ms_ready, 1)
            dve.wait_ge(root_ready, n0 + 1)
            v.link(dve, nc.vector.reciprocal(rs[:], rs[:]))
            for n in range(4):
                nc.vector.tensor_tensor(core.hT[:, 4 * n:4 * n + 4, :], core.xT[:, 4 * n:4 * n + 4, :],
                                        bcast(rs[:], 4), ALU.mult).then_inc(inv_ready, 1)
            dve.wait_ge(inv_ready, 4 * n0 + 4)
            for k in range(0, KT, 2):
                if which is None:
                    nc.vector.tensor_scalar(core.hT[:, k, :], core.hT[:, k, :], core.aff[:, 0, k:k + 1], None,
                                            ALU.mult)
                else:
                    nc.vector.tensor_scalar(core.hT[:, k, :], core.hT[:, k, :], core.aff[:, 0, k:k + 1],
                                            core.mod[:, which, shift + k:shift + k + 1], ALU.mult, ALU.add)


def phase_residual_norm(nc, core, y, gain, gate):
    n0 = core.norms
    core.norms += 1
    with ExitStack() as ctx:
        sq_ready, sums_ready, ms_ready, root_ready, scaled = core.norm_sems
        x_added = ctx.enter_context(nc.semaphore(f"x_added_{gain}"))
        rs = ctx.enter_context(nc.sbuf_tensor(f"inv_rms_{gain}", [P, SEQ], F32))
        block = ctx.enter_context(nc.Block())

        @block.scalar
        def _(act):
            for n in range(4):
                squares(nc, core, act, y, n).then_inc(sq_ready, 1)
            act.wait_ge(ms_ready, n0 + 1)
            nc.scalar.activation(rs[:], rs[:], ACT.Sqrt).then_inc(root_ready, 1)
            for n in range(4):
                act.wait_ge(x_added, n + 1)
                squares(nc, core, act, core.xT, n).then_inc(sq_ready, 1)

        @block.tensor
        def _(pe):
            sum_squares(nc, core, pe, n0, 0)
            sum_squares(nc, core, pe, n0 + 1, SUMS_X)

        @block.vector
        def _(dve):
            v = core.dve
            v.link(dve, nc.vector.tensor_tensor(core.aff[:, 0, :], core.mod[:, 0, gate:gate + KT],
                                                core.cols[:, gain:gain + KT], ALU.mult))
            dve.wait_ge(sums_ready, n0 + 1)
            nc.vector.tensor_scalar(rs[:], core.ps[:, 0, 0:SEQ], 1.0 / D, EPS, ALU.mult, ALU.add
                                    ).then_inc(ms_ready, 1)
            dve.wait_ge(root_ready, n0 + 1)
            v.link(dve, nc.vector.reciprocal(rs[:], rs[:]))
            for n in range(4):
                nc.vector.tensor_tensor(core.hT[:, 4 * n:4 * n + 4, :], y[:, 4 * n:4 * n + 4, :],
                                        bcast(rs[:], 4), ALU.mult).then_inc(scaled, 1)
            for k in range(KT):
                if k % 4 == 0:
                    dve.wait_ge(scaled, 4 * n0 + k // 4 + 1)
                ins = nc.vector.scalar_tensor_tensor(out=core.xT[:, k, :], in0=core.hT[:, k, :],
                                                     scalar=core.aff[:, 0, k:k + 1], in1=core.xT[:, k, :],
                                                     op0=ALU.mult, op1=ALU.add)
                if k % 4 == 3:
                    ins.then_inc(x_added, 1)





def phase_split_product(nc, core, name, following, chunk_steps, ada=None):
    st = core.streams[name]
    tr0, f0 = core.tiles_ready_n, list(core.claimed)
    g0, x0 = core.split_groups, core.split_phases
    chunks = len(chunk_steps)
    per_chunk = st.unit // chunks
    tiles_per_turn = KG * st.unit
    wide = per_chunk > 4
    depth = KG if ada and not wide else 2 * KG
    take = depth // KG
    rows_bank = NT * (2 - chunks)
    with ExitStack() as ctx:
        ada = Ada(ctx, nc, core, *ada, st.turns) if ada else None
        x = ctx.enter_context(nc.sbuf_tensor(f"h_parts_{g0}", [P, depth if wide else KT, 2, SEQ], F32R))
        w = ctx.enter_context(nc.sbuf_tensor(f"weight_parts_{g0}", [P, depth, 2, CW], F32R))
        block = ctx.enter_context(nc.Block())

        def row_tile(i, q, k):
            return i * tiles_per_turn + (KG * (g0 + q) + k)

        def tile_done(eng, i, c, nt):
            if nt < NT - 1:
                eng.wait_ge(core.tile_ready, i * (3 * chunks) + (tr0 + 3 * c + nt + 1))
            else:
                eng.wait_ge(core.parts_used, row_tile(i, per_chunk * (c + 1), 0))

        def empty(eng, which, i, c):
            on, step = chunk_steps[c]
            if on == which:
                for nt in range(NT):
                    tile_done(eng, i, c, nt)
                    step(eng, i, NT * c + nt, core.ps[:, NT * c + nt, 0:SEQ]).then_inc(core.free[c], 1)

        @block.sync
        def _(sp):
            load_rest(sp, core, st)
            if following:
                prefetch(sp, core, core.streams[following])

        @block.scalar
        def _(act):
            def high_x(n):
                if not wide:
                    tiles = slice(4 * n, 4 * n + 4)
                    nc.scalar.activation(x[:, tiles, 0, :], core.hT[:, tiles, :], ACT.Copy).then_inc(core.x_high, 1)

            def high(i, q):
                fills = st.unit // RING
                act.wait_ge(core.landed[q % RING], i * (16 * fills) + 16 * ((st.first + q) // RING + 1))
                for k in range(0, KG, take):
                    held, kt = (KG * q + k) % depth, KG * (q % per_chunk) + k
                    if g0 or KG * q + k >= depth or not isinstance(i, int):
                        act.wait_ge(core.parts_used, row_tile(i, q, k) + (take - depth))
                    if wide:
                        nc.scalar.activation(x[:, held:held + take, 0, :], core.big[:, kt:kt + take, :], ACT.Copy)
                    nc.scalar.activation(w[:, held:held + take, 0, :], core.ring[:, q % RING, k:k + take, :], ACT.Copy
                                         ).then_inc(core.high_ready, take)

            def turn(i):
                for q in range(1, st.unit):
                    high(i, q)
                    if q == per_chunk:
                        empty(act, "act", i, 0)
                if ada:
                    ada.store_rows(act, i, rows_bank)

            high_x(0)
            high(0, 0)
            for n in range(1, 4):
                high_x(n)
            with act.Fori(0, st.turns - 1) as i:
                turn(i)
                high(i + 1, 0)
                empty(act, "act", i, chunks - 1)
            turn(st.turns - 1)
            empty(act, "act", st.turns - 1, chunks - 1)

        @block.vector
        def _(dve):
            def low_x(n):
                if not wide:
                    tiles = slice(4 * n, 4 * n + 4)
                    dve.wait_ge(core.x_high, 4 * x0 + n + 1)
                    nc.vector.tensor_tensor(x[:, tiles, 1, :], core.hT[:, tiles, :], x[:, tiles, 0, :].bitcast(F32),
                                            ALU.subtract).then_inc(core.x_low, 1)

            def low(i, q):
                for k in range(0, KG, take):
                    held, kt = (KG * q + k) % depth, KG * (q % per_chunk) + k
                    dve.wait_ge(core.high_ready, row_tile(i, q, k) + take)
                    if wide:
                        nc.vector.tensor_tensor(x[:, held:held + take, 1, :], core.big[:, kt:kt + take, :],
                                                x[:, held:held + take, 0, :].bitcast(F32), ALU.subtract)
                    ins = nc.vector.tensor_tensor(w[:, held:held + take, 1, :], core.ring[:, q % RING, k:k + take, :],
                                                  w[:, held:held + take, 0, :].bitcast(F32), ALU.subtract)
                    if k + take == KG:
                        ins.then_inc(core.used, 1)
                    else:
                        ins.then_inc(core.low_ready, 1 if take == 1 else KG - 1)
                    if ada and q < st.unit - 1:
                        n, slots, at = ATURN * KT, KG * (st.unit - 1) // take, (KG * q + k) // take
                        for s in range(n * at // slots, n * (at + 1) // slots):
                            ada.step(dve, i, s)

            def turn(i):
                for q in range(1, st.unit):
                    low(i, q)
                    if q == per_chunk:
                        empty(dve, "dve", i, 0)

            low_x(0)
            low(0, 0)
            for n in range(1, 4):
                low_x(n)
            with dve.Fori(0, st.turns - 1) as i:
                turn(i)
                low(i + 1, 0)
                empty(dve, "dve", i, chunks - 1)
            turn(st.turns - 1)
            empty(dve, "dve", st.turns - 1, chunks - 1)

        @block.tensor
        def _(pe):
            with pe.Fori(0, st.turns) as i:
                for q in range(st.unit):
                    c = q // per_chunk
                    if ada and q == st.unit - 1:
                        if chunks == 2:
                            pe.wait_ge(core.free[0], i * NT + (f0[0] + 2 * NT))
                        ada.sum_rows(pe, i, rows_bank)
                    for k in range(KG):
                        kt = KG * (q % per_chunk) + k
                        accs = [core.ps[:, NT * c + nt, 0:SEQ] for nt in range(NT)]
                        cols = [slice(nt * P, (nt + 1) * P) for nt in range(NT)]
                        held = (KG * q + k) % depth
                        xk = x[:, held if wide else kt]
                        if not wide and c == 0 and k == 0:
                            pe.wait_ge(core.x_low, 4 * x0 + q + 1)
                        pe.wait_ge(core.high_ready, row_tile(i, q, k) + 1)
                        for nt in range(NT):
                            if kt == 0:
                                if ada and c == 0 and nt == 0:
                                    pe.wait_ge(core.ada_rows_taken, i + ada.before)
                                pe.wait_ge(core.free[c], i * NT + (f0[c] + nt + 1))
                            nc.tensor.matmul(accs[nt], w[:, held, 0, cols[nt]], xk[:, 0, :], start=(kt == 0), stop=False)
                        if k < KG - take:
                            pe.wait_ge(core.low_ready, i * ((KG - 1) * st.unit) + ((KG - 1) * (g0 + q) + k + 1))
                        else:
                            pe.wait_ge(core.used, i * st.unit + (st.first + q + 1))
                        for nt in range(NT):
                            nc.tensor.matmul(accs[nt], w[:, held, 0, cols[nt]], xk[:, 1, :], start=False, stop=False)
                            ins = nc.tensor.matmul(accs[nt], w[:, held, 1, cols[nt]], xk[:, 0, :], start=False,
                                                   stop=(kt == KG * per_chunk - 1))
                            if kt == KG * per_chunk - 1 and nt < NT - 1:
                                ins.then_inc(core.tile_ready, 1)
                        ins.then_inc(core.parts_used, 1)

        if ada:
            @block.gpsimd
            def _(pool):
                ada.first_loads(pool)
                ada.other_loads(pool)
    core.split_groups += st.groups
    core.split_phases += 0 if wide else 1
    core.tiles_ready_n += 3 * chunks * st.turns
    for c in range(chunks):
        core.claimed[c] += NT * st.turns



class Banks:

    COUNT = 6

    def __init__(self, ctx, nc, uses):
        self.at, self.order = {}, []
        seen = {"act": 0, "dve": 0}
        for name, engine in uses:
            seen[engine] += 1
            self.at[name] = len(self.order)
            self.order.append((engine, seen[engine]))
        self.filled = ctx.enter_context(nc.semaphore("bank_filled"))
        self.emptied = {e: ctx.enter_context(nc.semaphore(f"bank_emptied_{e}")) for e in seen}

    def bank(self, name):
        return self.at[name] % self.COUNT

    def wait_empty(self, pe, name):
        before = self.at[name] - self.COUNT
        if before >= 0:
            engine, n = self.order[before]
            pe.wait_ge(self.emptied[engine], n)

    def wait_filled(self, eng, name):
        eng.wait_ge(self.filled, self.at[name] + 1)



def phase_hgrn(nc, core, conv):
    big, ps = core.big, core.ps
    flat = lambda a, n: big[:, a:a + n, :].rearrange("p a b -> p (a b)")
    q_all, k_all = flat(HQ, HH), flat(HF, HH)
    NL = len(LEVELS) + 1
    uses = [("gates", "act")] + [(("v", n), "act") for n in range(4)] + [(("diag", n), "dve") for n in range(4)]
    uses += [(("cross", n), "act") for n in range(2)]
    uses += [(("level", l, n), "dve") for l in range(1, NL) for n in range(4)]
    uses += [(("o", n), "act") for n in range(4)] + [(("ss", n), "act") for n in range(4)]
    with ExitStack() as ctx:
        banks = Banks(ctx, nc, uses)
        sem = lambda n: ctx.enter_context(nc.semaphore(n))
        sig_ready, f_ready, lf_ready, k_ready, diff_ready, exp_ready, prod_ready, a_ready, sq_ready, \
            rs_ready, silu_ready, first_tap = (sem(n) for n in (
                "sig_ready", "f_ready", "lf_ready", "k_ready", "diff_ready", "exp_ready", "prod_ready", "a_ready",
                "sq_ready", "rs_ready", "silu_ready", "first_tap"))
        b = ctx.enter_context(nc.sbuf_tensor("log_decay", [P, HH * SEQ], F32))
        X = ctx.enter_context(nc.sbuf_tensor("scaled", [P, 2, HH * SEQ], F32))
        A = ctx.enter_context(nc.sbuf_tensor("attn_t", [P, HH, 3, P], F32))
        tapped = ctx.enter_context(nc.sbuf_tensor("tapped", [P, HH, SEQ], F32))
        block = ctx.enter_context(nc.Block())

        def conv_weight(part, tap, j):
            column = C_CONV + tap * 3 * HH + part * HH + j
            return core.cols[:, column:column + 1]

        @block.gpsimd
        def _(pool):
            def products(part, tap, dst):
                back = 3 - tap
                for j in range(HH):
                    ins = nc.gpsimd.tensor_scalar(dst[:, j, back:SEQ], core.big[:, GQ + part * HH + j, 0:SEQ - back],
                                                  conv_weight(part, tap, j), None, ALU.mult)
                return ins

            for part in (0, 1):
                products(part, 3, conv[:, part * HH:(part + 1) * HH]).then_inc(first_tap, 1)
            v = conv[:, 2 * HH:3 * HH]
            core.pool.link(pool, products(2, 3, v))
            for tap in (2, 1, 0):
                back = 3 - tap
                core.pool.link(pool, products(2, tap, tapped))
                core.pool.link(pool, nc.gpsimd.tensor_tensor(v[:, :, back:SEQ], v[:, :, back:SEQ],
                                                             tapped[:, :, back:SEQ], ALU.add))

        @block.scalar
        def _(act):
            hf = flat(HF, HH)
            nc.scalar.activation(hf, hf, ACT.Sigmoid).then_inc(sig_ready, 1)
            for g in (HG, GG):
                nc.scalar.activation(flat(g, HH), flat(g, HH), ACT.Silu).then_inc(silu_ready, 1)
            banks.wait_filled(act, "gates")
            nc.scalar.activation(core.gates[:, 0:2 * SEQ], ps[0:HH, banks.bank("gates"), :], ACT.Copy
                                 ).then_inc(banks.emptied["act"], 1)
            act.wait_ge(f_ready, 1)
            nc.scalar.activation(X[:, 1, :], X[:, 0, :], ACT.Ln).then_inc(lf_ready, 1)
            for n in range(4):
                banks.wait_filled(act, ("v", n))
                nc.scalar.activation(big[:, HI + 2 * n:HI + 2 * n + 2, :], ps[:, banks.bank(("v", n)), :], ACT.Copy
                                     ).then_inc(banks.emptied["act"], 1)
            for l in range(NL):
                act.wait_ge(diff_ready, l + 1)
                nc.scalar.activation(X[:, l % 2, :], X[:, l % 2, :], ACT.Exp).then_inc(exp_ready, 1)
                if l == 1:
                    for n in range(2):
                        banks.wait_filled(act, ("cross", n))
                        nc.scalar.activation(A[:, 4 * n:4 * n + 4, 2, :],
                                             ps[:, banks.bank(("cross", n)), :].rearrange("p (h t) -> p h t", h=4),
                                             ACT.Copy).then_inc(banks.emptied["act"], 1)
            for n in range(4):
                banks.wait_filled(act, ("o", n))
                pso = ps[:, banks.bank(("o", n)), :]
                nc.scalar.activation(X[:, 0, 512 * n:512 * n + 512], pso, ACT.Square).then_inc(sq_ready, 1)
                nc.scalar.activation(core.hT[:, 2 * n:2 * n + 2, :], pso, ACT.Copy
                                     ).then_inc(banks.emptied["act"], 1)
            for n in range(4):
                banks.wait_filled(act, ("ss", n))
                core.act.link(act, nc.scalar.activation(X[:, 1, 512 * n:512 * n + 512],
                                                        ps[:, banks.bank(("ss", n)), :], ACT.Ln,
                                                        bias=core.eps[:], scale=1.0 / P))
            nc.scalar.activation(X[:, 1, :], X[:, 1, :], ACT.Exp, scale=-0.5).then_inc(rs_ready, 1)

        @block.tensor
        def _(pe):
            bank = banks.bank("gates")
            for m in range(2):
                for k in range(KT):
                    ins = nc.tensor.matmul(ps[0:HH, bank, m * SEQ:(m + 1) * SEQ],
                                           core.w_gates[:, k, m * HH:(m + 1) * HH],
                                           core.hT[:, k, :], start=(k == 0), stop=(k == KT - 1))
            ins.then_inc(banks.filled, 1)
            for n in range(4):
                for j in range(4):
                    ins = nc.tensor.transpose(ps[:, banks.bank(("v", n)), j * P:(j + 1) * P],
                                              big[:, HI + 2 * n + j // 2, (j % 2) * P:(j % 2 + 1) * P], core.ident[:])
                ins.then_inc(banks.filled, 1)
            pe.wait_ge(k_ready, 1)
            for n in range(4):
                banks.wait_empty(pe, ("diag", n))
                for j in range(4):
                    at = n * 512 + j * P
                    ins = nc.tensor.matmul(ps[:, banks.bank(("diag", n)), j * P:(j + 1) * P], k_all[:, at:at + P],
                                           q_all[:, at:at + P], start=True, stop=True)
                ins.then_inc(banks.filled, 1)
            for l in range(NL):
                pe.wait_ge(prod_ready, l + 1)
                if l == 0:
                    for n in range(2):
                        banks.wait_empty(pe, ("cross", n))
                        for j in range(4):
                            at = (4 * n + j) * SEQ
                            ins = nc.tensor.matmul(ps[:, banks.bank(("cross", n)), j * P:(j + 1) * P],
                                                   X[:, 0, at:at + P], X[:, 0, at + P:at + SEQ],
                                                   start=True, stop=True)
                        ins.then_inc(banks.filled, 1)
                else:
                    for n in range(4):
                        banks.wait_empty(pe, ("level", l, n))
                        for j in range(4):
                            at = n * 512 + j * P
                            ins = nc.tensor.matmul(ps[:, banks.bank(("level", l, n)), j * P:(j + 1) * P],
                                                   X[:, l % 2, at:at + P], X[:, l % 2, at:at + P],
                                                   start=True, stop=True)
                        ins.then_inc(banks.filled, 1)
            pe.wait_ge(banks.emptied["act"], 7)
            pe.wait_ge(a_ready, 1)
            for n in range(4):
                banks.wait_empty(pe, ("o", n))
                for j in range(2):
                    h = 2 * n + j
                    out = ps[:, banks.bank(("o", n)), j * SEQ:(j + 1) * SEQ]
                    v0, v1 = big[:, HI + h, 0:P], big[:, HI + h, P:SEQ]
                    nc.tensor.matmul(out[:, 0:P], v0, A[:, h, 0, :], start=True, stop=True)
                    nc.tensor.matmul(out[:, P:SEQ], v0, A[:, h, 2, :], start=True, stop=False)
                    ins = nc.tensor.matmul(out[:, P:SEQ], v1, A[:, h, 1, :], start=False, stop=True)
                ins.then_inc(banks.filled, 1)
            for n in range(4):
                banks.wait_empty(pe, ("ss", n))
                pe.wait_ge(sq_ready, n + 1)
                nc.tensor.matmul(ps[:, banks.bank(("ss", n)), :], core.ones[:], X[:, 0, 512 * n:512 * n + 512],
                                 start=True, stop=True).then_inc(banks.filled, 1)

        @block.vector
        def _(dve):
            v = core.dve

            def convolve(part):
                dve.wait_ge(first_tap, part + 1)
                for tap in (2, 1, 0):
                    back = 3 - tap
                    for j in range(HH):
                        dst = conv[:, part * HH + j, back:SEQ]
                        ins = nc.vector.scalar_tensor_tensor(
                            out=dst, in0=core.big[:, GQ + part * HH + j, 0:SEQ - back],
                            scalar=conv_weight(part, tap, j), in1=dst, op0=ALU.mult, op1=ALU.add)
                    v.link(dve, ins)

            dve.wait_ge(sig_ready, 1)
            for h in range(HH):
                ins = nc.vector.tensor_scalar(X[:, 0, h * SEQ:(h + 1) * SEQ], big[:, HF + h, :], core.lb[:, 1, h:h + 1],
                                              core.lb[:, 0, h:h + 1], ALU.mult, ALU.add)
            ins.then_inc(f_ready, 1)
            dve.wait_ge(f_ready, 1)
            nc.vector.tensor_scalar(k_all, X[:, 0, :], -1.0, 1.0, ALU.mult, ALU.add).then_inc(k_ready, 1)
            convolve(0)
            dve.wait_ge(lf_ready, 1)
            for h in range(HH):
                ins = nc.vector.tensor_tensor_scan(b[:, h * SEQ:(h + 1) * SEQ], core.keep[:],
                                                   X[:, 1, h * SEQ:(h + 1) * SEQ], 0.0, ALU.mult, ALU.add)
            v.link(dve, ins)

            def halves(a, L):
                w = a.rearrange("p (n two l) -> p n two l", two=2, l=L)
                return w[:, :, 0, :], w[:, :, 1, :]

            def level_L(l):
                return P if l == 0 else LEVELS[l - 1]

            def diffs(l):
                L = level_L(l)
                if l >= 2:
                    banks.wait_filled(dve, ("cross", 1) if l == 2 else ("level", l - 2, 3))
                b0, b1 = halves(b[:], L)
                x0, x1 = halves(X[:, l % 2, :], L)
                ref = b0[:, :, L - 1:L].to_broadcast(list(b0.shape))
                nc.vector.tensor_tensor(x0, ref, b0, ALU.subtract)
                if l == 0:
                    nc.vector.tensor_copy(x1, b1).then_inc(diff_ready, 1)
                else:
                    nc.vector.tensor_tensor(x1, b1, ref, ALU.subtract).then_inc(diff_ready, 1)

            def products(l):
                L = level_L(l)
                x0, x1 = halves(X[:, l % 2, :], L)
                k0, _ = halves(k_all, L)
                _, q1 = halves(q_all, L)
                dve.wait_ge(exp_ready, l + 1)
                nc.vector.tensor_tensor(x0, x0, k0, ALU.mult)
                nc.vector.tensor_tensor(x1, x1, q1, ALU.mult).then_inc(prod_ready, 1)

            def take(l):
                for n in range(4):
                    banks.wait_filled(dve, ("level", l, n))
                    nc.vector.copy_predicated(
                        A[:, 2 * n:2 * n + 2, 0:2, :],
                        bcast(bcast(core.up_mask[:, l - 1, :].bitcast(I32), 2), 2),
                        ps[:, banks.bank(("level", l, n)), :].rearrange("p (h c t) -> p h c t", h=2, c=2)
                    ).then_inc(banks.emptied["dve"], 1)

            diffs(0)
            for n in range(4):
                banks.wait_filled(dve, ("diag", n))
                nc.vector.tensor_tensor(A[:, 2 * n:2 * n + 2, 0:2, :],
                                        ps[:, banks.bank(("diag", n)), :].rearrange("p (h c t) -> p h c t", h=2, c=2),
                                        bcast(bcast(core.ident[:], 2), 2), ALU.mult
                                        ).then_inc(banks.emptied["dve"], 1)
            dve.wait_ge(banks.emptied["dve"], 4)
            for l in range(NL):
                if l + 1 < NL:
                    diffs(l + 1)
                products(l)
                if l >= 2:
                    if l >= 3:
                        dve.wait_ge(banks.emptied["dve"], 4 + 4 * (l - 2))
                    take(l - 1)
            dve.wait_ge(banks.emptied["dve"], 4 + 4 * (NL - 2))
            take(NL - 1)
            dve.wait_ge(banks.emptied["dve"], 4 + 4 * (NL - 1))
            dve.sem_inc(a_ready, 1)
            convolve(1)
            dve.wait_ge(silu_ready, 1)
            dve.wait_ge(rs_ready, 1)
            o = core.hT[:, 0:HH, :].rearrange("p a b -> p (a b)")
            v.link(dve, nc.vector.scalar_tensor_tensor(out=o, in0=o, scalar=core.cols[:, C_HGNORM:C_HGNORM + 1],
                                                       in1=X[:, 1, :], op0=ALU.mult, op1=ALU.mult))
            v.link(dve, nc.vector.tensor_tensor(o, o, flat(HG, HH), ALU.mult))



def phase_gdn(nc, core, conv):
    big, ps = core.big, core.ps
    flat = lambda a, n: big[:, a:a + n, :].rearrange("p a b -> p (a b)")
    blocks = lambda a: flat(a, HH).rearrange("p (n t) -> p n t", t=P)
    q_all, k_all = flat(GQ, HH), flat(GK, HH)
    inv_levels = list(reversed(LEVELS))[1:]
    NI = len(inv_levels)
    uses = [(("ssq", n), "act") for n in range(8)] + [("columns", "dve")]
    uses += [(("rows", h), "act") for h in range(HH)] + [(("v", n), "act") for n in range(4)]
    uses += [(("kt", n), "dve") for n in range(2)]
    uses += [(("qk", n), "dve") for n in range(4)] + [(("kk", n), "dve") for n in range(4)]
    uses += [(("nt", n), "dve") for n in range(4)]
    for l in range(NI):
        uses += [(("p", l, n), "act") for n in range(4)]
        for n in range(4):
            uses += [(("d", l, n), "dve")] if l < NI - 1 else []
            uses += [(("dt", l, n), "dve")]
    uses += [(("vn0", n), "act") for n in range(2)] + [(("s", n), "act") for n in range(2)]
    uses += [(("ks", n), "dve") for n in range(2)] + [(("vn1", n), "act") for n in range(2)]
    uses += [(("o", n), "act") for n in range(4)] + [(("ss", n), "act") for n in range(4)]
    with ExitStack() as ctx:
        banks = Banks(ctx, nc, uses)
        sem = lambda n: ctx.enter_context(nc.semaphore(n))
        conv_act, squares, norm_rs, qk_normed, sp_b, z_ready, g_ready, eg_ready, \
            g1_ready, g1_exp, nt_ready, tu_ready, r0_ready, eg_bc, qd_ready, sq_ready, \
            rs_ready, r1_ready, qkm_ready = (sem(n) for n in (
                "conv_act", "squares", "norm_rs", "qk_normed", "sp_b", "z_ready",
                "g_ready", "eg_ready", "g1_ready", "g1_exp", "nt_ready", "tu_ready", "r0_ready",
                "eg_bc", "qd_ready", "sq_ready", "rs_ready", "r1_ready", "qkm_ready"))
        W = ctx.enter_context(nc.sbuf_tensor("gdn_work", [P, 5, HH * SEQ], F32))
        G1, QK, NT_, GB, BB = (W[:, n, :] for n in range(5))
        rows = ctx.enter_context(nc.sbuf_tensor("gdn_rows", [HH, 6, SEQ], F32))
        pc = ctx.enter_context(nc.sbuf_tensor("gdn_token_cols", [P, 8, HH], F32))
        C0, C1, C2, C3 = 0, 8, 16, 24
        T, U, P1 = blocks(C0), blocks(C1), blocks(C2)
        KTOK, QD = blocks(C3)[:, 0:HH, :], blocks(C3)[:, HH:2 * HH, :]
        R, VN = blocks(C0), blocks(C2)
        S = G1.rearrange("p (n t) -> p n t", t=P)[:, 0:HH, :]
        block = ctx.enter_context(nc.Block())
        quad = lambda a, n: a[:, 4 * n:4 * n + 4, :]
        quad_ps = lambda name: ps[:, banks.bank(name), :].rearrange("p (n t) -> p n t", t=P)
        as_blocks = lambda a: a.rearrange("p (n t) -> p n t", t=P)

        @block.scalar
        def _(act):
            a = core.act
            gates = core.gates
            a.link(act, nc.scalar.activation(rows[:, 1, :], gates[:, SEQ:2 * SEQ], ACT.Sigmoid))
            for part in range(3):
                nc.scalar.activation(flat(GQ + part * HH, HH),
                                     conv[:, part * HH:(part + 1) * HH, :].rearrange("p a b -> p (a b)"), ACT.Silu
                                     ).then_inc(conv_act, 1)
            act.wait_ge(conv_act, 2)
            for part, sq in ((0, G1), (1, QK)):
                nc.scalar.activation(sq, flat(GQ + part * HH, HH), ACT.Square).then_inc(squares, 1)
            act.wait_ge(z_ready, 1)
            a.link(act, nc.scalar.activation(rows[:, 4, :], rows[:, 4, :], ACT.Exp))
            nc.scalar.activation(rows[:, 4, :], rows[:, 4, :], ACT.Ln, bias=core.one[0:HH, :]).then_inc(sp_b, 1)
            for n in range(8):
                banks.wait_filled(act, ("ssq", n))
                dst = (NT_ if n < 4 else GB)[:, 512 * (n % 4):512 * (n % 4) + 512]
                nc.scalar.activation(dst, ps[:, banks.bank(("ssq", n)), :], ACT.Ln, bias=core.eps[:]
                                     ).then_inc(banks.emptied["act"], 1)
            act.wait_ge(banks.emptied["act"], 8)
            nc.scalar.activation(NT_, NT_, ACT.Exp, scale=-0.5).then_inc(norm_rs, 1)
            nc.scalar.activation(GB, GB, ACT.Exp, scale=-0.5).then_inc(norm_rs, 1)
            act.wait_ge(g_ready, 1)
            nc.scalar.activation(rows[:, 2, :], rows[:, 0, :], ACT.Exp).then_inc(eg_ready, 1)
            nc.scalar.activation(rows[:, 3, 0:P], rows[:, 0, 0:P], ACT.Exp, scale=-1.0, bias=rows[:, 0, P - 1:P]
                                 ).then_inc(eg_ready, 1)
            act.wait_ge(qk_normed, 1)
            for h in range(HH):
                banks.wait_filled(act, ("rows", h))
                nc.scalar.activation(W[:, 3:5, h * SEQ:(h + 1) * SEQ],
                                     ps[:, banks.bank(("rows", h)), :].rearrange("p (a t) -> p a t", a=2), ACT.Copy
                                     ).then_inc(banks.emptied["act"], 1)
            for n in range(4):
                banks.wait_filled(act, ("v", n))
                nc.scalar.activation(big[:, GV + 2 * n:GV + 2 * n + 2, :], ps[:, banks.bank(("v", n)), :], ACT.Copy
                                     ).then_inc(banks.emptied["act"], 1)
            act.wait_ge(g1_ready, 1)
            nc.scalar.activation(G1, G1, ACT.Exp).then_inc(g1_exp, 1)
            nc.scalar.activation(GB, GB, ACT.Exp).then_inc(eg_bc, 1)
            for l in range(NI):
                for n in range(4):
                    banks.wait_filled(act, ("p", l, n))
                    nc.scalar.activation(quad(P1, n), quad_ps(("p", l, n)), ACT.Copy
                                         ).then_inc(banks.emptied["act"], 1)
            for name, dst in (("vn0", VN[:, 0:HH, :]), ("s", S), ("vn1", VN[:, HH:2 * HH, :])):
                for n in range(2):
                    banks.wait_filled(act, (name, n))
                    nc.scalar.activation(dst[:, 4 * n:4 * n + 4, :], quad_ps((name, n)), ACT.Copy
                                         ).then_inc(banks.emptied["act"], 1)
            for n in range(4):
                banks.wait_filled(act, ("o", n))
                pso = ps[:, banks.bank(("o", n)), :]
                nc.scalar.activation(BB[:, 512 * n:512 * n + 512], pso, ACT.Square).then_inc(sq_ready, 1)
                nc.scalar.activation(core.hT[:, HH + 2 * n:HH + 2 * n + 2, :], pso, ACT.Copy
                                     ).then_inc(banks.emptied["act"], 1)
            for n in range(4):
                banks.wait_filled(act, ("ss", n))
                a.link(act, nc.scalar.activation(GB[:, 512 * n:512 * n + 512], ps[:, banks.bank(("ss", n)), :],
                                                 ACT.Ln, bias=core.eps[:], scale=1.0 / P))
            nc.scalar.activation(GB, GB, ACT.Exp, scale=-0.5).then_inc(rs_ready, 1)

        n_act = {name: banks.order[banks.at[name]][1] for name, e in uses if e == "act"}
        n_dve = {name: banks.order[banks.at[name]][1] for name, e in uses if e == "dve"}

        @block.tensor
        def _(pe):
            def fill(name, parts):
                banks.wait_empty(pe, name)
                for out, lhsT, rhs, start, stop in parts:
                    ins = nc.tensor.matmul(out, lhsT, rhs, start=start, stop=stop)
                ins.then_inc(banks.filled, 1)

            def fill_turned(name, sources):
                banks.wait_empty(pe, name)
                for j, s in enumerate(sources):
                    ins = nc.tensor.transpose(quad_ps(name)[:, j, :], s, core.ident[:])
                ins.then_inc(banks.filled, 1)

            for n in range(8):
                pe.wait_ge(squares, n // 4 + 1)
                sq = (G1 if n < 4 else QK)[:, 512 * (n % 4):512 * (n % 4) + 512]
                fill(("ssq", n), [(ps[:, banks.bank(("ssq", n)), :], core.ones[:], sq, True, True)])
            pe.wait_ge(eg_ready, 2)
            banks.wait_empty(pe, "columns")
            for j, (r, c) in enumerate(((0, 0), (0, 1), (1, 0), (1, 1), (2, 1), (3, 0))):
                ins = nc.tensor.transpose(ps[:, banks.bank("columns"), j * HH:(j + 1) * HH],
                                          rows[:, r, c * P:(c + 1) * P], core.ident[0:HH, 0:HH])
            ins.then_inc(banks.filled, 1)
            for h in range(HH):
                fill(("rows", h), [(ps[:, banks.bank(("rows", h)), :], core.pick[:, h, :],
                                    rows[:, 0:2, :].rearrange("p a t -> p (a t)"), True, True)])
            pe.wait_ge(conv_act, 3)
            for n in range(4):
                fill_turned(("v", n), [big[:, GV + 2 * n + j // 2, (j % 2) * P:(j % 2 + 1) * P] for j in range(4)])
            pe.wait_ge(qk_normed, 1)
            for n in range(2):
                fill_turned(("kt", n), [big[:, GK + 4 * n + j, 0:P] for j in range(4)])
            for name, rhs in (("qk", q_all), ("kk", k_all)):
                for n in range(4):
                    fill((name, n), [(quad_ps((name, n))[:, j, :], k_all[:, 512 * n + j * P:512 * n + (j + 1) * P],
                                      rhs[:, 512 * n + j * P:512 * n + (j + 1) * P], True, True) for j in range(4)])
            pe.wait_ge(nt_ready, 1)
            NTb = as_blocks(NT_)
            for n in range(4):
                fill_turned(("nt", n), [NTb[:, 4 * n + j, :] for j in range(4)])
            for l in range(NI):
                for n in range(4):
                    pe.wait_ge(tu_ready, 4 * l + n + 1)
                    fill(("p", l, n), [(quad_ps(("p", l, n))[:, j, :], NTb[:, 4 * n + j, :], T[:, 4 * n + j, :],
                                        True, True) for j in range(4)])
                for n in range(4):
                    pe.wait_ge(banks.emptied["act"], n_act[("p", l, n)])
                    if l < NI - 1:
                        fill(("d", l, n), [(quad_ps(("d", l, n))[:, j, :], U[:, 4 * n + j, :], P1[:, 4 * n + j, :],
                                            True, True) for j in range(4)])
                    fill(("dt", l, n), [(quad_ps(("dt", l, n))[:, j, :], P1[:, 4 * n + j, :], U[:, 4 * n + j, :],
                                         True, True) for j in range(4)])
            pe.wait_ge(tu_ready, 4 * NI + 4)
            pe.wait_ge(r0_ready, 1)
            for n in range(2):
                fill(("vn0", n), [(quad_ps(("vn0", n))[:, j, :], U[:, 2 * (4 * n + j), :], R[:, 4 * n + j, :],
                                   True, True) for j in range(4)])
            for n in range(2):
                pe.wait_ge(banks.emptied["act"], n_act[("vn0", n)])
                fill(("s", n), [(quad_ps(("s", n))[:, j, :], KTOK[:, 4 * n + j, :], VN[:, 4 * n + j, :],
                                 True, True) for j in range(4)])
            for n in range(2):
                pe.wait_ge(banks.emptied["act"], n_act[("s", n)])
                fill(("ks", n), [(quad_ps(("ks", n))[:, j, :], big[:, GK + 4 * n + j, P:SEQ], S[:, 4 * n + j, :],
                                  True, True) for j in range(4)])
            for n in range(2):
                pe.wait_ge(r1_ready, n + 1)
                fill(("vn1", n), [(quad_ps(("vn1", n))[:, j, :], U[:, 2 * (4 * n + j) + 1, :],
                                   R[:, HH + 4 * n + j, :], True, True) for j in range(4)])
            pe.wait_ge(qd_ready, 1)
            pe.wait_ge(qkm_ready, 1)
            QKb = as_blocks(QK)
            for n in range(4):
                pe.wait_ge(banks.emptied["act"], n_act[("vn1", n // 2)])
                parts = []
                for j in range(2):
                    h = 2 * n + j
                    out = ps[:, banks.bank(("o", n)), j * SEQ:(j + 1) * SEQ]
                    parts += [(out[:, 0:P], VN[:, h, :], QKb[:, 2 * h, :], True, True),
                              (out[:, P:SEQ], S[:, h, :], QD[:, h, :], True, False),
                              (out[:, P:SEQ], VN[:, HH + h, :], QKb[:, 2 * h + 1, :], False, True)]
                fill(("o", n), parts)
            for n in range(4):
                pe.wait_ge(sq_ready, n + 1)
                fill(("ss", n), [(ps[:, banks.bank(("ss", n)), :], core.ones[:], BB[:, 512 * n:512 * n + 512],
                                  True, True)])

        @block.vector
        def _(dve):
            v = core.dve
            v.link(dve, nc.vector.tensor_scalar(rows[:, 5, :], core.gates[:, 0:SEQ], core.gdn_cols[:, 1:2], None,
                                                ALU.add))
            v.link(dve, nc.vector.tensor_scalar(rows[:, 4, :], rows[:, 5, :], -1.0, None, ALU.mult))
            nc.vector.tensor_tensor(rows[:, 4, :], rows[:, 4, :], rows[:, 5, :], ALU.min).then_inc(z_ready, 1)
            dve.wait_ge(sp_b, 1)
            v.link(dve, nc.vector.scalar_tensor_tensor(out=rows[:, 4, :], in0=rows[:, 5, :], scalar=0.0,
                                                       in1=rows[:, 4, :], op0=ALU.max, op1=ALU.add))
            v.link(dve, nc.vector.tensor_scalar(rows[:, 4, :], rows[:, 4, :], core.gdn_cols[:, 3:4], None, ALU.mult))
            nc.vector.tensor_tensor_scan(rows[:, 0, :], core.keep[0:HH, :], rows[:, 4, :], 0.0, ALU.mult, ALU.add
                                         ).then_inc(g_ready, 1)
            dve.wait_ge(norm_rs, 2)
            nc.vector.scalar_tensor_tensor(out=q_all, in0=q_all, scalar=float(P) ** -0.5, in1=NT_, op0=ALU.mult,
                                           op1=ALU.mult)
            nc.vector.tensor_tensor(k_all, k_all, GB, ALU.mult).then_inc(qk_normed, 1)
            banks.wait_filled(dve, "columns")
            nc.vector.tensor_copy(pc[:, 0:6, :], ps[:, banks.bank("columns"), 0:6 * HH].rearrange(
                "p (a h) -> p a h", a=6)).then_inc(banks.emptied["dve"], 1)
            dve.wait_ge(banks.emptied["dve"], 1)
            nc.vector.scalar_tensor_tensor(out=pc[:, 6, :], in0=pc[:, 3, :], scalar=-1.0, in1=pc[:, 4, :],
                                           op0=ALU.mult, op1=ALU.mult)
            dve.wait_ge(banks.emptied["act"], n_act[("rows", HH - 1)])
            for h in range(HH):
                for c in range(2):
                    at = h * SEQ + c * P
                    ins = nc.vector.tensor_scalar(G1[:, at:at + P], GB[:, at:at + P], pc[:, c, h:h + 1], 0.0,
                                                  ALU.subtract, ALU.min)
            ins.then_inc(g1_ready, 1)
            for n in range(2):
                banks.wait_filled(dve, ("kt", n))
                for j in range(4):
                    ins = nc.vector.tensor_scalar(KTOK[:, 4 * n + j, :], quad_ps(("kt", n))[:, j, :],
                                                  pc[:, 5, 4 * n + j:4 * n + j + 1], None, ALU.mult)
                ins.then_inc(banks.emptied["dve"], 1)
            dve.wait_ge(g1_exp, 1)
            for name, dst in (("qk", QK), ("kk", NT_)):
                for n in range(4):
                    banks.wait_filled(dve, (name, n))
                    nc.vector.tensor_tensor(dst[:, 512 * n:512 * n + 512], ps[:, banks.bank((name, n)), :],
                                            G1[:, 512 * n:512 * n + 512], ALU.mult).then_inc(banks.emptied["dve"], 1)
            dve.wait_ge(banks.emptied["dve"], n_dve[("kk", 3)])
            v.link(dve, nc.vector.tensor_tensor(NT_, NT_, BB, ALU.mult))
            nc.vector.scalar_tensor_tensor(out=as_blocks(NT_), in0=as_blocks(NT_), scalar=-1.0,
                                           in1=bcast(core.strict[:], 2 * HH), op0=ALU.mult, op1=ALU.mult
                                           ).then_inc(nt_ready, 1)
            nc.vector.tensor_copy(T, bcast(core.ident[:], 2 * HH))
            v.mark(nc.vector.tensor_copy(U, bcast(core.ident[:], 2 * HH)))
            nc.vector.tensor_tensor(as_blocks(QK), as_blocks(QK), bcast(core.incl[:], 2 * HH), ALU.mult
                                    ).then_inc(qkm_ready, 1)
            dve.wait_ge(nt_ready, 1)
            dve.wait_ge(v.sem, v.n)
            for n in range(4):
                banks.wait_filled(dve, ("nt", n))
                nc.vector.copy_predicated(quad(T, n), bcast(core.low_mask[:, len(LEVELS) - 1, :].bitcast(I32), 4),
                                          quad_ps(("nt", n))).then_inc(banks.emptied["dve"], 1)
                nc.vector.copy_predicated(quad(U, n), bcast(core.up_mask[:, len(LEVELS) - 1, :].bitcast(I32), 4),
                                          quad(as_blocks(NT_), n)).then_inc(tu_ready, 1)
            dve.wait_ge(eg_bc, 1)
            nc.vector.tensor_tensor(QD, big[:, GQ:GQ + HH, P:SEQ],
                                    GB.rearrange("p (h t) -> p h t", t=SEQ)[:, :, P:SEQ], ALU.mult
                                    ).then_inc(qd_ready, 1)
            for l, L in enumerate(inv_levels):
                m = LEVELS.index(L)
                for n in range(4):
                    dve.wait_ge(tu_ready, 4 * l + n + 1)
                    if l < NI - 1:
                        banks.wait_filled(dve, ("d", l, n))
                        nc.vector.copy_predicated(quad(T, n), bcast(core.low_mask[:, m, :].bitcast(I32), 4),
                                                  quad_ps(("d", l, n))).then_inc(banks.emptied["dve"], 1)
                    banks.wait_filled(dve, ("dt", l, n))
                    nc.vector.copy_predicated(quad(U, n), bcast(core.up_mask[:, m, :].bitcast(I32), 4),
                                              quad_ps(("dt", l, n))).then_inc(banks.emptied["dve"], 1)
                    dve.wait_ge(banks.emptied["dve"], n_dve[("dt", l, n)])
                    dve.sem_inc(tu_ready, 1)
            dve.wait_ge(banks.emptied["act"], n_act[("v", 3)])
            for c in range(2):
                for h in range(HH):
                    ins = nc.vector.tensor_scalar(R[:, c * HH + h, :], big[:, GV + h, c * P:(c + 1) * P],
                                                  pc[:, 2 + c, h:h + 1], None, ALU.mult)
            ins.then_inc(r0_ready, 1)
            dve.wait_ge(r0_ready, 1)
            for n in range(2):
                banks.wait_filled(dve, ("ks", n))
                for j in range(4):
                    h = 4 * n + j
                    ins = nc.vector.scalar_tensor_tensor(out=R[:, HH + h, :], in0=quad_ps(("ks", n))[:, j, :],
                                                         scalar=pc[:, 6, h:h + 1], in1=R[:, HH + h, :],
                                                         op0=ALU.mult, op1=ALU.add)
                ins.then_inc(banks.emptied["dve"], 1)
                dve.wait_ge(banks.emptied["dve"], n_dve[("ks", n)])
                dve.sem_inc(r1_ready, 1)
            dve.wait_ge(rs_ready, 1)
            o = core.hT[:, HH:2 * HH, :].rearrange("p a b -> p (a b)")
            v.link(dve, nc.vector.scalar_tensor_tensor(out=o, in0=o, scalar=core.cols[:, C_GDNNORM:C_GDNNORM + 1],
                                                       in1=GB, op0=ALU.mult, op1=ALU.mult))
            v.link(dve, nc.vector.tensor_tensor(o, o, flat(GG, HH), ALU.mult))



def phase_swiglu(nc, core):
    f0 = list(core.claimed)
    with ExitStack() as ctx:
        gate = ctx.enter_context(nc.sbuf_tensor("gate", [P, NT, SEQ], F32))

        def silu(act, i, nt, acc):
            act.wait_ge(core.free[1], i * NT + (f0[1] + nt + 1))
            return nc.scalar.activation(gate[:, nt, :], acc, ACT.Silu)

        def multiply(dve, i, tile, acc):
            nt = tile - NT
            dve.wait_ge(core.free[0], i * NT + (f0[0] + NT + nt + 1))
            return nc.vector.tensor_tensor(core.big[:, bass.ds(i * NT + nt, 1), :], acc.unsqueeze(1),
                                           gate[:, nt, :].unsqueeze(1), ALU.mult)

        phase_split_product(nc, core, "gate_up", "down", [("act", silu), ("dve", multiply)])


def phase_write_out(nc, core, out):
    y = core.big[:, 0:16, :].rearrange("p a b -> p (a b)").rearrange("p (t f) -> p t f", t=TT)
    with ExitStack() as ctx:
        turned, copied, stored = (ctx.enter_context(nc.semaphore(n)) for n in ("turned", "copied", "stored"))
        block = ctx.enter_context(nc.Block())

        @block.tensor
        def _(pe):
            for n in range(8):
                for j in range(4):
                    ins = nc.tensor.transpose(core.ps[:, n, j * P:(j + 1) * P],
                                              core.hT[:, 4 * (n % 4) + j, (n // 4) * P:(n // 4 + 1) * P],
                                              core.ident[:])
                ins.then_inc(turned, 1)

        @block.scalar
        def _(act):
            for n in range(8):
                act.wait_ge(turned, n + 1)
                nc.scalar.activation(y[:, n // 4, 512 * (n % 4):512 * (n % 4) + 512], core.ps[:, n, :], ACT.Copy
                                     ).then_inc(copied, 1)

        @block.sync
        def _(sp):
            rows = out[0].rearrange("(t p) f -> p t f", p=P)
            for n in range(4):
                sp.wait_ge(copied, 2 * n + 2)
                t, f = n // 2, 1024 * (n % 2)
                sp.dma_start(rows[:, t, f:f + 1024], y[:, t, f:f + 1024]).then_inc(stored, 16)
            sp.wait_ge(stored, 64)



HD = 64
FOX, NSA, DIL, DIFF, GROUPS = 7, 8, 9, 4, 2
N_CMP = SEQ // 16 - 1
FAR = 1.0e32
LAM_INIT = 0.8 - 0.6
SCALE = HD ** -0.5

T_FOXQ, T_FOXK, T_NSAQ, T_CMPK, T_CMPV, T_SLCK, T_WINK, T_DILQ, T_DILK, T_DIFFQ, T_DIFFK = (
    0, 4, 8, 12, 13, 14, 15, 16, 21, 26, 30)
T_TOKENS, T_FOXROW = 34, 49
V_FOX, V_SLC, V_WIN, V_DIL, V_DIFF, V_FOXF, V_GATE = 0, 448, 576, 704, 1280, 1792, 1799

def _features(tile, widths, scale=1.0, at=0):
    return [("f", at + P * n, w, tile + n, scale) for n, w in enumerate(widths)]


def _stationary(chunk_width, at, width):
    start = at if at + P <= chunk_width else at + width - P
    return start, at - start


IN_2 = [
    (0, 448, _features(T_FOXQ, [128, 128, 128, 64], SCALE)),
    (448, 448, _features(T_FOXK, [128, 128, 128, 64])),
    (896, 456, [("t", 0, 456, [(0, 448, V_FOX), (448, 7, V_FOXF)])]),
    (1351, 512, [("pair", P * n, P, n, SCALE) for n in range(4)]),
    (1863, 384, _features(T_CMPK, [128, 128, 128])),
    (2247, 408, [("t", 0, 408, [(0, 128, V_SLC), (256, 128, V_WIN), (384, 24, V_GATE)]),
                 ("f", 128, 128, T_WINK, 1.0)]),
    (2655, 512, _features(T_DILQ, [128] * 4, SCALE)),
    (3167, 448, [("f", 0, 64, T_DILQ + 4, SCALE)] + _features(T_DILK, [128] * 3, at=64)),
    (3615, 448, _features(T_DILK + 3, [128, 64]) + [("t", 192, 256, [(0, 256, V_DIL)])]),
    (4063, 320, [("t", 0, 320, [(0, 320, V_DIL + 256)])]),
    (4383, 512, _features(T_DIFFQ, [128] * 4, SCALE)),
    (4895, 512, _features(T_DIFFK, [128] * 4)),
    (5407, 256, [("t", 0, 256, [(0, 256, V_DIFF)])]),
    (5663, 256, [("t", 0, 256, [(0, 256, V_DIFF + 256)])]),
]


def in_2_source(w):
    v = w.rearrange("(g k p) n -> p g k n", p=P, k=KG)

    def source(i, q):
        at, width, _ = IN_2[2 * i + q // 4]
        return v[:, q % 4, :, at:at + width]
    return source


def tokens(core):
    return core.big[:, T_TOKENS:T_TOKENS + 15, :].rearrange("p a b -> p (a b)").rearrange(
        "p (t c) -> p t c", t=TT)


def phase_in_2(nc, core, mix, t):
    st = core.streams["in_2"]
    f0, g0 = list(core.claimed), core.split_groups
    tok = tokens(core)

    def row_tile(c, kg, k):
        return KG * (g0 + 4 * c + kg) + k

    with ExitStack() as ctx:
        x = ctx.enter_context(nc.sbuf_tensor("in_2_h_parts", [P, KG, 2, SEQ], F32R))
        w = ctx.enter_context(nc.sbuf_tensor("in_2_weight_parts", [P, KG, 2, CW], F32R))
        iota_done, dist_f, causal_done = (ctx.enter_context(nc.semaphore(n)) for n in
                                                    ("iota_done", "dist_f", "causal_done"))
        disti = mix.PT[:, 0, 0:2, 0:SEQ].bitcast(I32)
        odd = mix.PT[:, 0, 2:4, 0:SEQ].bitcast(I32)
        far = mix.PT[:, 1, 0:2, 0:SEQ]
        cmpi = mix.PT[:, 1, 2, 0:TT * N_CMP].rearrange("p (t c) -> p t c", t=TT).bitcast(I32)
        block = ctx.enter_context(nc.Block())

        @block.sync
        def _(sp):
            for g in range(RING, st.groups):
                refill(sp, core, st, g // TURN, g % TURN)
            prefetch(sp, core, core.streams["out_2"])

        @block.tensor
        def _(pe):
            for c, (_, chunk_width, pieces) in enumerate(IN_2):
                half = c % 2
                pe.wait_ge(core.free[half], f0[half] + NT * (c // 2 + 1))
                for kt in range(KT):
                    kg, k = kt // KG, kt % KG
                    if k < KG - 1:
                        pe.wait_ge(core.low_ready, (KG - 1) * (g0 + 4 * c + kg) + k + 1)
                    else:
                        pe.wait_ge(core.used, st.first + 4 * c + kg + 1)
                    bank = NT * half
                    for kind, at, width, *_ in pieces:
                        for part in range(TT if kind == "t" else 1):
                            if kind == "t":
                                out = core.ps[:, bank, 0:width]
                                stationary, moving = x[:, k, :, part * P:(part + 1) * P], w[:, k, :, at:at + width]
                            else:
                                out = core.ps[:, bank, 0:SEQ]
                                start, _ = _stationary(chunk_width, at, width)
                                stationary, moving = w[:, k, :, start:start + P], x[:, k]
                            for n, (a, b) in enumerate(((1, 0), (0, 1), (0, 0))):
                                ins = nc.tensor.matmul(out, stationary[:, a], moving[:, b],
                                                       start=(kt == 0 and n == 0), stop=(kt == KT - 1 and n == 2))
                            bank += 1
                    ins.then_inc(core.parts_used, 1)

        @block.scalar
        def _(act):
            for g in range(GROUPS):
                rows = slice(g * HD, (g + 1) * HD)
                for a in range(2):
                    src = t["nsa_cmp_w1_2"][0, a].rearrange("(l d) o -> d l o", d=HD)
                    act.dma_start(mix.W1[rows, a], src).then_inc(mix.w_in, 16)
            for a in range(2):
                for g in range(GROUPS):
                    act.dma_start(mix.W2[0:HD, a, g * HD:(g + 1) * HD], t["nsa_cmp_w2_2"][0, a]
                                  ).then_inc(mix.w_in, 16)
            act.dma_start(mix.lam_rows[:], t["diff_lambda_2"].rearrange("l a d -> l (a d)")).then_inc(mix.w_in, 16)
            with nc.allow_non_contiguous_dma("seven numbers, one a partition"):
                act.dma_start(mix.fox_bias[:], t["fox_f_bias_2"].rearrange("l h -> h l")).then_inc(mix.w_in, 16)

            def high(c, kg):
                g = st.first + 4 * c + kg
                width = IN_2[c][1]
                act.wait_ge(core.landed[g % RING], 16 * (g // RING + 1))
                for k in range(KG):
                    act.wait_ge(core.parts_used, row_tile(c, kg, k) - (KG - 1))
                    nc.scalar.activation(x[:, k, 0, :], core.hT[:, KG * kg + k, :], ACT.Copy)
                    nc.scalar.activation(w[:, k, 0, 0:width], core.ring[:, g % RING, k, 0:width], ACT.Copy
                                         ).then_inc(core.high_ready, 1)

            def empty(c):
                half = c % 2
                bank = NT * half
                _, chunk_width, pieces = IN_2[c]
                act.wait_ge(core.parts_used, row_tile(c + 1, 0, 0))
                for kind, at, width, *rest in pieces:
                    if kind == "t":
                        for part in range(TT):
                            for col, n, dst in rest[0]:
                                ins = nc.scalar.activation(tok[:, part, dst:dst + n],
                                                           core.ps[:, bank, col:col + n], ACT.Copy)
                            bank += 1
                    elif kind == "pair":
                        for h in range(2 * rest[0], 2 * rest[0] + 2):
                            r, g = h % 2 * HD, h // (NSA // GROUPS) * HD
                            ins = nc.scalar.activation(core.big[g:g + HD, T_NSAQ + h % 4, :],
                                                       core.ps[r:r + HD, bank, 0:SEQ], ACT.Copy, scale=rest[1])
                        bank += 1
                    else:
                        tile, scale = rest
                        _, row = _stationary(chunk_width, at, width)
                        ins = nc.scalar.activation(core.big[0:width, tile, :], core.ps[row:row + width, bank, 0:SEQ],
                                                   ACT.Copy, scale=scale)
                        bank += 1
                ins.then_inc(core.free[half], NT)

            for c in range(len(IN_2)):
                for kg in range(4):
                    high(c, kg)
                    if c and kg == 0:
                        empty(c - 1)
            empty(len(IN_2) - 1)

        @block.gpsimd
        def _(pool):
            nc.gpsimd.iota(disti, [[P, TT], [-1, SEQ]], base=0, channel_multiplier=1)
            nc.gpsimd.iota(cmpi, [[P, TT], [-16, N_CMP]], base=-31, channel_multiplier=1).then_inc(iota_done, 1)
            core.pool.link(pool, nc.gpsimd.memset(far, FAR))
            core.pool.link(pool, nc.gpsimd.memset(mix.VC[:], 0.0))
            pool.wait_ge(dist_f, 1)
            for n in range(4):
                nc.gpsimd.affine_select(out=mix.dist[:, n], in_=mix.dist[:, n], compare_op=ALU.is_ge, fill=FAR,
                                        base=0, pattern=[[P, TT], [-1, SEQ]], channel_multiplier=1)
            nc.gpsimd.affine_select(out=mix.valid_cmp[:], in_=mix.dist_cmp[:], compare_op=ALU.is_ge, fill=FAR,
                                    base=-31, pattern=[[P, TT], [-16, N_CMP]], channel_multiplier=1
                                    ).then_inc(causal_done, 1)
            pool.wait_ge(causal_done, 1)
            nc.gpsimd.affine_select(out=mix.dist[:, 1], in_=mix.dist[:, 1], compare_op=ALU.is_ge, fill=FAR,
                                    base=128, pattern=[[-P, TT], [1, SEQ]], channel_multiplier=-1
                                    ).then_inc(causal_done, 1)

        @block.vector
        def _(dve):
            def low(c):
                width = IN_2[c][1]
                for kt in range(KT):
                    kg, k = kt // KG, kt % KG
                    dve.wait_ge(core.high_ready, row_tile(c, kg, k) + 1)
                    nc.vector.tensor_tensor(x[:, k, 1, :], core.hT[:, kt, :], x[:, k, 0, :].bitcast(F32),
                                            ALU.subtract)
                    ins = nc.vector.tensor_tensor(w[:, k, 1, 0:width],
                                                  core.ring[:, (st.first + 4 * c + kg) % RING, k, 0:width],
                                                  w[:, k, 0, 0:width].bitcast(F32), ALU.subtract)
                    ins.then_inc(core.low_ready if k < KG - 1 else core.used, 1)

            def distances():
                dve.wait_ge(iota_done, 1)
                for n in range(4):
                    nc.vector.tensor_copy(mix.dist[:, n], disti)
                nc.vector.tensor_copy(mix.dist_cmp[:], cmpi).then_inc(dist_f, 1)

            def masks(n, mod):
                core.dve.link(dve, nc.vector.tensor_scalar(odd, disti, mod - 1, None, ALU.bitwise_and))
                core.dve.link(dve, nc.vector.copy_predicated(mix.dist[:, n], odd, far))

            def additions():
                nc.vector.tensor_scalar(mix.fox_mask, mix.dist[:, 0], 0.5 * FAR, -FAR, ALU.is_ge, ALU.mult)
                core.dve.link(dve, nc.vector.tensor_copy(mix.dist_cmp[:], mix.valid_cmp[:]))
                core.dve.link(dve, nc.vector.tensor_scalar(mix.valid_cmp[:], mix.dist_cmp[:], 0.5 * FAR, None,
                                                           ALU.is_lt))

            for c in range(len(IN_2)):
                low(c)
                if c == 0:
                    distances()
                elif c == 3:
                    dve.wait_ge(causal_done, 2)
                    masks(2, 4)
                elif c == 4:
                    masks(3, 16)
                elif c == 5:
                    additions()
    core.split_groups += st.groups
    for half in range(2):
        core.claimed[half] += NT * st.turns


def alibi(heads):
    return [float(np.float32(2.0 ** (-8.0 * (h + 1) / heads))) for h in range(heads)]


def attention_packs():
    packs = []
    for heads in (range(0, 4), range(4, FOX)):
        packs.append(("fox", [(T_FOXQ + h // 2, T_FOXK + h // 2, h % 2, ("fox", h)) for h in heads],
                      [(HD * h, HD, [(m, V_FOX + HD * h)]) for m, h in enumerate(heads)], None))
    slopes = alibi(NSA)
    for i in range(0, NSA, 2):
        maps, outs = [], []
        for m, h in enumerate((i, i + 1)):
            g = h // (NSA // GROUPS)
            for k_tile in (T_SLCK, T_WINK):
                maps.append((T_NSAQ + h % 4, k_tile, g, (0, slopes[h])))
            outs.append((HD * (FOX + h), HD, [(2 * m, V_SLC + HD * g), (2 * m + 1, V_WIN + HD * g), (("cmp", h), g)]))
        packs.append(("nsa", maps, outs, i))
    slopes = alibi(DIL)
    for j in range(3):
        maps, outs = [], []
        for m, h in enumerate((j, 3 + j, 6 + j)):
            maps.append((T_DILQ + h // 2, T_DILK + h // 2, h % 2, (1 + m, slopes[h])))
            outs.append((HD * (FOX + NSA + h), HD, [(m, V_DIL + HD * h)]))
        packs.append(("dil", maps, outs, None))
    slopes = alibi(DIFF)
    for i in range(0, DIFF, 2):
        maps, outs = [], []
        for m, h in enumerate((i, i + 1)):
            maps += [(T_DIFFQ + h, T_DIFFK + h, half, (0, slopes[h])) for half in range(2)]
            outs.append((HD * (FOX + NSA + DIL) + P * h, P, [(2 * m, V_DIFF + P * h), (2 * m + 1, V_DIFF + P * h)]))
        packs.append(("diff", maps, outs, None))
    return packs


def phase_compress(nc, core, mix):
    ps, tok = core.ps, tokens(core)
    steps = ("blocks_ready", "hidden_ready", "gelu_ready", "kv_ready", "kv_taken", "sc_ready", "sc_diff", "sc_exp",
             "p_ready", "pt_ready", "pt_free", "f_turned", "f_z", "f_exp", "f_cum", "f_cols", "f_rows", "rows_free",
             "lam_sums", "lam_exp", "lam_ready", "lam_wide", "gates_ready")
    with ExitStack() as ctx:
        s = {n: ctx.enter_context(nc.semaphore(n)) for n in steps}
        blk = ctx.enter_context(nc.sbuf_tensor("blocks", [P, 2, 32, N_CMP], F32))
        hid = ctx.enter_context(nc.sbuf_tensor("cmp_hidden", [HD, 4 * N_CMP], F32))
        kc = ctx.enter_context(nc.sbuf_tensor("cmp_keys", [P, N_CMP], F32))
        sc = ctx.enter_context(nc.sbuf_tensor("cmp_scores", [P, NSA * TT, N_CMP], F32))
        st = ctx.enter_context(nc.sbuf_tensor("cmp_stats", [P, 4, NSA * TT], F32))
        frow = ctx.enter_context(nc.sbuf_tensor("fox_rows", [FOX, 3, SEQ], F32))
        lam = ctx.enter_context(nc.sbuf_tensor("lambda_parts", [1, 2, HD + 2], F32))
        block = ctx.enter_context(nc.Block())

        @block.tensor
        def _(pe):
            for c in range(TT):
                ins = nc.tensor.transpose(ps[0:FOX, 5, c * P:(c + 1) * P], tok[:, c, V_FOXF:V_FOXF + FOX], core.ident[:])
            ins.then_inc(s["f_turned"], 1)
            pe.wait_ge(mix.w_in, 16 * 10)
            for a in range(2):
                pe.wait_ge(s["blocks_ready"], a + 1)
                for g in range(GROUPS):
                    rows, at = slice(g * HD, (g + 1) * HD), (2 * a + g) * N_CMP
                    for l in range(32):
                        ins = nc.tensor.matmul(ps[0:HD, g, at:at + N_CMP], mix.W1[rows, a, l, :], blk[rows, a, l, :],
                                               start=(l == 0), stop=(l == 31))
            ins.then_inc(s["hidden_ready"], 1)
            pe.wait_ge(s["gelu_ready"], 1)
            for g in range(GROUPS):
                nc.tensor.matmul(ps[:, 2, g * N_CMP:(g + 1) * N_CMP], mix.W2[0:HD, 0, :],
                                 hid[:, g * N_CMP:(g + 1) * N_CMP], start=True, stop=True)
            for g in range(GROUPS):
                ins = nc.tensor.matmul(ps[0:N_CMP, 3, g * HD:(g + 1) * HD], hid[:, (2 + g) * N_CMP:(3 + g) * N_CMP],
                                       mix.W2[0:HD, 1, 0:HD], start=True, stop=True)
            ins.then_inc(s["kv_ready"], 1)
            pe.wait_ge(s["f_cum"], 1)
            for c in range(TT):
                ins = nc.tensor.transpose(ps[:, 5, SEQ + c * FOX:SEQ + (c + 1) * FOX], frow[:, 2, c * P:(c + 1) * P],
                                          core.ident[0:FOX, 0:FOX])
            ins.then_inc(s["f_cols"], 1)
            for h in range(FOX):
                if h >= 2:
                    pe.wait_ge(s["rows_free"], h - 1)
                nc.tensor.matmul(ps[:, (6, 4)[h % 2], 0:SEQ],
                                 core.pick[0:FOX, h, :], frow[:, 2, :], start=True, stop=True).then_inc(s["f_rows"], 1)
            pe.wait_ge(s["lam_ready"], 1)
            nc.tensor.matmul(ps[:, 5, 500:501], core.ones[0:1, :], lam[0:1, 0, HD:HD + 1], start=True, stop=True
                             ).then_inc(s["lam_wide"], 1)
            pe.wait_ge(s["kv_taken"], 1)
            for h in range(NSA):
                g = h // 4
                rows = slice(g * HD, (g + 1) * HD)
                for c in range(TT):
                    at = (h * TT + c) * N_CMP
                    ins = nc.tensor.matmul(ps[:, g, at:at + N_CMP], core.big[rows, T_NSAQ + h % 4, c * P:(c + 1) * P],
                                           kc[rows, :], start=True, stop=True)
            ins.then_inc(s["sc_ready"], 1)
            pe.wait_ge(s["p_ready"], 1)
            for n in range(4):
                for j in range(4):
                    ins = nc.tensor.transpose(ps[0:N_CMP, n, j * P:(j + 1) * P], sc[:, 4 * n + j, :], core.ident[:])
                ins.then_inc(s["pt_ready"], 1)

        @block.scalar
        def _(act):
            a = core.act
            nc.scalar.activation(mix.gates[:], tok[:, :, V_GATE:V_GATE + 3 * NSA], ACT.Sigmoid
                                 ).then_inc(s["gates_ready"], 1)
            act.wait_ge(s["hidden_ready"], 1)
            hid_g = hid[:].rearrange("p (a g c) -> p a g c", a=2, g=2)
            for g in range(GROUPS):
                ins = nc.scalar.activation(hid_g[:, :, g, :], ps[0:HD, g, 0:4 * N_CMP].rearrange(
                    "p (a g c) -> p a g c", a=2, g=2)[:, :, g, :], ACT.Gelu_apprx_tanh)
            ins.then_inc(s["gelu_ready"], 1)
            act.wait_ge(s["kv_ready"], 1)
            for g in range(GROUPS):
                rows = slice(g * HD, (g + 1) * HD)
                nc.scalar.activation(kc[rows, :], ps[rows, 2, g * N_CMP:(g + 1) * N_CMP], ACT.Copy)
            nc.scalar.activation(mix.VC[0:N_CMP, HD:3 * HD], ps[0:N_CMP, 3, 0:2 * HD], ACT.Copy
                                 ).then_inc(s["kv_taken"], 1)
            act.wait_ge(s["f_z"], 1)
            a.link(act, nc.scalar.activation(frow[:, 1, :], frow[:, 1, :], ACT.Exp))
            nc.scalar.activation(frow[:, 1, :], frow[:, 1, :], ACT.Ln, bias=core.one[0:FOX, :]).then_inc(s["f_exp"], 1)
            act.wait_ge(s["lam_sums"], 1)
            nc.scalar.activation(lam[0:1, 1, 0:2], lam[0:1, 0, HD:HD + 2], ACT.Exp).then_inc(s["lam_exp"], 1)
            act.wait_ge(s["sc_diff"], 1)
            nc.scalar.activation(sc[:], sc[:], ACT.Exp).then_inc(s["sc_exp"], 1)
            for n in range(4):
                act.wait_ge(s["pt_ready"], n + 1)
                nc.scalar.activation(mix.PTC[0:N_CMP, 2 * n:2 * n + 2, :], ps[0:N_CMP, n, :], ACT.Copy)

        @block.vector
        def _(dve):
            v = core.dve
            for a, tile in enumerate((T_CMPK, T_CMPV)):
                src = core.big[:, tile, :].rearrange("p (c l) -> p l c", l=16)
                for r in range(2):
                    pos = core.cols[:, C_POS + 32 * a + 16 * r:C_POS + 32 * a + 16 * r + 16]
                    ins = nc.vector.tensor_tensor(blk[:, a, 16 * r:16 * r + 16, :], src[:, :, r:r + N_CMP],
                                                  bcast(pos, N_CMP, 2), ALU.add)
                ins.then_inc(s["blocks_ready"], 1)
            dve.wait_ge(s["f_turned"], 1)
            dve.wait_ge(mix.w_in, 16 * 10)
            v.link(dve, nc.vector.tensor_scalar(frow[:, 0, :], ps[0:FOX, 5, 0:SEQ], mix.fox_bias[:], None, ALU.add))
            v.link(dve, nc.vector.tensor_scalar(frow[:, 1, :], frow[:, 0, :], -1.0, None, ALU.mult))
            nc.vector.tensor_tensor(frow[:, 1, :], frow[:, 1, :], frow[:, 0, :], ALU.min).then_inc(s["f_z"], 1)
            lv = mix.lam_rows[:].rearrange("p (a d) -> p a d", a=4)
            for n in range(2):
                v.link(dve, nc.vector.tensor_tensor(lam[0:1, 1, 0:HD], lv[:, 2 * n, :], lv[:, 2 * n + 1, :], ALU.mult))
                v.link(dve, nc.vector.tensor_reduce(lam[0:1, 0, HD + n:HD + n + 1], lam[0:1, 1, 0:HD], AX.X, ALU.add))
            dve.sem_inc(s["lam_sums"], 1)
            dve.wait_ge(s["f_exp"], 1)
            v.link(dve, nc.vector.scalar_tensor_tensor(out=frow[:, 1, :], in0=frow[:, 0, :], scalar=0.0,
                                                       in1=frow[:, 1, :], op0=ALU.min, op1=ALU.subtract))
            v.link(dve, nc.vector.memset(frow[:, 0, :], 1.0))
            nc.vector.tensor_tensor_scan(frow[:, 2, :], frow[:, 0, :], frow[:, 1, :], 0.0, ALU.mult, ALU.add
                                         ).then_inc(s["f_cum"], 1)
            dve.wait_ge(s["lam_exp"], 1)
            v.link(dve, nc.vector.tensor_tensor(lam[0:1, 0, HD:HD + 1], lam[0:1, 1, 1:2], lam[0:1, 1, 0:1],
                                                ALU.subtract))
            nc.vector.tensor_scalar(lam[0:1, 0, HD:HD + 1], lam[0:1, 0, HD:HD + 1], -LAM_INIT, None, ALU.add
                                    ).then_inc(s["lam_ready"], 1)
            dve.wait_ge(s["f_cols"], 1)
            nc.vector.tensor_copy(mix.fox_cum[:], ps[:, 5, SEQ:SEQ + TT * FOX].rearrange("p (c h) -> p c h", c=TT))
            for h in range(FOX):
                dve.wait_ge(s["f_rows"], h + 1)
                nc.vector.tensor_tensor(core.big[:, T_FOXROW + 2 * h:T_FOXROW + 2 * h + 2, :], mix.fox_mask,
                                        bcast(ps[:, (6, 4)[h % 2], 0:SEQ], TT), ALU.subtract
                                        ).then_inc(s["rows_free"], 1)
            dve.wait_ge(s["lam_wide"], 1)
            nc.vector.tensor_copy(mix.neg_lam[:], ps[:, 5, 500:501])
            dve.wait_ge(s["sc_ready"], 1)
            for h, slope in enumerate(alibi(NSA)):
                g = h // 4
                at = h * TT * N_CMP
                ins = nc.vector.scalar_tensor_tensor(
                    out=sc[:, h * TT:(h + 1) * TT, :], in0=mix.dist_cmp[:], scalar=-slope,
                    in1=ps[:, g, at:at + TT * N_CMP].rearrange("p (t c) -> p t c", t=TT), op0=ALU.mult, op1=ALU.add)
            v.link(dve, ins)
            v.link(dve, nc.vector.tensor_reduce(st[:, 0, :], sc[:], AX.X, ALU.max))
            nc.vector.tensor_tensor(sc[:], sc[:], bcast(st[:, 0, :], N_CMP, 2), ALU.subtract
                                    ).then_inc(s["sc_diff"], 1)
            dve.wait_ge(s["sc_exp"], 1)
            v.link(dve, nc.vector.tensor_reduce(st[:, 1, :], sc[:], AX.X, ALU.add))
            v.link(dve, nc.vector.reciprocal(st[:, 1, :], st[:, 1, :]))
            dve.wait_ge(s["gates_ready"], 1)
            v.link(dve, nc.vector.tensor_tensor(
                st[:, 2, :].rearrange("p (h t) -> p h t", t=TT), st[:, 1, :].rearrange("p (h t) -> p h t", t=TT),
                mix.gates[:].rearrange("p t (h b) -> p h t b", b=3)[:, :, :, 0], ALU.mult))
            v.link(dve, nc.vector.tensor_tensor(sc[:], sc[:], bcast(st[:, 2, :], N_CMP, 2), ALU.mult))
            nc.vector.tensor_tensor(sc[:].rearrange("p (h t) c -> p h (t c)", t=TT),
                                    sc[:].rearrange("p (h t) c -> p h (t c)", t=TT),
                                    bcast(mix.valid_cmp[:].rearrange("p t c -> p (t c)"), NSA), ALU.mult
                                    ).then_inc(s["p_ready"], 1)


def phase_attention(nc, core, mix):
    ps, tok, big = core.ps, tokens(core), core.big
    packs = attention_packs()
    N = len(packs)
    maps_before = [sum(len(p[1]) for p in packs[:n]) for n in range(N + 1)]
    pairs = [[p[2][i:i + 2] for i in range(0, len(p[2]), 2)] for p in packs]
    pairs_before = [sum(len(x) for x in pairs[:n]) for n in range(N + 1)]
    dil_before = [sum(p[0] == "dil" for p in packs[:n]) for n in range(N + 1)]
    with ExitStack() as ctx:
        sem = lambda n: ctx.enter_context(nc.semaphore(n))
        scores_ready, scores_free, max_ready, exp_ready, p_ready, pt_ready, pt_free, pv_ready, pv_free, dil_diff, \
            dil_exp, sq_ready, ss_ready, rs_ready = (sem(n) for n in (
                "scores_ready", "scores_free", "max_ready", "exp_ready", "p_ready", "pt_ready", "pt_free",
                "pv_ready", "pv_free", "dil_diff", "dil_exp", "sq_ready", "ss_ready", "rs_ready"))
        stats = ctx.enter_context(nc.sbuf_tensor("stats", [P, 2, 6, 4, TT], F32))
        block = ctx.enter_context(nc.Block())
        S, PT = mix.S, mix.PT

        @block.tensor
        def _(pe):
            def scores(n):
                for m, (qt, kt, half, _) in enumerate(packs[n][1]):
                    if n >= 1:
                        before = min(m + 1, len(packs[n - 1][1]))
                        pe.wait_ge(scores_free, maps_before[n - 1] + before)
                    rows = slice(half * HD, (half + 1) * HD)
                    for c in range(TT):
                        ins = nc.tensor.matmul(ps[:, m, c * SEQ:(c + 1) * SEQ], big[rows, qt, c * P:(c + 1) * P],
                                               big[rows, kt, :], start=True, stop=True)
                    ins.then_inc(scores_ready, 1)

            scores(0)
            for n in range(N):
                if n + 1 < N:
                    scores(n + 1)
                pe.wait_ge(p_ready, n + 1)
                for m in range(len(packs[n][1])):
                    u = maps_before[n] + m
                    if u >= 2:
                        pe.wait_ge(pt_free, u - 1)
                    for j, (c, k) in enumerate(((0, 0), (1, 0), (1, 1))):
                        ins = nc.tensor.transpose(ps[:, 4 + u % 2, j * P:(j + 1) * P],
                                                  S[:, n % 2, m, c, k * P:(k + 1) * P], core.ident[:])
                    ins.then_inc(pt_ready, 1)
                pe.wait_ge(pt_free, maps_before[n + 1])
                for x, pair in enumerate(pairs[n]):
                    u = pairs_before[n] + x
                    if u >= 1:
                        pe.wait_ge(pv_free, u)
                    for y, (row, width, terms) in enumerate(pair):
                        up = width == HD and row % P == HD
                        parts = []
                        for m, col in terms:
                            if isinstance(m, tuple):
                                c0 = HD + HD * col
                                lhsT = mix.VC[0:N_CMP, c0 - HD * up:c0 + HD]
                                parts.append((0, SEQ, lhsT, mix.PTC[0:N_CMP, m[1], :]))
                            else:
                                for k in range(TT):
                                    lhsT = tok[:, k, col - HD * up:col + width]
                                    rhs = PT[:, n % 2, m, 0:SEQ] if k == 0 else PT[:, n % 2, m, SEQ:SEQ + P]
                                    parts.append((k * P, SEQ, lhsT, rhs))
                        height = HD + HD * up if width == HD else P
                        for z, (a, b, lhsT, rhs) in enumerate(parts):
                            ins = nc.tensor.matmul(ps[0:height, 6, y * SEQ + a:y * SEQ + b], lhsT, rhs,
                                                   start=(z == 0), stop=(z == len(parts) - 1),
                                                   skip_group_check=True)
                    ins.then_inc(pv_ready, 1)
            for n in range(2):
                pe.wait_ge(sq_ready, 1)
                nc.tensor.matmul(ps[:, n, :], core.ones[:], S[:, 0, n, :, :].rearrange("p c k -> p (c k)"),
                                 start=True, stop=True).then_inc(ss_ready, 1)

        @block.scalar
        def _(act):
            def exps(n):
                b = n % 2
                act.wait_ge(max_ready, n + 1)
                for m in range(len(packs[n][1])):
                    for c in range(TT):
                        ins = nc.scalar.activation(S[:, b, m, c, :], S[:, b, m, c, :], ACT.Exp,
                                                   bias=stats[:, b, 0, m, c:c + 1], accum_out=stats[:, b, 1, m, c:c + 1])
                ins.then_inc(exp_ready, 1)

            exps(0)
            for n in range(N):
                if n + 1 < N:
                    exps(n + 1)
                if packs[n][0] == "dil":
                    part = stats[:, n % 2, 2, 0:3, :]
                    act.wait_ge(dil_diff, dil_before[n] + 1)
                    nc.scalar.activation(part, part, ACT.Exp).then_inc(dil_exp, 1)
                for m in range(len(packs[n][1])):
                    u = maps_before[n] + m
                    act.wait_ge(pt_ready, u + 1)
                    nc.scalar.activation(PT[:, n % 2, m, :], ps[:, 4 + u % 2, 0:3 * P], ACT.Copy).then_inc(pt_free, 1)
                for x, pair in enumerate(pairs[n]):
                    act.wait_ge(pv_ready, pairs_before[n] + x + 1)
                    for y, (row, width, _) in enumerate(pair):
                        rows = slice(row % P, row % P + width)
                        ins = nc.scalar.activation(core.hT[rows, row // P, :], ps[rows, 6, y * SEQ:(y + 1) * SEQ],
                                                   ACT.Copy)
                    ins.then_inc(pv_free, 1)
            act.wait_ge(pv_free, pairs_before[N])
            heads = core.hT[:, KT - DIFF:KT, :]
            nc.scalar.activation(S[:, 0, 0:2, :, :].rearrange("p m c k -> p (m c k)"),
                                 heads.rearrange("p a b -> p (a b)"), ACT.Square).then_inc(sq_ready, 1)
            for n in range(2):
                act.wait_ge(ss_ready, n + 1)
                ins = nc.scalar.activation(S[:, 1, n, :, :].rearrange("p c k -> p (c k)"), ps[:, n, :], ACT.Ln,
                                           bias=core.eps[:], scale=1.0 / P)
            core.act.link(act, ins)
            nc.scalar.activation(S[:, 1, 0:2, :, :], S[:, 1, 0:2, :, :], ACT.Exp, scale=-0.5).then_inc(rs_ready, 1)

        @block.vector
        def _(dve):
            v = core.dve

            def biases(n):
                b = n % 2
                maps = packs[n][1]
                for m, (_, _, _, (table, slope)) in enumerate(maps):
                    dve.wait_ge(scores_ready, maps_before[n] + m + 1)
                    if table == "fox":
                        for c in range(TT):
                            ins = nc.vector.scalar_tensor_tensor(
                                out=S[:, b, m, c, :], in0=ps[:, m, c * SEQ:(c + 1) * SEQ],
                                scalar=mix.fox_cum[:, c, slope:slope + 1],
                                in1=big[:, T_FOXROW + 2 * slope + c, :], op0=ALU.add, op1=ALU.add)
                    else:
                        ins = nc.vector.scalar_tensor_tensor(
                            out=S[:, b, m, :, :], in0=mix.dist[:, table], scalar=-slope,
                            in1=ps[:, m, :].rearrange("p (c k) -> p c k", c=TT), op0=ALU.mult, op1=ALU.add)
                    ins.then_inc(scores_free, 1)
                dve.wait_ge(scores_free, maps_before[n + 1])
                nc.vector.tensor_reduce(stats[:, b, 0, 0:len(maps), :], S[:, b, 0:len(maps), :, :], AX.X, ALU.max,
                                        negate=True).then_inc(max_ready, 1)

            def weigh(n):
                b = n % 2
                kind, maps, _, first = packs[n]
                M = len(maps)
                top, total, part, factor = (stats[:, b, j] for j in range(4))
                dve.wait_ge(exp_ready, n + 1)
                if kind == "dil":
                    v.link(dve, nc.vector.tensor_reduce(factor[:, 3, :], top[:, 0:3, :].rearrange("p m c -> p c m"),
                                                        AX.X, ALU.min))
                    nc.vector.tensor_tensor(part[:, 0:3, :], bcast(factor[:, 3, :], 3), top[:, 0:3, :], ALU.subtract
                                            ).then_inc(dil_diff, 1)
                    dve.wait_ge(dil_exp, dil_before[n] + 1)
                    v.link(dve, nc.vector.tensor_tensor(total[:, 0:3, :], total[:, 0:3, :], part[:, 0:3, :], ALU.mult))
                    v.link(dve, nc.vector.tensor_reduce(factor[:, 3, :], total[:, 0:3, :].rearrange("p m c -> p c m"),
                                                        AX.X, ALU.add))
                    v.link(dve, nc.vector.reciprocal(factor[:, 3, :], factor[:, 3, :]))
                    v.link(dve, nc.vector.tensor_tensor(factor[:, 0:3, :], part[:, 0:3, :], bcast(factor[:, 3, :], 3),
                                                        ALU.mult))
                else:
                    v.link(dve, nc.vector.reciprocal(factor[:, 0:M, :], total[:, 0:M, :]))
                if kind == "nsa":
                    for m in range(M):
                        g = (first + m // 2) * 3 + 1 + m % 2
                        ins = nc.vector.tensor_tensor(factor[:, m, :], factor[:, m, :], mix.gates[:, :, g], ALU.mult)
                    v.link(dve, ins)
                if kind == "diff":
                    f = factor.rearrange("p (h m) c -> p h m c", m=2)[:, :, 1, :]
                    v.link(dve, nc.vector.tensor_scalar(f, f, mix.neg_lam[:], None, ALU.mult))
                nc.vector.tensor_tensor(S[:, b, 0:M].rearrange("p m c k -> p (m c) k"),
                                        S[:, b, 0:M].rearrange("p m c k -> p (m c) k"),
                                        bcast(factor[:, 0:M, :].rearrange("p m c -> p (m c)"), SEQ, 2), ALU.mult
                                        ).then_inc(p_ready, 1)

            biases(0)
            for n in range(N):
                if n + 1 < N:
                    if n >= 1:
                        dve.wait_ge(pt_ready, maps_before[n])
                    biases(n + 1)
                weigh(n)
            v.link(dve, nc.vector.tensor_scalar(core.aff[:, 0, 0:1], core.cols[:, C_SUBLN:C_SUBLN + 1],
                                                1.0 - LAM_INIT, None, ALU.mult))
            dve.wait_ge(rs_ready, 1)
            o = core.hT[:, KT - DIFF:KT, :].rearrange("p a b -> p (a b)")
            v.link(dve, nc.vector.scalar_tensor_tensor(out=o, in0=o, scalar=core.aff[:, 0, 0:1],
                                                       in1=S[:, 1, 0:2, :, :].rearrange("p m c k -> p (m c k)"),
                                                       op0=ALU.mult, op1=ALU.mult))


def mixer_memory(nc, ctx):
    mix = Core()
    sb = lambda name, shape: ctx.enter_context(nc.sbuf_tensor(name, shape, F32))
    mix.S = sb("scores", [P, 2, 4, TT, SEQ])
    mix.W1 = mix.S[:].rearrange("p b m c k -> p (b m c k)").rearrange("p (a l o) -> p a l o", a=2, l=32)
    mix.PT = sb("maps_t", [P, 2, 4, 3 * P])
    mix.PTC = sb("cmp_maps_t", [16, NSA, SEQ])
    mix.dist = sb("distances", [P, 4, TT, SEQ])
    mix.dist_cmp, mix.valid_cmp = sb("dist_cmp", [P, TT, N_CMP]), sb("valid_cmp", [P, TT, N_CMP])
    mix.fox_mask = mix.PT[:, 0, 2:4, 0:SEQ]
    mix.fox_cum, mix.gates = sb("fox_cum", [P, TT, FOX]), sb("nsa_gates", [P, TT, 3 * NSA])
    mix.neg_lam, mix.fox_bias = sb("neg_lambda", [P, 1]), sb("fox_bias", [FOX, 1])
    mix.lam_rows = sb("lambda_rows", [1, 4 * HD])
    mix.W2 = sb("cmp_w2", [HD, 2, 2 * HD])
    mix.VC = sb("cmp_values", [16, 3 * HD])
    mix.w_in = ctx.enter_context(nc.semaphore("small_weights_in"))
    return mix



def build(nc, t, out):
    with ExitStack() as ctx:
        core = Core()
        sb = lambda name, shape, dt=F32: ctx.enter_context(nc.sbuf_tensor(name, shape, dt))
        sem = lambda name: ctx.enter_context(nc.semaphore(name))
        core.ps = ctx.enter_context(nc.psum_tensor("accumulators", [P, 8, 512], F32))
        core.xT = sb("x_t", [P, KT, SEQ])
        core.hT = sb("h_t", [P, KT, SEQ])
        core.big = sb("wide", [P, 64, SEQ])
        core.ring = sb("weights", [P, RING, KG, CW])
        core.cols = sb("small_vectors", [P, N_VEC])
        core.mod = sb("modulation", [P, 2, NMOD])
        core.c_act = sb("c_act", [P, 2 * KT])
        core.aff = sb("affine", [P, 1, KT])
        core.lb = sb("lower_bounds", [P, 2, HH])
        core.ident, core.ones, core.incl, core.strict = (sb(n, [P, P]) for n in ("ident", "ones", "incl", "strict"))
        core.up_mask, core.low_mask = (sb(n, [P, len(LEVELS), P]) for n in ("up_mask", "low_mask"))
        core.keep = sb("keep", [P, SEQ])
        core.pick = sb("pick", [HH, HH, P])
        core.gates = sb("gates", [HH, 4 * SEQ])
        core.gdn_cols = sb("gdn_cols", [HH, 4])
        core.w_gates = sb("w_gates", [P, KT, 2 * HH])
        core.eps, core.one = sb("eps", [P, 1]), sb("one", [P, 1])
        core.used = sem("weights_used")
        core.landed = [sem(f"weights_landed_{s}") for s in range(RING)]
        core.free = [sem("low_accumulators_free"), sem("high_accumulators_free")]
        core.tile_ready, core.relu_steps = sem("tile_ready"), sem("relu_steps")
        core.act, core.dve, core.pool = (Chain(sem(f"{n}_steps")) for n in ("scalar", "vector", "pool"))
        core.x_high, core.x_low, core.high_ready, core.low_ready, core.parts_used = (
            sem(n) for n in ("x_high_ready", "x_low_ready", "high_ready", "low_ready", "parts_used"))
        core.split_groups, core.split_phases = 0, 0
        core.tiles_ready_n, core.claimed = 0, [0, 0]
        core.ada_turns, core.norms, core.mods = 0, 0, 0
        core.norm_sems = [sem(n) for n in ("squares_ready", "sums_ready", "mean_ready", "root_ready", "scaled")]
        core.mod_rows_in, core.mod_turned = sem("mod_rows_in"), sem("mod_turned")
        core.ada_landed = {n: [sem(f"ada_landed_{n}_{s}") for s in range(n)] for n in (ASLOTS, FIRST_ASLOTS)}
        core.ada_landed_turns = {ASLOTS: 0, FIRST_ASLOTS: 0}
        core.ada_steps, core.ada_sums_ready, core.ada_rows_ready, core.ada_rows_taken, core.ada_stored = (
            sem(f"ada_{n}") for n in ("steps", "sums_ready", "rows_ready", "rows_taken", "stored"))
        core.mod_dram = nc.dram_tensor("modulation_rows", (2, NMOD * P), F32, kind="Internal").ap()

        core.streams, at = {}, 0
        w_ff2 = t["w_ff2"][0].rearrange("(g k p) n -> p g k n", p=P, k=KG)
        w_down = t["ffn_w_down_2"][0].rearrange("(g k p) n -> p g k n", p=P, k=KG)
        gate, up = (t[n][0].rearrange("(g k p) n -> p g k n", p=P, k=KG) for n in ("ffn_w_gate_2", "ffn_w_up_2"))
        for name, source, unit, turns in (
                ("in_1", by_columns(t["w_in"][0]), TURN, 8),
                ("out_1", by_columns(t["w_out"][0]), TURN, 2),
                ("ff_1", by_columns(t["w_ff1"][0]), TURN, 8),
                ("ff_2", lambda i, q: w_ff2[:, q, :, bass.ds(i * CW, CW)], 2 * TURN, 4),
                ("in_2", in_2_source(t["w_in_2"][0]), TURN, 7),
                ("out_2", by_columns(t["w_out_2"][0]), TURN, 2),
                ("gate_up", lambda i, q: gate[:, q, :, bass.ds(i * CW, CW)] if q < 4 else
                 up[:, q - 4, :, bass.ds((i * 2) * (CW // 2), CW)], TURN, 11),
                ("down", lambda i, q: w_down[:, q % 11, :, bass.ds((i * 2 + q // 11) * CW, CW)], 22, 2)):
            core.streams[name] = Stream(source, unit, turns, at)
            at += unit * turns

        def into(dst):
            return lambda eng, i, tile, acc: nc.scalar.activation(
                dst[:, bass.ds(i * (2 * NT) + tile, 1), :], acc.unsqueeze(1), ACT.Copy)

        def add_to_x(gate):
            def step(eng, i, tile, acc):
                k = i * (2 * NT) + tile
                x = core.xT[:, bass.ds(k, 1), :].rearrange("p a b -> p (a b)")
                return nc.vector.scalar_tensor_tensor(out=x, in0=acc, scalar=core.mod[:, 1, bass.ds(k + gate, 1)],
                                                      in1=x, op0=ALU.mult, op1=ALU.add)
            return step

        def square_relu(eng, i, tile, acc):
            nc.scalar.activation(acc, acc, ACT.Relu).then_inc(core.relu_steps, 1)
            eng.wait_ge(core.relu_steps, i * (2 * NT) + (tile + 1))
            return nc.scalar.activation(core.big[:, bass.ds(i * (2 * NT) + tile, 1), :], acc.unsqueeze(1), ACT.Square)

        def ff2_tile(eng, i, tile, acc):
            return nc.scalar.activation(core.hT[:, bass.ds(i * NT + tile, 1), :], acc.unsqueeze(1), ACT.Copy)

        def on(engine, step):
            return [(engine, step)] * 2

        w_ada, w_ada_2 = t["w_ada"][0], t["ada_w_2"][0]
        with ExitStack() as first:
            ada = Ada(first, nc, core, w_ada, 0, 0, 4, FIRST_ASLOTS)
            phase_setup(nc, core, t, ada)
            phase_ada_first(nc, core, ada)
        phase_modulation(nc, core, 0, 0, 8)
        phase_norm(nc, core, C_PREMIX, 0, 0, KT, summed=True)
        phase_split_product(nc, core, "in_1", "out_1", on("act", into(core.big)), ada=(w_ada, 0, 8))
        phase_modulation(nc, core, 0, 8, 16)
        with nc.sbuf_tensor("convolved", [P, 3 * HH, SEQ], F32) as conv:
            phase_hgrn(nc, core, conv)
            phase_gdn(nc, core, conv)
        phase_split_product(nc, core, "out_1", "ff_1", on("act", into(core.big[:, KT:2 * KT, :])))
        phase_residual_norm(nc, core, core.big[:, KT:2 * KT, :], C_POSTMIX, 2 * KT)
        phase_norm(nc, core, C_PREFFN, 0, 3 * KT, 4 * KT, summed=True)
        phase_split_product(nc, core, "ff_1", "ff_2", on("act", square_relu), ada=(w_ada_2, 1, 0))
        phase_split_product(nc, core, "ff_2", "in_2", [("act", ff2_tile)], ada=(w_ada_2, 1, 16))
        phase_modulation(nc, core, 1, 0, 24)
        phase_residual_norm(nc, core, core.hT, C_POSTFFN, 5 * KT)
        phase_norm(nc, core, C_MIX2, 1, 0, KT, summed=True)
        with ExitStack() as mix_ctx:
            mix = mixer_memory(nc, mix_ctx)
            phase_in_2(nc, core, mix, t)
            phase_compress(nc, core, mix)
            phase_attention(nc, core, mix)
        phase_split_product(nc, core, "out_2", "gate_up", on("dve", add_to_x(2 * KT)))
        phase_norm(nc, core, C_FFN2, 1, 3 * KT, 4 * KT)
        phase_swiglu(nc, core)
        phase_split_product(nc, core, "down", None, on("dve", add_to_x(5 * KT)))
        phase_norm(nc, core, C_FINAL)
        phase_write_out(nc, core, out)


INPUTS = ["x", "c", "w_ada", "b_ada", "pre_mix_norm", "post_mix_norm", "pre_ffn_norm", "post_ffn_norm", "w_in",
          "hg_lb_logits", "hg_norm", "gdn_conv_w", "gdn_a_log", "gdn_dt_bias", "gdn_norm", "w_out", "w_ff1", "w_ff2",
          "c_2", "ada_w_2", "ada_b_2", "norm_mix_g_2", "norm_ffn_g_2", "w_in_2", "fox_f_bias_2", "nsa_cmp_w1_2",
          "nsa_cmp_w2_2", "nsa_cmp_pos_2", "diff_lambda_2", "diff_subln_g_2", "w_out_2", "ffn_w_gate_2",
          "ffn_w_up_2", "ffn_w_down_2", "final_norm_g_2"]


def kernel(**inputs):
    import concourse.bacc as bacc
    from concourse.bass_utils import run_bass_kernel_spmd

    nc = bacc.Bacc("TRN2", target_bir_lowering=False, num_devices=1)
    arrays, t = {}, {}
    for name in INPUTS:
        a = np.ascontiguousarray(inputs[name])
        arrays[f"in_{name}"] = a
        t[name] = nc.dram_tensor(f"in_{name}", a.shape, mybir.dt.from_np(a.dtype), kind="ExternalInput").ap()
    out = nc.dram_tensor("out", (1, SEQ, D), F32, kind="ExternalOutput").ap()
    build(nc, t, out)
    return run_bass_kernel_spmd(nc, [arrays], core_ids=[0]).results[0]["out"]
```
